# Optimizing a Trainium2 kernel written in Bass

```python
import jax, jax.numpy as jnp
from jax import lax
import numpy as np

D_MODEL = 1024
BATCH = 1
SEQ = 1024
DEPTH = 1

N_MEM = 256
HEAD_DIM = 64
MIX_WIDTH = D_MODEL
NSA_HEADS = (MIX_WIDTH // 2) // HEAD_DIM
NSA_KV_GROUPS = 2
NSA_HPG = NSA_HEADS // NSA_KV_GROUPS
NSA_WIDTH = NSA_HEADS * HEAD_DIM
NSA_KV_WIDTH = NSA_KV_GROUPS * HEAD_DIM
CMP_BLOCK = 32
CMP_STRIDE = 16
CMP_HIDDEN = 2 * HEAD_DIM
SEL_BLOCK = 64
SEL_TOPK = 8
WINDOW = 512
Q_BLOCK = 128
RET_HEADS = (MIX_WIDTH - NSA_WIDTH) // HEAD_DIM
RET_WIDTH = RET_HEADS * HEAD_DIM
RET_CHUNK = 128
ROPE_BASE = 10000.0
PROJ_WIDTH = NSA_WIDTH + 6 * NSA_KV_WIDTH + 3 * NSA_HEADS + 4 * RET_WIDTH
PROJ_SPLIT_POINTS = (NSA_WIDTH, NSA_WIDTH + 6 * NSA_KV_WIDTH,
                     NSA_WIDTH + 6 * NSA_KV_WIDTH + 3 * NSA_HEADS)
MEM_HEADS = 4
MEM_WIDTH = MEM_HEADS * HEAD_DIM
N_GROUPS = 4
EXPERTS_PER_GROUP = 8
N_EXPERTS = N_GROUPS * EXPERTS_PER_GROUP
TOP_K_IN_GROUP = 2
EXPERT_FF = D_MODEL // 4
MOE_BLOCK = 128

EPS = 1e-6
NEG_INF = -1e30
FORCE_SCORE = 1e9

kernel_name = 'hymba_nsa_retention_hmoe_layer'

def rms_norm(x, g):
    xf = x.astype(jnp.float32)
    y = xf * lax.rsqrt(jnp.mean(xf * xf, axis=-1, keepdims=True) + EPS)
    return (y * g.astype(jnp.float32)).astype(x.dtype)

def masked_softmax(s, mask):
    s = jnp.where(mask, s.astype(jnp.float32), NEG_INF)
    m = jnp.max(s, axis=-1, keepdims=True)
    p = jnp.exp(s - m) * mask
    return p / jnp.maximum(jnp.sum(p, axis=-1, keepdims=True), 1e-30)

def compress_blocks(kv, pos, w1, w2):
    B, S, G, Dh = kv.shape
    n_c = (S - CMP_BLOCK) // CMP_STRIDE + 1
    idx = np.arange(n_c)[:, None] * CMP_STRIDE + np.arange(CMP_BLOCK)[None, :]
    blk = kv[:, idx] + pos[None, None, :, None, :]
    blk = jnp.moveaxis(blk, 3, 2).reshape(B, n_c, G, CMP_BLOCK * Dh)
    return jax.nn.silu(blk @ w1) @ w2

def sel_from_cmp_matrix(n_c, n_sel):
    c0 = np.arange(n_c) * CMP_STRIDE
    s0 = np.arange(n_sel) * SEL_BLOCK
    ov = np.minimum(c0[None, :] + CMP_BLOCK, s0[:, None] + SEL_BLOCK) - np.maximum(c0[None, :], s0[:, None])
    return (np.clip(ov, 0, None) / CMP_BLOCK).astype(np.float32)

def nsa_mixer(q, kc, vc, ks, vs, kw, vw, gates, q_norm, kc_norm, ks_norm, kw_norm,
              pos_k, pos_v, ck_w1, ck_w2, cv_w1, cv_w2):
    B, S = q.shape[:2]
    G, R, Dh = NSA_KV_GROUPS, NSA_HPG, HEAD_DIM
    q = rms_norm(q.reshape(B, S, G, R, Dh), q_norm) * (Dh ** -0.5)
    t_pos = jnp.arange(S)
    kcmp = rms_norm(compress_blocks(kc, pos_k, ck_w1, ck_w2), kc_norm)
    vcmp = compress_blocks(vc, pos_v, cv_w1, cv_w2)
    n_c = kcmp.shape[1]
    c_end = jnp.arange(n_c) * CMP_STRIDE + CMP_BLOCK - 1
    cmask = c_end[None, :] <= t_pos[:, None]
    s_c = jnp.einsum('bsgrd,bcgd->bsgrc', q, kcmp)
    p_c = masked_softmax(s_c, cmask[None, :, None, None, :])
    o_cmp = jnp.einsum('bsgrc,bcgd->bsgrd', p_c.astype(vcmp.dtype), vcmp)
    n_sel = S // SEL_BLOCK
    m_sc = jnp.asarray(sel_from_cmp_matrix(n_c, n_sel))
    imp = jnp.einsum('bsgrc,jc->bsgj', p_c, m_sc)
    blk_id = jnp.arange(n_sel)[None, :]
    cur = (t_pos // SEL_BLOCK)[:, None]
    forced = (blk_id == 0) | (blk_id == cur) | (blk_id == cur - 1)
    future = blk_id > cur
    imp = jnp.where(forced[None, :, None, :], FORCE_SCORE,
                    jnp.where(future[None, :, None, :], NEG_INF, imp))
    k_top = min(SEL_TOPK, n_sel)
    _, sel_idx = lax.top_k(imp, k_top)
    ks = rms_norm(ks, ks_norm)
    kw = rms_norm(kw, kw_norm)
    k_blocks = ks.reshape(B, n_sel, SEL_BLOCK, G, Dh).transpose(0, 3, 1, 2, 4)
    v_blocks = vs.reshape(B, n_sel, SEL_BLOCK, G, Dh).transpose(0, 3, 1, 2, 4)
    kw_pad = jnp.pad(kw, ((0, 0), (WINDOW, 0), (0, 0), (0, 0)))
    vw_pad = jnp.pad(vw, ((0, 0), (WINDOW, 0), (0, 0), (0, 0)))
    nq = S // Q_BLOCK
    q_blocks = q.reshape(B, nq, Q_BLOCK, G, R, Dh).transpose(1, 0, 2, 3, 4, 5)
    idx_blocks = sel_idx.reshape(B, nq, Q_BLOCK, G, k_top).transpose(1, 0, 3, 2, 4)
    gather = jax.vmap(jax.vmap(lambda kb, ib: kb[ib]))

    def block_attn(args):
        i, qb, ib = args
        t = i * Q_BLOCK + jnp.arange(Q_BLOCK)
        ksel = gather(k_blocks, ib).reshape(B, G, Q_BLOCK, k_top * SEL_BLOCK, Dh)
        vsel = gather(v_blocks, ib).reshape(B, G, Q_BLOCK, k_top * SEL_BLOCK, Dh)
        kpos = (ib[..., None] * SEL_BLOCK + jnp.arange(SEL_BLOCK)).reshape(B, G, Q_BLOCK, k_top * SEL_BLOCK)
        smask = (kpos <= t[None, None, :, None]).transpose(0, 2, 1, 3)[:, :, :, None, :]
        s_s = jnp.einsum('bqgrd,bgqkd->bqgrk', qb, ksel)
        p_s = masked_softmax(s_s, smask)
        o_s = jnp.einsum('bqgrk,bgqkd->bqgrd', p_s.astype(vsel.dtype), vsel)
        kwin = lax.dynamic_slice_in_dim(kw_pad, i * Q_BLOCK, Q_BLOCK + WINDOW, axis=1)
        vwin = lax.dynamic_slice_in_dim(vw_pad, i * Q_BLOCK, Q_BLOCK + WINDOW, axis=1)
        wpos = i * Q_BLOCK - WINDOW + jnp.arange(Q_BLOCK + WINDOW)
        diff = t[:, None] - wpos[None, :]
        wmask = (wpos[None, :] >= 0) & (diff >= 0) & (diff < WINDOW)
        s_w = jnp.einsum('bqgrd,bkgd->bqgrk', qb, kwin)
        p_w = masked_softmax(s_w, wmask[None, :, None, None, :])
        o_w = jnp.einsum('bqgrk,bkgd->bqgrd', p_w.astype(vwin.dtype), vwin)
        return o_s, o_w

    o_sel, o_win = lax.map(block_attn, (jnp.arange(nq), q_blocks, idx_blocks))
    o_sel = o_sel.transpose(1, 0, 2, 3, 4, 5).reshape(B, S, G, R, Dh)
    o_win = o_win.transpose(1, 0, 2, 3, 4, 5).reshape(B, S, G, R, Dh)
    g = jax.nn.sigmoid(gates.astype(jnp.float32)).reshape(B, S, G, R, 3).astype(o_cmp.dtype)
    out = g[..., 0:1] * o_cmp + g[..., 1:2] * o_sel + g[..., 2:3] * o_win
    return out.reshape(B, S, NSA_HEADS, Dh)

def rotary(x, pos):
    half = x.shape[-1] // 2
    inv_freq = ROPE_BASE ** (-jnp.arange(half, dtype=jnp.float32) / half)
    ang = pos.astype(jnp.float32)[:, None] * inv_freq[None, :]
    cos, sin = jnp.cos(ang)[None, :, None, :], jnp.sin(ang)[None, :, None, :]
    x1, x2 = x[..., :half], x[..., half:]
    return jnp.concatenate([x1 * cos - x2 * sin, x1 * sin + x2 * cos], axis=-1)

def retention_mixer(q, k, v, g, out_norm):
    B, S = q.shape[:2]
    H, Dh, C = RET_HEADS, HEAD_DIM, RET_CHUNK
    f32 = jnp.float32
    pos = jnp.arange(S)
    q = rotary(q.reshape(B, S, H, Dh).astype(f32), pos)
    k = rotary(k.reshape(B, S, H, Dh).astype(f32), pos) * (Dh ** -0.5)
    v = v.reshape(B, S, H, Dh).astype(f32)
    log_gamma = jnp.log1p(-jnp.power(2.0, -5.0 - jnp.arange(H, dtype=f32)))
    n_ch = S // C
    i = jnp.arange(C, dtype=f32)
    rel = i[:, None] - i[None, :]
    decay = jnp.where(rel >= 0, jnp.exp(jnp.maximum(rel, 0.0)[None] * log_gamma[:, None, None]), 0.0)
    qc = q.reshape(B, n_ch, C, H, Dh)
    kc = k.reshape(B, n_ch, C, H, Dh)
    vc = v.reshape(B, n_ch, C, H, Dh)
    inner = jnp.einsum('bnihd,bnjhd->bnhij', qc, kc) * decay[None, None]
    o_inner = jnp.einsum('bnhij,bnjhd->bnihd', inner, vc)
    xi = jnp.exp((i + 1.0)[:, None] * log_gamma[None, :])
    zeta = jnp.exp((C - 1.0 - i)[:, None] * log_gamma[None, :])
    gamma_c = jnp.exp(C * log_gamma)

    def step(state, xs):
        qn, kn, vn = xs
        cross = jnp.einsum('bihd,bhde->bihe', qn, state) * xi[None, :, :, None]
        state = gamma_c[None, :, None, None] * state + jnp.einsum('bjhd,bjhe->bhde', kn * zeta[None, :, :, None], vn)
        return state, cross

    state0 = jnp.zeros((B, H, Dh, Dh), f32)
    _, o_cross = lax.scan(step, state0, (qc.transpose(1, 0, 2, 3, 4), kc.transpose(1, 0, 2, 3, 4), vc.transpose(1, 0, 2, 3, 4)))
    y = (o_inner + o_cross.transpose(1, 0, 2, 3, 4)).reshape(B, S, H, Dh)
    mu = jnp.mean(y, axis=-1, keepdims=True)
    var = jnp.mean(jnp.square(y - mu), axis=-1, keepdims=True)
    y = (y - mu) * lax.rsqrt(var + EPS) * out_norm.astype(f32).reshape(H, Dh)
    return (jax.nn.silu(g.astype(f32)).reshape(B, S, H, Dh) * y).astype(g.dtype)

def memory_cross_attention(x, mem, norm_x, norm_mem, wq, wkv, q_norm, k_norm, wo):
    B, S, _ = x.shape
    M = mem.shape[1]
    h = rms_norm(x, norm_x)
    hm = rms_norm(mem, norm_mem)
    q = rms_norm((h @ wq).reshape(B, S, MEM_HEADS, HEAD_DIM), q_norm) * (HEAD_DIM ** -0.5)
    k, v = jnp.split(hm @ wkv, 2, axis=-1)
    k = rms_norm(k.reshape(B, M, MEM_HEADS, HEAD_DIM), k_norm)
    v = v.reshape(B, M, MEM_HEADS, HEAD_DIM)
    p = jax.nn.softmax(jnp.einsum('bshd,bmhd->bhsm', q, k).astype(jnp.float32), axis=-1)
    o = jnp.einsum('bhsm,bmhd->bshd', p.astype(v.dtype), v).reshape(B, S, MEM_WIDTH)
    return o @ wo

def hierarchical_moe(x, norm_g, w_rg, b_rg, w_re, b_re, w_gate, w_up, w_down):
    B, S, Dm = x.shape
    T = B * S
    K = TOP_K_IN_GROUP
    h = rms_norm(x, norm_g).reshape(T, Dm)
    g_logits = (h @ w_rg).astype(jnp.float32) + b_rg.astype(jnp.float32)
    g_prob = jax.nn.softmax(g_logits, axis=-1)
    grp = jnp.argmax(g_logits, axis=-1)
    g_w = jnp.take_along_axis(g_prob, grp[:, None], axis=-1)
    e_all = jnp.einsum('td,gde->tge', h, w_re).astype(jnp.float32) + b_re.astype(jnp.float32)
    e_logits = jnp.take_along_axis(e_all, grp[:, None, None], axis=1)[:, 0]
    top_val, top_local = lax.top_k(e_logits, K)
    e_w = jax.nn.softmax(top_val, axis=-1) * g_w
    expert_id = grp[:, None] * EXPERTS_PER_GROUP + top_local
    A = T * K
    flat_e = expert_id.reshape(A)
    flat_tok = jnp.repeat(jnp.arange(T, dtype=jnp.int32), K)
    flat_w = e_w.reshape(A)
    order = jnp.argsort(flat_e)
    se, stok, sw = flat_e[order], flat_tok[order], flat_w[order]
    counts = jnp.bincount(flat_e, length=N_EXPERTS)
    start = jnp.cumsum(counts) - counts
    padded = (counts + MOE_BLOCK - 1) // MOE_BLOCK * MOE_BLOCK
    pend = jnp.cumsum(padded)
    pstart = pend - padded
    dest = pstart[se] + jnp.arange(A) - start[se]
    P = A + N_EXPERTS * MOE_BLOCK
    n_blocks = P // MOE_BLOCK
    row_tok = jnp.full((P,), T, jnp.int32).at[dest].set(stok)
    row_w = jnp.zeros((P,), h.dtype).at[dest].set(sw.astype(h.dtype))
    blk_e = jnp.minimum(jnp.searchsorted(pend, jnp.arange(n_blocks) * MOE_BLOCK, side='right'), N_EXPERTS - 1)
    h_pad = jnp.concatenate([h, jnp.zeros((1, Dm), h.dtype)], axis=0)
    x_rows = h_pad[row_tok].reshape(n_blocks, MOE_BLOCK, Dm)

    def expert_block(args):
        xb, e = args
        return (jax.nn.silu(xb @ w_gate[e]) * (xb @ w_up[e])) @ w_down[e]

    y_rows = lax.map(expert_block, (x_rows, blk_e)).reshape(P, Dm)
    y = jax.ops.segment_sum(y_rows * row_w[:, None], row_tok, num_segments=T + 1)[:T]
    return y.reshape(B, S, Dm)

def setup_inputs(seed: int = 0) -> dict:
    key = jax.random.key(seed)
    keys = iter(jax.random.split(key, 48))
    f32 = jnp.float32
    L, Dh, D = DEPTH, HEAD_DIM, D_MODEL

    def nrm(shape, scale):
        return jax.random.normal(next(keys), shape, f32) * scale

    def gain(shape):
        return 1.0 + nrm(shape, 0.02)

    return {
        'x': nrm((BATCH, SEQ, D), 1.0),
        'mem': nrm((BATCH, N_MEM, D), 1.0),
        'mix_norm': gain((L, D)),
        'w_in': nrm((L, D, PROJ_WIDTH), D ** -0.5),
        'nsa_q_norm': gain((L, Dh)),
        'nsa_kcmp_norm': gain((L, Dh)),
        'nsa_ksel_norm': gain((L, Dh)),
        'nsa_kwin_norm': gain((L, Dh)),
        'cmp_pos_k': nrm((L, CMP_BLOCK, Dh), 0.1),
        'cmp_pos_v': nrm((L, CMP_BLOCK, Dh), 0.1),
        'cmp_k_w1': nrm((L, CMP_BLOCK * Dh, CMP_HIDDEN), (CMP_BLOCK * Dh) ** -0.5),
        'cmp_k_w2': nrm((L, CMP_HIDDEN, Dh), CMP_HIDDEN ** -0.5),
        'cmp_v_w1': nrm((L, CMP_BLOCK * Dh, CMP_HIDDEN), (CMP_BLOCK * Dh) ** -0.5),
        'cmp_v_w2': nrm((L, CMP_HIDDEN, Dh), CMP_HIDDEN ** -0.5),
        'nsa_out_norm': gain((L, NSA_WIDTH)),
        'ret_out_norm': gain((L, RET_WIDTH)),
        'w_out': nrm((L, MIX_WIDTH, D), MIX_WIDTH ** -0.5),
        'mem_x_norm': gain((L, D)),
        'mem_kv_norm': gain((L, D)),
        'mem_wq': nrm((L, D, MEM_WIDTH), D ** -0.5),
        'mem_wkv': nrm((L, D, 2 * MEM_WIDTH), D ** -0.5),
        'mem_q_norm': gain((L, Dh)),
        'mem_k_norm': gain((L, Dh)),
        'mem_wo': nrm((L, MEM_WIDTH, D), MEM_WIDTH ** -0.5),
        'ffn_norm': gain((L, D)),
        'router_group_w': nrm((L, D, N_GROUPS), D ** -0.5),
        'router_group_b': nrm((L, N_GROUPS), 0.01),
        'router_expert_w': nrm((L, N_GROUPS, D, EXPERTS_PER_GROUP), D ** -0.5),
        'router_expert_b': nrm((L, N_GROUPS, EXPERTS_PER_GROUP), 0.01),
        'exp_w_gate': nrm((L, N_EXPERTS, D, EXPERT_FF), D ** -0.5),
        'exp_w_up': nrm((L, N_EXPERTS, D, EXPERT_FF), D ** -0.5),
        'exp_w_down': nrm((L, N_EXPERTS, EXPERT_FF, D), EXPERT_FF ** -0.5),
    }

def reference(x, mem, mix_norm, w_in, nsa_q_norm, nsa_kcmp_norm, nsa_ksel_norm, nsa_kwin_norm,
              cmp_pos_k, cmp_pos_v, cmp_k_w1, cmp_k_w2, cmp_v_w1, cmp_v_w2,
              nsa_out_norm, ret_out_norm, w_out,
              mem_x_norm, mem_kv_norm, mem_wq, mem_wkv, mem_q_norm, mem_k_norm, mem_wo,
              ffn_norm, router_group_w, router_group_b, router_expert_w, router_expert_b,
              exp_w_gate, exp_w_up, exp_w_down):
    B, S, _ = x.shape
    G, Dh = NSA_KV_GROUPS, HEAD_DIM
    for l in range(DEPTH):
        h = rms_norm(x, mix_norm[l])
        proj = h @ w_in[l]
        q_a, kv_a, gate_a, ret_a = jnp.split(proj, list(PROJ_SPLIT_POINTS), axis=-1)
        kc, vc, ks, vs, kw, vw = jnp.split(kv_a.reshape(B, S, 6, G, Dh), 6, axis=2)
        o_a = nsa_mixer(q_a, kc[:, :, 0], vc[:, :, 0], ks[:, :, 0], vs[:, :, 0], kw[:, :, 0], vw[:, :, 0], gate_a,
                        nsa_q_norm[l], nsa_kcmp_norm[l], nsa_ksel_norm[l], nsa_kwin_norm[l],
                        cmp_pos_k[l], cmp_pos_v[l], cmp_k_w1[l], cmp_k_w2[l], cmp_v_w1[l], cmp_v_w2[l])
        o_a = rms_norm(o_a, nsa_out_norm[l].reshape(NSA_HEADS, Dh)).reshape(B, S, NSA_WIDTH)
        q_r, k_r, v_r, g_r = jnp.split(ret_a, 4, axis=-1)
        o_b = retention_mixer(q_r, k_r, v_r, g_r, ret_out_norm[l]).reshape(B, S, RET_WIDTH)
        x = x + jnp.concatenate([o_a, o_b], axis=-1) @ w_out[l]
        x = x + memory_cross_attention(x, mem, mem_x_norm[l], mem_kv_norm[l], mem_wq[l], mem_wkv[l],
                                       mem_q_norm[l], mem_k_norm[l], mem_wo[l])
        x = x + hierarchical_moe(x, ffn_norm[l], router_group_w[l], router_group_b[l],
                                 router_expert_w[l], router_expert_b[l],
                                 exp_w_gate[l], exp_w_up[l], exp_w_down[l])
    return x


_drawn_inputs = setup_inputs


def setup_inputs(seed=0):
    import zlib

    import numpy as np

    out = dict(_drawn_inputs(seed))
    spreads = {}
    factors = {'nsa_q_norm': 3.144,
     'nsa_kcmp_norm': 2.951,
     'nsa_ksel_norm': 5.447,
     'nsa_kwin_norm': 6.598,
     'nsa_out_norm': 3.29,
     'ret_out_norm': 4.91,
     'mem_x_norm': 8.0,
     'mem_kv_norm': 8.0,
     'mem_q_norm': 8.0,
     'mem_k_norm': 8.0,
     'router_group_b': 64.0,
     'router_expert_b': 39.224,
     'ffn_norm': 8.0}
    for name, (base, spread) in spreads.items():
        noise = np.random.default_rng([zlib.crc32(name.encode()), seed]).standard_normal(out[name].shape)
        drawn = base * np.exp(spread * noise) if base else spread * noise
        out[name] = __import__('jax').numpy.asarray(drawn.astype(out[name].dtype))
    for name, factor in factors.items():
        out[name] = (out[name] * factor).astype(out[name].dtype)
    return out
```

```python
from contextlib import ExitStack

import numpy as np
import concourse.bass as bass
from concourse import mybir

F32 = mybir.dt.float32
BF16 = mybir.dt.bfloat16
I32 = mybir.dt.int32
ALU = mybir.AluOpType
ACT = mybir.ActivationFunctionType
AX = mybir.AxisListType

P = 128
D = 1024
S = 1024
KT = D // P
NT = S // P
HD = 64
NH = 8
NG = 2
HPG = NH // NG
PROJ = 3352
NMEM = 256
MH = 4
NC = 64
NCR = 63
CB = 32
CS = 16
NSEL = 16
NE = 32
EG = 8
FF = 256
MAXI = 48
SLOTS = 4
MASKED = -1e30
TAKEN = -3e38
EPS = 1e-6

CHUNKS = [(1304, 512), (1816, 512), (2328, 512), (0, 512), (512, 512), (1024, 280), (2840, 512)]
RQ, RK, RV, Q, KV1, KV2, RG = range(7)



def pack(items):
    at, places = 0, {}
    for name, n in items:
        places[name] = (at, n)
        at += n
    return places, at


EARLY, NEARLY = pack([("ident", 128), ("tri", 128), ("gammac", 512)])
MIDDLE, NMIDDLE = pack([("causal", 128), ("window", 128), ("cbias", 512), ("cmask", 512), ("impa", 128), ("impb", 128),
                        ("selm", 16), ("esel", 1024)])
LATE, NLATE = pack([("before", 128), ("ones", 128), ("iota", 128), ("thr", 16), ("eid", 32), ("pref8", 8),
                    ("tokid", 8), ("item", 48), ("thr4", 4)])


class Chain:

    def __init__(self, eng, sem, base=0):
        self.eng, self.sem, self.base, self.n = eng, sem, base, 0

    def __call__(self, ins):
        ins.then_inc(self.sem, 1)
        self.n += 1
        self.eng.wait_ge(self.sem, self.base + self.n)


class Memory:

    def __init__(self):
        self.taken = []


def phase_semaphores(nc, m):
    def take(name):
        m.taken.append(nc.alloc_semaphore(name=name))
        return m.taken[-1]

    return take


def bc(ap, shape):
    return ap.to_broadcast(shape)


def heads(ap, n=NH):
    return ap.rearrange("p (h d) -> p h d", h=n)


def phase_project(nc, m, io):
    with ExitStack() as st:
        sem = phase_semaphores(nc, m)
        sb = lambda n, s, d=F32: st.enter_context(nc.sbuf_tensor(n, s, d))
        ps = lambda n: st.enter_context(nc.psum_tensor(n, [P, 512], F32))
        x = sb("x", [P, D])
        grow = sb("grow", [P, D])
        xs = sb("xs", [P, D])
        xT = sb("xT", [P, KT, P])
        rope = sb("rope", [P, 4, 256])
        raw = sb("raw", [P, 7, 512])
        rq, rk, t1, t2 = [sb(n, [P, 512]) for n in "rq rk t1 t2".split()]
        yc, qn = t2, rq
        rqT = sb("rqT", [P, 4, P])
        rkT = sb("rkT", [P, 4, P])
        inT = sb("inT", [P, NH, P])
        qT = sb("qT", [P, 512])
        kd = sb("kd", [P, 2, NG, 2, HD])
        state = sb("state", [P, 4, P])
        gret = sb("gret", [P, 512])
        sg = sb("sg", [P, 512])
        ssx = sb("ssx", [P, 1])
        stat = sb("stat", [P, 16])
        pw = sb("pw", [P, 16])
        ystat = sb("ystat", [P, 16])
        ypw = sb("ypw", [P, 8])
        tp = [ps("tp0"), ps("tp1")]
        pj = [ps("pj0"), ps("pj1")]
        inn = [ps("in0"), ps("in1")]
        yp, sp_ = ps("yp"), ps("stp")
        s = {n: sem("p_" + n) for n in (
            "const_in gret_in x_in rope_in sq xs turned evac proj raw roped inner masked outer ready2 upd y "
            "ms rs qn yms yrs sig qout out oout chain qgain").split()}
        w_in_sem = [sem(f"w_in{c}") for c in range(7)]
        w, at = {}, 0
        for c in (RV, Q, KV1, KV2, RG, RQ, RK):
            n = CHUNKS[c][1]
            w[c] = m.arena[:, at:at + KT * n].rearrange("p (k n) -> p k n", k=KT)
            at += KT * n
        NCH = 21
        xv = io["x"].rearrange("(t p) d -> t p d", p=P)
        rv = io["rope"].rearrange("(t p) n -> t p n", p=P)
        ocv = m.oc_d.rearrange("(t p) d -> t p d", p=P)

        def tiles(eng, body):
            with eng.Fori(0, NT - 1) as i:
                body(i, False)
            body(NT - 1, True)

        with nc.Block() as block:

            @block.sync
            def _(sp):
                sp.dma_start(x[:], xv[0]).then_inc(s["x_in"], 16)
                sp.dma_start(grow[:], io["g_mix"]).then_inc(s["const_in"], 16)
                sp.dma_start(m.early[:], io["early"]).then_inc(s["const_in"], 16)
                sp.dma_start(m.gcol[:], io["gcol"]).then_inc(s["const_in"], 16)
                for c in range(7):
                    at, n = CHUNKS[c]
                    sp.dma_start(w[c], io["w_in"].rearrange("(k p) n -> p k n", p=P)[:, :, at:at + n]
                                 ).then_inc(w_in_sem[c], 16)
                    if c == 0:
                        sp.dma_start(rope[:].rearrange("p a b -> p (a b)"), rv[0]).then_inc(s["rope_in"], 16)
                sp.dma_start(gret[:], io["g_out"][:, 512:1024]).then_inc(s["gret_in"], 16)

                def body(i, last):
                    if not last:
                        sp.wait_ge(s["xs"], i + 1)
                        sp.dma_start(x[:], xv[i + 1]).then_inc(s["x_in"], 16)
                        sp.wait_ge(s["roped"], 2 * i + 2)
                        sp.dma_start(rope[:].rearrange("p a b -> p (a b)"), rv[i + 1]).then_inc(s["rope_in"], 16)
                    sp.wait_ge(s["evac"], 7 * i + 5)
                    sp.dma_start(m.q_d[i], qT[:]).then_inc(s["qout"], 16)
                    sp.wait_ge(s["out"], i + 1)
                    sp.dma_start(ocv[i, :, 512:1024], sg[:]).then_inc(s["oout"], 16)

                with sp.Fori(0, NT - 1) as i:
                    body(i, False)
                sp.wait_ge(s["proj"], 7 * (NT - 1) + RK + 1)
                for a, w1 in enumerate((io["cmp_k_w1"], io["cmp_v_w1"])):
                    for half in range(2):
                        sp.dma_start(m.w1[HD * half:HD * half + HD, a, :].rearrange("d (p n) -> d p n", p=CB),
                                     w1.rearrange("(p d) n -> d p n", d=HD)).then_inc(m.w1_in[a], 16)
                body(NT - 1, True)
                sp.wait_ge(s["qout"], 16 * NT)
                sp.wait_ge(s["oout"], 16 * NT)

            @block.scalar
            def _(act):
                squares = raw[:, Q:Q + 2, :].rearrange("p a b -> p (a b)")

                def square(i):
                    act.wait_ge(s["x_in"], 16 * i + 16)
                    nc.scalar.activation(squares, x[:], ACT.Square, accum_out=ssx[:]).then_inc(s["sq"], 1)

                def turn_x(u):
                    for h in range(2):
                        act.wait_ge(s["turned"], u + h + 1)
                        nc.scalar.activation(xT[:, 4 * h:4 * h + 4, :],
                                             tp[1 - h][:].rearrange("p (k q) -> p k q", k=4),
                                             ACT.Copy).then_inc(s["evac"], 1)

                def evac(i, c):
                    act.wait_ge(s["proj"], 7 * i + c + 1)
                    n = CHUNKS[c][1]
                    src = inn[0] if c == RG else pj[c % 2]
                    nc.scalar.activation(raw[:, c, 0:n], src[:, 0:n], ACT.Copy).then_inc(s["raw"], 1)

                def body(i, last):
                    u = 2 + 7 * i
                    evac(i, RQ)
                    if not last:
                        square(i + 1)
                    evac(i, RK)
                    for n, dst in enumerate((rqT, rkT)):
                        act.wait_ge(s["turned"], u + n + 1)
                        nc.scalar.activation(dst[:], tp[n][:].rearrange("p (k q) -> p k q", k=4),
                                             ACT.Copy).then_inc(s["evac"], 1)
                        evac(i, RV + n)
                    evac(i, KV1)
                    evac(i, KV2)
                    act.wait_ge(s["raw"], 7 * i + 6)
                    nc.scalar.activation(m.gate[:, bass.ts(i, 24)], raw[:, KV2, 256:280], ACT.Sigmoid)
                    evac(i, RG)
                    act.wait_ge(s["raw"], 7 * i + 7)
                    act.wait_ge(s["oout"], 16 * i)
                    nc.scalar.activation(sg[:], raw[:, RG, :], ACT.Sigmoid).then_inc(s["sig"], 1)
                    act.wait_ge(s["turned"], u + 3)
                    act.wait_ge(s["qout"], 16 * i)
                    nc.scalar.activation(qT[:], tp[0][:], ACT.Copy, scale=m.qgain[:]).then_inc(s["evac"], 1)
                    act.wait_ge(s["turned"], u + 4)
                    nc.scalar.activation(m.kcvcT[:, :, bass.ts(i, P)],
                                         tp[1][:, 0:256].rearrange("p (a q) -> p a q", a=2), ACT.Copy)
                    nc.scalar.activation(m.ksT[:, :, bass.ts(i, P)],
                                         tp[1][:, 256:512].rearrange("p (a q) -> p a q", a=2), ACT.Copy,
                                         scale=m.gcol[:, 1:2]).then_inc(s["evac"], 1)
                    act.wait_ge(s["turned"], u + 5)
                    nc.scalar.activation(m.kwT[:, :, bass.ts(i, P)],
                                         tp[0][:, 0:256].rearrange("p (a q) -> p a q", a=2), ACT.Copy,
                                         scale=m.gcol[:, 2:3]).then_inc(s["evac"], 1)
                    if not last:
                        turn_x(u + 5)

                square(0)
                turn_x(0)
                act.wait_ge(s["qgain"], 1)
                tiles(act, body)

            @block.gpsimd
            def _(pool):
                def body(i, last):
                    pool.wait_ge(s["raw"], 7 * i + 6)
                    nc.gpsimd.tensor_copy(m.vs[:, bass.ts(i, P)], raw[:, KV1, 384:512])
                    nc.gpsimd.tensor_copy(m.vw[:, bass.ts(i, P)], raw[:, KV2, 128:256])
                    pool.wait_ge(s["ms"], i + 2)
                    nc.gpsimd.tensor_tensor(pw[:], stat[:], m.mhalf[:, 0:16], ALU.pow).then_inc(s["rs"], 1)
                    pool.wait_ge(s["yms"], i + 1)
                    nc.gpsimd.tensor_tensor(ypw[:], ystat[:, 0:8], m.mhalf[:, 0:8], ALU.pow).then_inc(s["yrs"], 1)

                pool.wait_ge(s["ms"], 1)
                nc.gpsimd.tensor_tensor(pw[:, 12:13], stat[:, 12:13], m.mhalf[:, 0:1], ALU.pow).then_inc(s["rs"], 1)
                tiles(pool, body)

            @block.vector
            def _(dve):
                def rotate(done, src, dst, cos, sin, last_sem):
                    v = src.rearrange("p (h a d) -> p h a d", h=NH, a=2)
                    o = dst[:].rearrange("p (h a d) -> p h a d", h=NH, a=2)
                    a = t1[:].rearrange("p (h a d) -> p h a d", h=NH, a=2)
                    b = t2[:].rearrange("p (h a d) -> p h a d", h=NH, a=2)
                    c = rope[:, cos, :].rearrange("p (h o d) -> p h o d", h=NH, o=1)
                    sn = rope[:, sin, :].rearrange("p (h o d) -> p h o d", h=NH, o=1)
                    done(nc.vector.tensor_tensor(a, v, bc(c, [P, NH, 2, 32]), ALU.mult))
                    done(nc.vector.tensor_tensor(b, v, bc(sn, [P, NH, 2, 32]), ALU.mult))
                    done(nc.vector.tensor_tensor(o[:, :, 0], a[:, :, 0], b[:, :, 1], ALU.subtract))
                    nc.vector.tensor_tensor(o[:, :, 1], b[:, :, 0], a[:, :, 1], ALU.add).then_inc(last_sem, 1)

                def norm_x(i):
                    nc.vector.scalar_tensor_tensor(xs[:], x[:], pw[:, 12:13], grow[:], ALU.mult,
                                                   ALU.mult).then_inc(s["xs"], 1)
                    dve.wait_ge(s["xs"], i + 1)

                def body(i, last):
                    done = Chain(dve, s["chain"], 4 + NCH * i)
                    dve.wait_ge(s["rope_in"], 16 * i + 16)
                    dve.wait_ge(s["raw"], 7 * i + 1)
                    rotate(done, raw[:, RQ, :], rq, 0, 1, s["roped"])
                    dve.wait_ge(s["roped"], 2 * i + 1)
                    dve.wait_ge(s["raw"], 7 * i + 2)
                    rotate(done, raw[:, RK, :], rk, 2, 3, s["roped"])
                    dve.wait_ge(s["roped"], 2 * i + 2)
                    for h in range(2):
                        dve.wait_ge(s["inner"], 2 * i + h + 1)
                        nc.vector.tensor_tensor(inT[:].rearrange("p (a b) q -> p b a q", b=2)[:, h],
                                                inn[h][:].rearrange("p (a q) -> p a q", a=4),
                                                bc(m.c("tri").unsqueeze(1), [P, 4, P]), ALU.mult).then_inc(s["masked"], 1)
                        dve.wait_ge(s["masked"], 2 * i + h + 1)
                    dve.wait_ge(s["raw"], 7 * i + 6)
                    done(nc.vector.tensor_tensor(t1[:], raw[:, Q, :], raw[:, Q, :], ALU.mult))
                    done(nc.vector.tensor_reduce(stat[:, 0:8], heads(t1[:]), AX.X, ALU.add))
                    done(nc.vector.tensor_tensor(t1[:, 0:128], raw[:, KV1, 256:384], raw[:, KV1, 256:384], ALU.mult))
                    done(nc.vector.tensor_tensor(t1[:, 128:256], raw[:, KV2, 0:128], raw[:, KV2, 0:128], ALU.mult))
                    done(nc.vector.tensor_reduce(stat[:, 8:12], heads(t1[:, 0:256], 4), AX.X, ALU.add))
                    if last:
                        nc.vector.tensor_scalar(stat[:, 0:12], stat[:, 0:12], 1.0 / HD, EPS, ALU.mult,
                                                ALU.add).then_inc(s["ms"], 1)
                    else:
                        done(nc.vector.tensor_scalar(stat[:, 0:12], stat[:, 0:12], 1.0 / HD, EPS, ALU.mult, ALU.add))
                        dve.wait_ge(s["sq"], i + 2)
                        nc.vector.tensor_scalar(stat[:, 12:13], ssx[:], 1.0 / D, EPS, ALU.mult,
                                                ALU.add).then_inc(s["ms"], 1)
                    dve.wait_ge(s["rs"], i + 2)
                    nc.vector.tensor_tensor(heads(qn[:]), heads(raw[:, Q, :]),
                                            bc(pw[:, 0:8].unsqueeze(2), [P, NH, HD]), ALU.mult).then_inc(s["qn"], 1)
                    for b, (c, at) in enumerate(((KV1, 256), (KV2, 0))):
                        for dup in range(2):
                            nc.vector.tensor_tensor(kd[:, b, :, dup, :], heads(raw[:, c, at:at + 128], 2),
                                                    bc(pw[:, 8 + 2 * b:10 + 2 * b].unsqueeze(2), [P, NG, HD]),
                                                    ALU.mult).then_inc(s["qn"], 1)
                    dve.wait_ge(s["qn"], 5 * i + 5)
                    dve.wait_ge(s["y"], i + 1)
                    dve.wait_ge(s["upd"], i + 1)
                    st2 = state[:].rearrange("p a b -> p (a b)")
                    done(nc.vector.tensor_tensor(st2, st2, sp_[:], ALU.add))
                    nc.vector.tensor_tensor(st2, st2, m.c("gammac"), ALU.mult).then_inc(s["ready2"], 1)
                    dve.wait_ge(s["ready2"], i + 2)
                    if not last:
                        norm_x(i + 1)
                    done(nc.vector.tensor_reduce(ystat[:, 0:8], heads(yp[:]), AX.X, ALU.add))
                    done(nc.vector.tensor_scalar(ystat[:, 8:16], ystat[:, 0:8], 1.0 / HD, None, ALU.mult))
                    done(nc.vector.tensor_tensor(heads(yc[:]), heads(yp[:]),
                                                 bc(ystat[:, 8:16].unsqueeze(2), [P, NH, HD]), ALU.subtract))
                    done(nc.vector.tensor_tensor(t1[:], yc[:], yc[:], ALU.mult))
                    done(nc.vector.tensor_reduce(ystat[:, 0:8], heads(t1[:]), AX.X, ALU.add))
                    nc.vector.tensor_scalar(ystat[:, 0:8], ystat[:, 0:8], 1.0 / HD, EPS, ALU.mult,
                                            ALU.add).then_inc(s["yms"], 1)
                    dve.wait_ge(s["sig"], i + 1)
                    done(nc.vector.tensor_tensor(t1[:], raw[:, RG, :], sg[:], ALU.mult))
                    dve.wait_ge(s["gret_in"], 16)
                    done(nc.vector.tensor_tensor(t1[:], t1[:], gret[:], ALU.mult))
                    dve.wait_ge(s["yrs"], i + 1)
                    done(nc.vector.tensor_tensor(heads(yc[:]), heads(yc[:]), bc(ypw[:].unsqueeze(2), [P, NH, HD]),
                                                 ALU.mult))
                    nc.vector.tensor_tensor(sg[:], yc[:], t1[:], ALU.mult).then_inc(s["out"], 1)
                    dve.wait_ge(s["out"], i + 1)
                    if not last:
                        assert done.n == NCH, done.n

                done = Chain(dve, s["chain"])
                done(nc.vector.memset(m.mhalf[:], -0.5))
                done(nc.vector.memset(stat[:], 1.0))
                done(nc.vector.memset(pw[:], 1.0))
                nc.vector.memset(state[:], 0.0).then_inc(s["ready2"], 1)
                dve.wait_ge(s["sq"], 1)
                nc.vector.tensor_scalar(stat[:, 12:13], ssx[:], 1.0 / D, EPS, ALU.mult, ALU.add).then_inc(s["ms"], 1)
                dve.wait_ge(s["rs"], 1)
                dve.wait_ge(s["const_in"], 48)
                norm_x(0)
                done(nc.vector.tensor_scalar(m.qgain[:], m.gcol[:, 0:1], HD ** -0.5, None, ALU.mult))
                nc.vector.tensor_scalar(m.mqgain[:], m.gcol[:, 3:4], HD ** -0.5, None, ALU.mult).then_inc(s["qgain"], 1)
                tiles(dve, body)

            @block.tensor
            def _(pe):
                def turn(bank, pieces):
                    for k, p in enumerate(pieces):
                        last = nc.tensor.transpose(tp[bank][:, k * P:(k + 1) * P], p, m.c("ident"))
                    last.then_inc(s["turned"], 1)

                def turn_x(i, u):
                    pe.wait_ge(s["xs"], i + 1)
                    for h in range(2):
                        if not isinstance(u, int) or u + h > 1:
                            pe.wait_ge(s["evac"], u + h - 1)
                        turn(1 - h, [xs[:, (4 * h + k) * P:(4 * h + k + 1) * P] for k in range(4)])

                def project(i, c):
                    n = CHUNKS[c][1]
                    if c == 0:
                        pe.wait_ge(s["evac"], 2 + 7 * i)
                    elif c >= 2:
                        pe.wait_ge(s["raw"], 7 * i + c - 1)
                    pe.wait_ge(w_in_sem[c], 16)
                    dst = inn[0] if c == RG else pj[c % 2]
                    for k in range(KT):
                        last = nc.tensor.matmul(dst[:, 0:n], xT[:, k, :], w[c][:, k, :],
                                                start=k == 0, stop=k == KT - 1)
                    last.then_inc(s["proj"], 1)

                def body(i, last_tile):
                    u = 2 + 7 * i
                    project(i, RQ)
                    project(i, RK)
                    pe.wait_ge(s["roped"], 2 * i + 1)
                    turn(0, [rq[:, k * P:(k + 1) * P] for k in range(4)])
                    project(i, RV)
                    pe.wait_ge(s["roped"], 2 * i + 2)
                    turn(1, [rk[:, k * P:(k + 1) * P] for k in range(4)])
                    project(i, Q)
                    pe.wait_ge(s["evac"], u + 2)
                    for h in [0, 2, 4, 6, 1, 3, 5, 7]:
                        r = slice(HD * (h % 2), HD * (h % 2) + HD)
                        last = nc.tensor.matmul(inn[h % 2][:, (h // 2) * P:(h // 2 + 1) * P], rkT[r, h // 2, :],
                                                rqT[r, h // 2, :], start=True, stop=True)
                        if h >= 6:
                            last.then_inc(s["inner"], 1)
                    pe.wait_ge(s["raw"], 7 * i + 3)
                    for a in range(4):
                        last = nc.tensor.matmul(sp_[:, a * P:(a + 1) * P], rk[:, a * P:(a + 1) * P],
                                                raw[:, RV, a * P:(a + 1) * P], start=True, stop=True)
                    last.then_inc(s["upd"], 1)
                    project(i, KV1)
                    pe.wait_ge(s["masked"], 2 * i + 2)
                    pe.wait_ge(s["ready2"], i + 1)
                    for a in range(4):
                        nc.tensor.matmul(yp[:, a * P:(a + 1) * P], rqT[:, a, :], state[:, a, :], start=True,
                                         stop=False)
                        for h in (2 * a, 2 * a + 1):
                            last = nc.tensor.matmul(yp[:, h * HD:(h + 1) * HD], inT[:, h, :],
                                                    raw[:, RV, h * HD:(h + 1) * HD], start=False, stop=h % 2 == 1)
                    last.then_inc(s["y"], 1)
                    project(i, KV2)
                    project(i, RG)
                    pe.wait_ge(s["qn"], 5 * i + 1)
                    pe.wait_ge(s["evac"], u + 1)
                    turn(0, [qn[:, k * P:(k + 1) * P] for k in range(4)])
                    pe.wait_ge(s["qn"], 5 * i + 5)
                    turn(1, [raw[:, KV1, 0:128], raw[:, KV1, 128:256]] +
                         [kd[:, 0, g].rearrange("p a d -> p (a d)") for g in range(NG)])
                    pe.wait_ge(s["evac"], u + 3)
                    turn(0, [kd[:, 1, g].rearrange("p a d -> p (a d)") for g in range(NG)])
                    if not last_tile:
                        turn_x(i + 1, u + 5)

                pe.wait_ge(s["const_in"], 48)
                turn_x(0, 0)
                tiles(pe, body)


def phase_keys(nc, m, io):
    T = 2
    with ExitStack() as st:
        sem = phase_semaphores(nc, m)
        sb = lambda n, s, d=F32: st.enter_context(nc.sbuf_tensor(n, s, d))
        ps = lambda n: st.enter_context(nc.psum_tensor(n, [P, 512], F32))
        w2 = sb("cw2", [P, 2, HD])
        pos = sb("cpos", [P, 2, CB])
        blk = sb("cblk", [P, CB, NC])
        sg = sb("csg", [P, 2 * NCR])
        hid = sb("chid", [P, 2, 2 * NCR])
        kc = sb("ckc", [NC, NG, HD])
        kn = sb("ckn", [NC, NG, 2, HD])
        stat = sb("cstat", [NC, 2])
        pw = sb("cpw", [NC, 2])
        spare = m.arena[:, 2 * m.slot_size:]
        wkv = spare[:, 0:KT * 512].rearrange("p (k n) -> p k n", k=KT)
        mem = spare[:, KT * 512:KT * 512 + T * D].rearrange("p (t d) -> p t d", t=T)
        hT = sb("memT", [P, KT, NMEM])
        squares = hT[:, 0:4, :].rearrange("p k q -> p (k q)")
        kv = sb("memkv", [P, T, 512])
        mkn = sb("memkn", [P, T, 256])
        mstat = sb("memstat", [P, 4 * T])
        mpw = sb("mempw", [P, 4 * T])
        gmem = sb("gmem", [P, D])
        hp = [ps(f"chp{g}") for g in range(NG)]
        op, ctp = ps("cop"), ps("ctp")
        tp = [ps("mtp0"), ps("mtp1")]
        pj = [ps("mpj0"), ps("mpj1")]
        s = {n: sem("k_" + n) for n in (
            "w2_in late_in blk hid sig act out ms rs kn cturned chain wkv_in mem_in ssq mms mrs normed turned evac "
            "projected kraw kready cleared").split()}
        with nc.Block() as block:

            @block.sync
            def _(sp):
                sp.dma_start(mem, io["mem"].rearrange("(t p) d -> p t d", p=P)).then_inc(s["mem_in"], 16)
                sp.dma_start(gmem[:], io["g_memkv"]).then_inc(s["mem_in"], 16)
                for a in range(2):
                    sp.dma_start(w2[:, a, :], (io["cmp_k_w2"], io["cmp_v_w2"])[a]).then_inc(s["w2_in"], 16)
                sp.dma_start(pos[:].rearrange("p a b -> p (a b)"), io["cmp_pos"]).then_inc(s["w2_in"], 16)
                sp.dma_start(wkv, io["mem_wkv"].rearrange("(k p) n -> p k n", p=P)).then_inc(s["wkv_in"], 16)
                sp.dma_start(m.middle[:], io["middle"]).then_inc(s["late_in"], 16)
                sp.dma_start(m.gout[:], io["g_out"][:, 0:512]).then_inc(s["late_in"], 16)
                for e in range(2):
                    load_expert(sp, m, io, e, e)

            @block.scalar
            def _(act):
                def gates(a):
                    act.wait_ge(s["hid"], a + 1)
                    if a:
                        act.wait_ge(s["act"], 2)
                    for g in range(NG):
                        nc.scalar.activation(sg[:, g * NCR:(g + 1) * NCR], hp[g][:, 0:NCR],
                                             ACT.Sigmoid).then_inc(s["sig"], 1)

                act.wait_ge(s["mem_in"], 32)
                for t in range(T):
                    nc.scalar.activation(squares, mem[:, t], ACT.Square, accum_out=mstat[:, t:t + 1]).then_inc(s["ssq"], 1)
                    act.wait_ge(s["ssq"], t + 1)
                gates(0)
                for n in range(4):
                    act.wait_ge(s["turned"], n + 1)
                    t, h = divmod(n, 2)
                    nc.scalar.activation(hT[:, 4 * h:4 * h + 4, t * P:(t + 1) * P],
                                         tp[n % 2][:].rearrange("p (k q) -> p k q", k=4), ACT.Copy).then_inc(s["evac"], 1)
                for t in range(T):
                    act.wait_ge(s["projected"], t + 1)
                    nc.scalar.activation(kv[:, t], pj[t][:], ACT.Copy).then_inc(s["kraw"], 1)
                gates(1)
                act.wait_ge(s["cleared"], 1)
                for t in range(T):
                    act.wait_ge(s["turned"], 4 + t + 1)
                    for half in range(2):
                        r = slice(HD * half, HD * half + HD)
                        nc.scalar.activation(m.kmT[r, :, half, t * P:(t + 1) * P],
                                             tp[t % 2][r, 0:256].rearrange("p (k q) -> p k q", k=2), ACT.Copy,
                                             scale=m.gcol[r, 4:5])
                act.wait_ge(s["cturned"], 1)
                for half in range(2):
                    r = slice(HD * half, HD * half + HD)
                    nc.scalar.activation(m.kcT[r, :, half, 0:NCR],
                                         ctp[r, 0:2 * NCR].rearrange("p (g c) -> p g c", g=NG),
                                         ACT.Copy, scale=m.gcol[r, 5:6])

            @block.gpsimd
            def _(pool):
                pool.wait_ge(s["mms"], 1)
                nc.gpsimd.tensor_tensor(mpw[:, 0:T], mstat[:, T:2 * T], m.mhalf[:, 0:T], ALU.pow).then_inc(s["mrs"], 1)
                for t in range(T):
                    pool.wait_ge(s["kraw"], t + 1)
                    nc.gpsimd.tensor_copy(m.vm[:, t], kv[:, t, 256:512])
                pool.wait_ge(s["mms"], 2)
                nc.gpsimd.tensor_tensor(mpw[:], mstat[:], m.mhalf[:, 0:4 * T], ALU.pow).then_inc(s["mrs"], 1)
                pool.wait_ge(s["ms"], 1)
                nc.gpsimd.tensor_tensor(pw[0:NCR], stat[0:NCR], m.mhalf[0:NCR, 0:2], ALU.pow).then_inc(s["rs"], 1)

            @block.vector
            def _(dve):
                done = Chain(dve, s["chain"])

                def blocks(a):
                    if a:
                        dve.wait_ge(s["hid"], a)
                    for half in range(2):
                        v = m.kcvcT[:, a, half * CS: half * CS + CS * NCR]
                        nc.vector.tensor_tensor(blk[:, half * CS:half * CS + CS, 0:NCR],
                                                v.rearrange("p (c q) -> p q c", q=CS),
                                                bc(pos[:, a, half * CS:half * CS + CS].unsqueeze(2), [P, CS, NCR]),
                                                ALU.add).then_inc(s["blk"], 1)

                def hidden(a):
                    dve.wait_ge(s["sig"], 2 * a + 2)
                    for g in range(NG):
                        c = slice(g * NCR, (g + 1) * NCR)
                        nc.vector.tensor_tensor(hid[:, a, c], hp[g][:, 0:NCR], sg[:, c], ALU.mult).then_inc(s["act"], 1)

                dve.wait_ge(s["w2_in"], 48)
                blocks(0)
                done(nc.vector.memset(m.kcT[:], 0.0))
                done(nc.vector.memset(m.vc[:], 0.0))
                nc.vector.memset(m.kmT[:], 0.0).then_inc(s["cleared"], 1)
                dve.wait_ge(s["ssq"], T)
                nc.vector.tensor_scalar(mstat[:, T:2 * T], mstat[:, 0:T], 1.0 / D, EPS, ALU.mult,
                                        ALU.add).then_inc(s["mms"], 1)
                dve.wait_ge(s["mem_in"], 32)
                dve.wait_ge(s["mrs"], 1)
                for t in range(T):
                    nc.vector.scalar_tensor_tensor(mem[:, t], mem[:, t], mpw[:, t:t + 1], gmem[:], ALU.mult,
                                                   ALU.mult).then_inc(s["normed"], 1)
                hidden(0)
                blocks(1)
                dve.wait_ge(s["late_in"], 32)
                done(nc.vector.tensor_copy(m.identb[:], m.c("ident")))
                done(nc.vector.tensor_copy(m.causalb[:], m.c("causal")))
                done(nc.vector.tensor_copy(m.windowb[:], m.c("window")))
                done(nc.vector.tensor_copy(m.eselb[:], m.c("esel")))
                dve.wait_ge(s["kraw"], T)
                done(nc.vector.tensor_tensor(mkn[:], kv[:, :, 0:256], kv[:, :, 0:256], ALU.mult))
                done(nc.vector.tensor_reduce(mstat[:], mkn[:].rearrange("p t (h d) -> p (t h) d", d=HD), AX.X, ALU.add))
                nc.vector.tensor_scalar(mstat[:], mstat[:], 1.0 / HD, EPS, ALU.mult, ALU.add).then_inc(s["mms"], 1)
                dve.wait_ge(s["mrs"], 2)
                nc.vector.tensor_tensor(mkn[:].rearrange("p t (h d) -> p t h d", d=HD),
                                        kv[:, :, 0:256].rearrange("p t (h d) -> p t h d", d=HD),
                                        bc(mpw[:].rearrange("p (t h o) -> p t h o", t=T, o=1), [P, T, MH, HD]),
                                        ALU.mult).then_inc(s["kready"], 1)
                hidden(1)
                dve.wait_ge(s["out"], 1)
                o = op[:].rearrange("p (a g d) -> p a g d", a=4, g=NG)
                done(nc.vector.tensor_copy(kc[0:NCR], o[0:NCR, 0]))
                done(nc.vector.tensor_tensor(kn[0:NCR, :, 0, :], kc[0:NCR], kc[0:NCR], ALU.mult))
                done(nc.vector.tensor_reduce(stat[0:NCR], kn[0:NCR, :, 0, :], AX.X, ALU.add))
                nc.vector.tensor_scalar(stat[0:NCR], stat[0:NCR], 1.0 / HD, EPS, ALU.mult, ALU.add).then_inc(s["ms"], 1)
                for half in range(2):
                    r = slice(HD * half, HD * half + NCR)
                    done(nc.vector.tensor_copy(m.vc[r, :, half, :], o[r, 1]))
                dve.wait_ge(s["rs"], 1)
                for dup in range(2):
                    nc.vector.tensor_tensor(kn[0:NCR, :, dup, :], kc[0:NCR],
                                            bc(pw[0:NCR].unsqueeze(2), [NCR, NG, HD]), ALU.mult).then_inc(s["kn"], 1)

            @block.tensor
            def _(pe):
                def first_layer(a):
                    pe.wait_ge(m.w1_in[a], 32)
                    pe.wait_ge(s["blk"], 2 * a + 2)
                    if a:
                        pe.wait_ge(s["act"], 2)
                    for p in range(CB):
                        for g in range(NG):
                            r = slice(HD * g, HD * g + HD)
                            last = nc.tensor.matmul(hp[g][:, 0:NCR], m.w1[r, a, p * P:(p + 1) * P],
                                                    blk[r, p, 0:NCR], start=p == 0, stop=p == CB - 1)
                    last.then_inc(s["hid"], 1)

                first_layer(0)
                for n in range(4):
                    t, h = divmod(n, 2)
                    pe.wait_ge(s["normed"], t + 1)
                    if n >= 2:
                        pe.wait_ge(s["evac"], n - 1)
                    for k in range(4):
                        last = nc.tensor.transpose(tp[n % 2][:, k * P:(k + 1) * P],
                                                   mem[:, t, (4 * h + k) * P:(4 * h + k + 1) * P], m.c("ident"))
                    last.then_inc(s["turned"], 1)
                pe.wait_ge(s["wkv_in"], 16)
                pe.wait_ge(s["evac"], 4)
                for t in range(T):
                    for k in range(KT):
                        last = nc.tensor.matmul(pj[t][:], hT[:, k, t * P:(t + 1) * P], wkv[:, k, :],
                                                start=k == 0, stop=k == KT - 1)
                    last.then_inc(s["projected"], 1)
                first_layer(1)
                pe.wait_ge(s["kready"], 1)
                for t in range(T):
                    for k in range(2):
                        last = nc.tensor.transpose(tp[t][:, k * P:(k + 1) * P], mkn[:, t, k * P:(k + 1) * P],
                                                   m.c("ident"))
                    last.then_inc(s["turned"], 1)
                pe.wait_ge(s["act"], 4)
                for a, half in ((0, 0), (1, 0), (1, 1)):
                    for g in range(NG):
                        last = nc.tensor.matmul(op[HD * half:HD * half + NCR, (a * NG + g) * HD:(a * NG + g + 1) * HD],
                                                hid[:, a, g * NCR:(g + 1) * NCR], w2[:, a, :], start=True, stop=True)
                last.then_inc(s["out"], 1)
                pe.wait_ge(s["kn"], 2)
                for g in range(NG):
                    last = nc.tensor.transpose(ctp[:, g * NCR:(g + 1) * NCR],
                                               kn[0:NCR, g].rearrange("p a d -> p (a d)"), m.c("ident")[0:NCR, 0:NCR])
                last.then_inc(s["cturned"], 1)


def load_expert(eng, m, io, e, slot):
    eng.dma_start(m.gateup[slot][:, :, 0:FF], io["w_gate"][e].rearrange("(p k) f -> p k f", p=P)).then_inc(m.w_sem[slot], 16)
    eng.dma_start(m.gateup[slot][:, :, FF:2 * FF], io["w_up"][e].rearrange("(p k) f -> p k f", p=P)).then_inc(m.w_sem[slot], 16)
    eng.dma_start(m.down[slot], io["w_down"][e].rearrange("(k p) d -> p k d", p=P)).then_inc(m.w_sem[slot], 16)


def phase_select(nc, m, io):
    with ExitStack() as st:
        sem = phase_semaphores(nc, m)
        sb = lambda n, s, d=F32: st.enter_context(nc.sbuf_tensor(n, s, d))
        ps = lambda n: st.enter_context(nc.psum_tensor(n, [P, 512], F32))
        qT = sb("sq", [P, NT, 512])
        sc = [sb(f"ssc{b}", [P, 512]) for b in range(2)]
        pT = [sb(f"spT{b}", [P, 4, P]) for b in range(2)]
        mx, den = sb("smx", [P, 8]), sb("sden", [P, 8])
        imp = sb("simp", [P, NG, NSEL])
        top = sb("stop", [P, NG, 8])
        notsel = sb("snot", [P, NG, NSEL])
        sp_ = [ps("ssp0"), ps("ssp1")]
        tp = [ps("stp0"), ps("stp1")]
        oc = [ps("soc0"), ps("soc1")]
        im, nt = ps("simp_"), ps("snt")
        s = {n: sem("s_" + n) for n in (
            "q_in scored shifted expd probs turned evac outed taken imped impt notsel nturned nevac chain cleared").split()}
        qs = [sem(f"s_q{i}") for i in range(NT)]
        first_sel = (8 * 64) // P
        m.first_sel = first_sel
        with nc.Block() as block:

            @block.sync
            def _(sp):
                for i in range(NT):
                    sp.dma_start(qT[:, i, :], m.q_d[i]).then_inc(qs[i], 16)
                sp.dma_start(m.w_out, io["w_out"].rearrange("(k p) n -> p k n", p=P)).then_inc(m.w_out_in, 16)
                sp.dma_start(m.wq, io["mem_wq"].rearrange("(k p) n -> p k n", p=P)).then_inc(m.w_out_in, 16)
                sp.dma_start(m.wo, io["mem_wo"].rearrange("(k p) n -> p k n", p=P)).then_inc(m.w_out_in, 16)

            @block.tensor
            def _(pe):
                def scores(i):
                    pe.wait_ge(qs[i], 16)
                    if i >= 2:
                        pe.wait_ge(s["shifted"], i - 1)
                    for a in range(4):
                        last = nc.tensor.matmul(sp_[i % 2][:, a * P:(a + 1) * P], qT[:, i, a * P:(a + 1) * P],
                                                m.kcT[:, a // 2].rearrange("p a c -> p (a c)"), start=True, stop=True)
                    last.then_inc(s["scored"], 1)

                def outputs(i):
                    pe.wait_ge(s["probs"], i + 1)
                    if i >= 2:
                        pe.wait_ge(s["evac"], i - 1)
                    for k in range(4):
                        last = nc.tensor.transpose(tp[i % 2][:, k * P:(k + 1) * P], sc[i % 2][:, k * P:(k + 1) * P],
                                                   m.c("ident"))
                    last.then_inc(s["turned"], 1)
                    pe.wait_ge(s["evac"], i + 1)
                    if i >= 2:
                        pe.wait_ge(s["taken"], i - 1)
                    for a in range(4):
                        last = nc.tensor.matmul(oc[i % 2][:, a * P:(a + 1) * P], pT[i % 2][:, a, :],
                                                m.vc[:, a // 2].rearrange("p a d -> p (a d)"), start=True, stop=True)
                    last.then_inc(s["outed"], 1)
                    if i >= first_sel:
                        n = i - first_sel
                        if n:
                            pe.wait_ge(s["impt"], n)
                        for a in range(4):
                            last = nc.tensor.matmul(im[:, a // 2 * NSEL:(a // 2 + 1) * NSEL], pT[i % 2][:, a, :],
                                                    m.c("selm"), start=a % 2 == 0, stop=a % 2 == 1)
                        last.then_inc(s["imped"], 1)

                def unchosen(n):
                    pe.wait_ge(s["notsel"], n + 1)
                    if n:
                        pe.wait_ge(s["nevac"], n)
                    for g in range(NG):
                        last = nc.tensor.transpose(nt[0:NSEL, g * P:(g + 1) * P], notsel[:, g, :], m.c("ident"))
                    last.then_inc(s["nturned"], 1)

                scores(0)
                scores(1)
                for i in range(NT + 1):
                    if i + 2 < NT:
                        scores(i + 2)
                    if i < NT:
                        outputs(i)
                    if i > first_sel:
                        unchosen(i - 1 - first_sel)

            @block.scalar
            def _(act):
                def exponentials(i):
                    act.wait_ge(s["shifted"], i + 1)
                    nc.scalar.activation(sc[i % 2][:], sc[i % 2][:], ACT.Exp).then_inc(s["expd"], 1)

                def unchosen(n):
                    act.wait_ge(s["nturned"], n + 1)
                    nc.scalar.activation(m.notselT[0:NSEL, n], nt[0:NSEL, 0:NG * P].rearrange("p (g q) -> p g q", g=NG),
                                         ACT.Copy).then_inc(s["nevac"], 1)

                act.wait_ge(s["cleared"], 1)
                exponentials(0)
                for i in range(NT):
                    if i + 1 < NT:
                        exponentials(i + 1)
                    act.wait_ge(s["turned"], i + 1)
                    if i >= 2:
                        act.wait_ge(s["outed"], i - 1)
                    nc.scalar.activation(pT[i % 2][:], tp[i % 2][:].rearrange("p (k q) -> p k q", k=4),
                                         ACT.Copy).then_inc(s["evac"], 1)
                    act.wait_ge(s["outed"], i + 1)
                    nc.scalar.activation(m.ocmp[:, i, :], oc[i % 2][:], ACT.Copy).then_inc(s["taken"], 1)
                    if i > first_sel:
                        unchosen(i - 1 - first_sel)
                unchosen(NT - 1 - first_sel)

            @block.vector
            def _(dve):
                done = Chain(dve, s["chain"])

                def shift(i):
                    dve.wait_ge(s["scored"], i + 1)
                    if i >= 2:
                        dve.wait_ge(s["turned"], i - 1)
                    b = heads(sc[i % 2][:])
                    done(nc.vector.tensor_tensor(b, heads(sp_[i % 2][:]),
                                                 bc(m.c("cbias")[:, i * NC:(i + 1) * NC].unsqueeze(1), [P, NH, NC]),
                                                 ALU.add))
                    done(nc.vector.tensor_reduce(mx[:], b, AX.X, ALU.max))
                    nc.vector.tensor_tensor(b, b, bc(mx[:].unsqueeze(2), [P, NH, NC]),
                                            ALU.subtract).then_inc(s["shifted"], 1)

                def finish(i):
                    dve.wait_ge(s["expd"], i + 1)
                    b = heads(sc[i % 2][:])
                    done(nc.vector.tensor_tensor(b, b, bc(m.c("cmask")[:, i * NC:(i + 1) * NC].unsqueeze(1),
                                                          [P, NH, NC]), ALU.mult))
                    done(nc.vector.tensor_reduce(den[:], b, AX.X, ALU.add))
                    done(nc.vector.tensor_scalar(den[:], den[:], 1e-30, None, ALU.max))
                    done(nc.vector.reciprocal(den[:], den[:]))
                    nc.vector.tensor_tensor(b, b, bc(den[:].unsqueeze(2), [P, NH, NC]), ALU.mult).then_inc(s["probs"], 1)

                def choose(i):
                    n = i - first_sel
                    dve.wait_ge(s["imped"], n + 1)
                    if n:
                        dve.wait_ge(s["nturned"], n)
                    a = m.c("impa")[:, i * NSEL:(i + 1) * NSEL].unsqueeze(1)
                    b = m.c("impb")[:, i * NSEL:(i + 1) * NSEL].unsqueeze(1)
                    nc.vector.tensor_tensor(imp[:], im[:, 0:NG * NSEL].rearrange("p (g j) -> p g j", g=NG),
                                            bc(a, [P, NG, NSEL]), ALU.mult).then_inc(s["impt"], 1)
                    dve.wait_ge(s["impt"], n + 1)
                    done(nc.vector.tensor_tensor(imp[:], imp[:], bc(b, [P, NG, NSEL]), ALU.add))
                    for g in range(NG):
                        done(nc.vector.max(top[:, g, :], imp[:, g, :]))
                    for g in range(NG):
                        done(nc.vector.match_replace(notsel[:, g, :], top[:, g, :], imp[:, g, :], TAKEN))
                    nc.vector.tensor_scalar(notsel[:], notsel[:], TAKEN, None, ALU.not_equal).then_inc(s["notsel"], 1)

                nc.vector.memset(m.notselT[:], 0.0).then_inc(s["cleared"], 1)
                shift(0)
                for i in range(NT):
                    if i + 1 < NT:
                        shift(i + 1)
                    finish(i)
                    if i > first_sel:
                        choose(i - 1)
                choose(NT - 1)


def attention_units():
    for i in range(NT):
        for h in range(NH):
            yield i, h, 0, 0, i + 1
            yield i, h, 1, max(0, i - 4), min(i + 1, 5)


def phase_attend(nc, m, io):
    units = list(attention_units())
    with ExitStack() as st:
        sem = phase_semaphores(nc, m)
        sb = lambda n, s, d=F32: st.enter_context(nc.sbuf_tensor(n, s, d))
        qT = [sb(f"aq{b}", [P, 4, 2, P]) for b in range(2)]
        probs = [sb(f"ap{b}", [P, S]) for b in range(2)]
        pT = [sb(f"apT{b}", [P, NT, P]) for b in range(2)]
        nmax = sb("anm", [P, 4])
        den = [sb(f"aden{b}", [P, 2 * NH]) for b in range(2)]
        w = [sb(f"aw{b}", [P, 3 * NH]) for b in range(2)]
        t1, t2, out = [m.tail[:, k * 512:(k + 1) * 512] for k in range(3)]
        stat, pw = sb("astat", [P, 8]), sb("apw", [P, 8])
        sc = [st.enter_context(nc.psum_tensor(f"asc{b}", [P, S], F32)) for b in range(2)]
        tp = [st.enter_context(nc.psum_tensor(f"atp{b}", [P, 512], F32)) for b in range(2)]
        ov = [st.enter_context(nc.psum_tensor(f"aov{b}", [P, 512], F32)) for b in range(2)]
        s = {n: sem("a_" + n) for n in (
            "scored nmax expd turned evac0 evac1 valued read ms rs out oout chain cleared spare").split()}
        q_in = [sem("a_q0"), sem("a_q1")]
        pieces = [[(k, min(4, n - k)) for k in range(0, n, 4)] for _, _, _, _, n in units]
        first_piece = [0]
        for p in pieces:
            first_piece.append(first_piece[-1] + len(p))
        ocv = m.oc_d.rearrange("(t p) d -> t p d", p=P)
        U = len(units)
        PER = 2 * NH

        with nc.Block() as block:

            @block.sync
            def _(sp):
                sp.wait_ge(m.w_out_in, 48)
                spare = m.y_d.rearrange("(b k p) d -> b p k d", p=P, k=KT)
                for b in range(NE // KT, MAXI // KT):
                    sp.dma_start(spare[b], m.w_out).then_inc(s["spare"], 16)
                sp.wait_ge(s["cleared"], 2)
                for i in range(NT):
                    if i >= 2:
                        sp.wait_ge(s["scored"], PER * (i - 1))
                    for half in range(2):
                        r = slice(HD * half, HD * half + HD)
                        sp.dma_start(qT[i % 2][r, :, half, :],
                                     m.q_d[i, r, :].rearrange("p (a q) -> p a q", a=4)).then_inc(q_in[i % 2], 16)
                    if i:
                        sp.wait_ge(s["out"], i)
                        sp.dma_start(ocv[i - 1, :, 0:512], out[:]).then_inc(s["oout"], 16)
                sp.wait_ge(s["out"], NT)
                sp.dma_start(ocv[NT - 1, :, 0:512], out[:]).then_inc(s["oout"], 16)
                sp.wait_ge(s["oout"], 16 * NT)
                sp.wait_ge(s["spare"], 32)

            @block.tensor
            def _(pe):
                def scores(u):
                    i, h, branch, k0, n = units[u]
                    if u % PER == 0:
                        pe.wait_ge(q_in[i % 2], 32 * (i // 2 + 1))
                    if u >= 2:
                        pe.wait_ge(s["expd"], u - 1)
                    g = h // HPG
                    kT = m.kwT if branch else m.ksT
                    q = qT[i % 2][:, h // 2, h % 2, :]
                    dst = sc[u % 2]
                    for c in range(0, n, 4):
                        m_ = min(4, n - c)
                        marks = []
                        if not branch and i >= m.first_sel:
                            marks.append((c, m_, m.notselT[:, i - m.first_sel, g, :],
                                          m.eselb[:, c * P:(c + m_) * P]))
                        if branch and i >= 4 and c == 0:
                            marks.append((0, 1, m.identb[:], m.windowb[:]))
                        if c <= n - 1 < c + m_:
                            marks.append((n - 1, 1, m.identb[:], m.causalb[:]))
                        last = nc.tensor.matmul(dst[:, c * P:(c + m_) * P], q,
                                                kT[:, g, (k0 + c) * P:(k0 + c + m_) * P],
                                                start=True, stop=not marks)
                        for j, (at, w_, a, b) in enumerate(marks):
                            last = nc.tensor.matmul(dst[:, at * P:(at + w_) * P], a, b, start=False,
                                                    stop=j == len(marks) - 1)
                    last.then_inc(s["scored"], 1)

                def turn(u):
                    pe.wait_ge(s["expd"], u + 1)
                    for j, (k, n) in enumerate(pieces[u]):
                        f = first_piece[u] + j
                        if f >= 2:
                            pe.wait_ge((s["evac0"], s["evac1"])[f % 2], f // 2)
                        for b in range(n):
                            last = nc.tensor.transpose(tp[f % 2][:, b * P:(b + 1) * P],
                                                       probs[u % 2][:, (k + b) * P:(k + b + 1) * P], m.c("ident"))
                        last.then_inc(s["turned"], 1)

                def values(u):
                    i, h, branch, k0, n = units[u]
                    v = m.vw if branch else m.vs
                    g = h // HPG
                    f = first_piece[u + 1]
                    pe.wait_ge(s["evac0"], (f + 1) // 2)
                    pe.wait_ge(s["evac1"], f // 2)
                    if h == 0 and i:
                        pe.wait_ge(s["read"], 2 * i)
                    for b in range(n):
                        at = (k0 + b) * P + g * HD
                        last = nc.tensor.matmul(ov[branch][:, h * HD:(h + 1) * HD], pT[u % 2][:, b, :],
                                                v[:, at:at + HD], start=b == 0, stop=b == n - 1)
                    last.then_inc(s["valued"], 1)

                for u in range(U + 3):
                    if u < U:
                        scores(u)
                    if 2 <= u < U + 2:
                        turn(u - 2)
                    if u >= 3:
                        values(u - 3)

            def evacuate(eng, copy, u, parity, sem_):
                for j, (k, n) in enumerate(pieces[u]):
                    f = first_piece[u] + j
                    if f % 2 == parity:
                        eng.wait_ge(s["turned"], f + 1)
                        if u >= 2:
                            eng.wait_ge(s["valued"], u - 1)
                        copy(pT[u % 2][:, k:k + n, :],
                             tp[f % 2][:, 0:n * P].rearrange("p (k q) -> p k q", k=n)).then_inc(sem_, 1)

            @block.scalar
            def _(act):
                def softmax(u):
                    i, h, branch, k0, n = units[u]
                    act.wait_ge(s["nmax"], u + 1)
                    if u >= 2:
                        act.wait_ge(s["turned"], first_piece[u - 1])
                    if h == 0 and i >= 2:
                        act.wait_ge(s["rs"], i - 1)
                    nc.scalar.activation(probs[u % 2][:, 0:n * P], sc[u % 2][:, 0:n * P], ACT.Exp,
                                         bias=nmax[:, u % 4:u % 4 + 1],
                                         accum_out=den[i % 2][:, branch * NH + h:branch * NH + h + 1]).then_inc(s["expd"], 1)

                for u in range(U + 2):
                    if u < U:
                        softmax(u)
                    if u >= 2:
                        evacuate(act, lambda o, a: nc.scalar.activation(o, a, ACT.Copy), u - 2, 0, s["evac0"])

            @block.gpsimd
            def _(pool):
                for i in range(NT):
                    pool.wait_ge(s["ms"], i + 1)
                    nc.gpsimd.tensor_tensor(pw[:], stat[:], m.mhalf[:, 0:8], ALU.pow).then_inc(s["rs"], 1)

            @block.vector
            def _(dve):
                done = Chain(dve, s["chain"])

                def maximum(u):
                    n = units[u][4]
                    dve.wait_ge(s["scored"], u + 1)
                    nc.vector.tensor_reduce(nmax[:, u % 4:u % 4 + 1], sc[u % 2][:, 0:n * P], AX.X, ALU.max,
                                            negate=True).then_inc(s["nmax"], 1)

                def gates(i):
                    b = i % 2
                    g3 = m.gate[:, i * 24:(i + 1) * 24].rearrange("p (h c) -> p c h", c=3)
                    dve.wait_ge(s["valued"], PER * (i + 1))
                    done(nc.vector.reciprocal(w[b][:, 0:16], den[b][:]))
                    done(nc.vector.tensor_tensor(w[b][:, 0:16].rearrange("p (c h) -> p c h", c=2),
                                                 w[b][:, 0:16].rearrange("p (c h) -> p c h", c=2), g3[:, 1:3, :],
                                                 ALU.mult))
                    nc.vector.tensor_tensor(heads(t1[:]), heads(ov[0][:]), bc(w[b][:, 0:8].unsqueeze(2), [P, NH, HD]),
                                            ALU.mult).then_inc(s["read"], 1)
                    nc.vector.tensor_tensor(heads(t2[:]), heads(ov[1][:]), bc(w[b][:, 8:16].unsqueeze(2), [P, NH, HD]),
                                            ALU.mult).then_inc(s["read"], 1)

                STEPS = 6

                def finish(i, step):
                    b = i % 2
                    g3 = m.gate[:, i * 24:(i + 1) * 24].rearrange("p (h c) -> p c h", c=3)
                    if step == 1:
                        dve.wait_ge(s["read"], 2 * i + 2)
                        done(nc.vector.tensor_tensor(t1[:], t1[:], t2[:], ALU.add))
                        done(nc.vector.tensor_copy(w[b][:, 16:24], g3[:, 0, :]))
                    elif step == 2:
                        done(nc.vector.tensor_tensor(heads(t2[:]), heads(m.ocmp[:, i, :]),
                                                     bc(w[b][:, 16:24].unsqueeze(2), [P, NH, HD]), ALU.mult))
                        done(nc.vector.tensor_tensor(t1[:], t1[:], t2[:], ALU.add))
                    elif step == 3:
                        done(nc.vector.tensor_tensor(t2[:], t1[:], t1[:], ALU.mult))
                    elif step == 4:
                        done(nc.vector.tensor_reduce(stat[:], heads(t2[:]), AX.X, ALU.add))
                        nc.vector.tensor_scalar(stat[:], stat[:], 1.0 / HD, EPS, ALU.mult,
                                                ALU.add).then_inc(s["ms"], 1)
                    elif step == 5:
                        dve.wait_ge(s["rs"], i + 1)
                        done(nc.vector.tensor_tensor(heads(t1[:]), heads(t1[:]), bc(pw[:].unsqueeze(2), [P, NH, HD]),
                                                     ALU.mult))
                    else:
                        if i:
                            dve.wait_ge(s["oout"], 16 * i)
                        nc.vector.tensor_tensor(out[:], t1[:], m.gout[:], ALU.mult).then_inc(s["out"], 1)
                        dve.wait_ge(s["out"], i + 1)

                for b in range(2):
                    nc.vector.memset(qT[b][:], 0.0).then_inc(s["cleared"], 1)
                for u in range(U + 3 + STEPS):
                    if u < U:
                        maximum(u)
                    if 2 <= u < U + 2:
                        evacuate(dve, lambda o, a: nc.vector.tensor_copy(o, a), u - 2, 1, s["evac1"])
                    i, since = divmod(u - 2, PER)
                    if i >= 1 and since == 0:
                        gates(i - 1)
                    elif i >= 1 and since <= STEPS:
                        finish(i - 1, since)


AGE = dict(A=0, B=1, C=2, D=3, E=4, F=5)
ORDER = "EFDCBA"
TURNS = dict(A=2, B=2, C=1, D=2, E=1, F=2)


def phase_mix(nc, m, io):
    steps = [[(X, st - AGE[X]) for X in ORDER if 0 <= st - AGE[X] < NT] for st in range(NT + 5)]
    use, f = {}, 0
    for step in steps:
        for X, t in step:
            use[X, t] = f
            f += TURNS[X]
    with ExitStack() as st:
        sem = phase_semaphores(nc, m)
        sb = lambda n, s, d=F32: st.enter_context(nc.sbuf_tensor(n, s, d))
        ps = lambda n, w=512: st.enter_context(nc.psum_tensor(n, [P, w], F32))
        o = [sb(f"xo{b}", [P, D]) for b in range(2)]
        gx, gf = sb("xgx", [P, D]), sb("xgf", [P, D])
        wr = sb("xwr", [P, KT, 36])
        br = sb("xbr", [P, 36])
        h1, h3, junk = sb("xh1", [P, D]), sb("xh3", [P, D]), sb("xjunk", [P, D], BF16)
        pr = sb("xpr", [P, MH, NMEM])
        qraw, qn, q2, om = [sb("x" + n, [P, 256]) for n in "qraw qn q2 om".split()]
        turned_to = {X: sb("xT" + X, [P, n, P]) for X, n in dict(A=8, B=8, C=2, D=8, E=2, F=8).items()}
        nm, den, rden, stq, pwq = [sb("x" + n, [P, 4]) for n in "nm den rden stq pwq".split()]
        ssA, msA, rsA, ssE, msE, rsE = [sb("x" + n, [P, 1]) for n in "ssA msA rsA ssE msE rsE".split()]
        sc = ps("xsc", 1024)
        tp = [ps("xtp0"), ps("xtp1")]
        pj = [ps("xpj0"), ps("xpj1")]
        qb, ov = ps("xqb"), ps("xov")
        s = {n: sem("x_" + n) for n in (
            "w_in turned evac mmA mmB mmC mmD mmE mmF x1 x2 sqA sqE msA msE msB rsA rsE rsB h1 h3 h3out qraw qn nmax "
            "expd om lg chain late_in").split()}
        o_in = [sem("x_o0"), sem("x_o1")]
        ocv = m.oc_d.rearrange("(t p) d -> t p d", p=P)
        xv = io["x"].rearrange("(t p) d -> t p d", p=P)
        hv = m.h_d.rearrange("(t p) d -> t p d", p=P)

        with nc.Block() as block:

            @block.sync
            def _(sp):
                def load(t):
                    if t >= 2:
                        sp.wait_ge(s["turned"], use["A", t - 2] + 2)
                    sp.dma_start(o[t % 2][:], ocv[t]).then_inc(o_in[t % 2], 16)
                    sp.dma_start(m.x1[:, t, :], xv[t]).then_inc(o_in[t % 2], 16)

                load(0)
                sp.dma_start(gx[:], io["g_memx"]).then_inc(s["w_in"], 16)
                sp.dma_start(gf[:], io["g_ffn"]).then_inc(s["w_in"], 16)
                sp.dma_start(wr[:], io["w_router"].rearrange("(p k) e -> p k e", p=P)).then_inc(s["w_in"], 16)
                sp.dma_start(br[:], io["b_router"]).then_inc(s["w_in"], 16)
                sp.dma_start(m.late[:], io["late"]).then_inc(s["late_in"], 16)
                for step in range(1, len(steps)):
                    if step < NT:
                        load(step)
                    t = step - AGE["E"]
                    if 0 <= t < NT:
                        sp.wait_ge(s["h3"], t + 1)
                        sp.dma_start(hv[t], h3[:]).then_inc(s["h3out"], 16)
                sp.wait_ge(s["h3out"], 16 * NT)
                sp.wait_ge(s["late_in"], 16)

            @block.tensor
            def _(pe):
                def turn(X, t):
                    f = use[X, t]
                    src = dict(A=lambda k: o[t % 2][:, k * P:(k + 1) * P], B=lambda k: h1[:, k * P:(k + 1) * P],
                               C=lambda k: qn[:, k * P:(k + 1) * P],
                               D=lambda k: pr[:].rearrange("p h c -> p (h c)")[:, k * P:(k + 1) * P],
                               E=lambda k: om[:, k * P:(k + 1) * P], F=lambda k: h3[:, k * P:(k + 1) * P])[X]
                    if X == "A":
                        pe.wait_ge(o_in[t % 2], 32 * (t // 2 + 1))
                    else:
                        ready, n = dict(B=(s["h1"], 1), C=(s["qn"], 1), D=(s["expd"], MH), E=(s["om"], 1), F=(s["h3"], 1))[X]
                        pe.wait_ge(ready, n * (t + 1))
                    for j in range(TURNS[X]):
                        if f + j >= 2:
                            pe.wait_ge(s["evac"], f + j - 1)
                        for k in range(4 if TURNS[X] == 2 else 2):
                            last = nc.tensor.transpose(tp[(f + j) % 2][:, k * P:(k + 1) * P], src(4 * j + k),
                                                       m.c("ident"))
                        last.then_inc(s["turned"], 1)

                def dense(X, t, out, w, n, kt):
                    for k in range(kt):
                        last = nc.tensor.matmul(out, turned_to[X][:, k, :], w(k), start=k == 0, stop=k == kt - 1)
                    last.then_inc(finished[X], 1)

                finished = dict(A=s["mmA"], B=s["mmB"], C=s["mmC"], D=s["mmD"], E=s["mmE"], F=s["mmF"])

                def product(X, t):
                    pe.wait_ge(s["evac"], use[X, t] + TURNS[X])
                    if X in "AE":
                        first, second = (t, max(0, t - AGE["E"] + 1)) if X == "A" else (min(NT, t + AGE["E"]), t)
                        if first:
                            pe.wait_ge(s["x1"], 2 * first)
                        if second:
                            pe.wait_ge(s["x2"], 2 * second)
                        w, kt = (m.w_out, KT) if X == "A" else (m.wo, 2)
                        for half in range(2):
                            dense(X, t, pj[half][:], lambda k: w[:, k, 512 * half:512 * half + 512], 512, kt)
                    elif X == "B":
                        f_before = max(0, t + AGE["B"] - AGE["F"] + 1)
                        if t:
                            pe.wait_ge(s["qraw"], t)
                        if f_before:
                            pe.wait_ge(s["lg"], min(NT, f_before))
                        dense(X, t, qb[:, 0:256], lambda k: m.wq[:, k, :], 256, KT)
                    elif X == "F":
                        pe.wait_ge(s["w_in"], 64)
                        b_before = min(NT, t + AGE["F"] - AGE["B"])
                        pe.wait_ge(s["qraw"], b_before)
                        if t:
                            pe.wait_ge(s["lg"], t)
                        dense(X, t, qb[:, 0:36], lambda k: wr[:, k, :], 36, KT)
                    elif X == "C":
                        if t:
                            pe.wait_ge(s["expd"], MH * t)
                        for a in range(2):
                            last = nc.tensor.matmul(sc[:, a * 512:(a + 1) * 512], turned_to[X][:, a, :],
                                                    m.kmT[:, a].rearrange("p a c -> p (a c)"), start=True, stop=True)
                        last.then_inc(s["mmC"], 1)
                    elif X == "D":
                        if t:
                            pe.wait_ge(s["om"], t)
                        for h in range(MH):
                            for k in range(2):
                                last = nc.tensor.matmul(ov[:, h * HD:(h + 1) * HD], turned_to[X][:, 2 * h + k, :],
                                                        m.vm[:, k, h * HD:(h + 1) * HD], start=k == 0, stop=k == 1)
                        last.then_inc(s["mmD"], 1)

                pe.wait_ge(m.w_out_in, 48)
                for step in steps:
                    for X, t in step:
                        turn(X, t)
                    for X, t in step:
                        product(X, t)

            @block.scalar
            def _(act):
                counts = dict(A=(s["mmA"], 2), B=(s["mmB"], 1), C=(s["mmC"], 1), D=(s["mmD"], 1), E=(s["mmE"], 2), F=(s["mmF"], 1))

                def evac(X, t):
                    f = use[X, t]
                    if t:
                        sm, n = counts[X]
                        act.wait_ge(sm, n * t)
                    for j in range(TURNS[X]):
                        act.wait_ge(s["turned"], f + j + 1)
                        k = 4 if TURNS[X] == 2 else 2
                        nc.scalar.activation(turned_to[X][:, 4 * j:4 * j + k, :],
                                             tp[(f + j) % 2][:, 0:k * P].rearrange("p (k q) -> p k q", k=k), ACT.Copy,
                                             scale=m.mqgain[:] if X == "C" else 1.0).then_inc(s["evac"], 1)

                def work(X, t):
                    if X == "A":
                        act.wait_ge(s["x1"], 2 * t + 2)
                        nc.scalar.activation(junk[:], m.x1[:, t, :], ACT.Square, accum_out=ssA[:]).then_inc(s["sqA"], 1)
                    elif X == "E":
                        act.wait_ge(s["x2"], 2 * t + 2)
                        nc.scalar.activation(junk[:], m.x1[:, t, :], ACT.Square, accum_out=ssE[:]).then_inc(s["sqE"], 1)
                    elif X == "B":
                        act.wait_ge(s["mmB"], t + 1)
                        nc.scalar.activation(qraw[:], qb[:, 0:256], ACT.Copy).then_inc(s["qraw"], 1)
                    elif X == "C":
                        act.wait_ge(s["nmax"], t + 1)
                        for h in range(MH):
                            nc.scalar.activation(pr[:, h, :], sc[:, h * NMEM:(h + 1) * NMEM], ACT.Exp,
                                                 bias=nm[:, h:h + 1], accum_out=den[:, h:h + 1]).then_inc(s["expd"], 1)

                for step in steps:
                    for X, t in step:
                        evac(X, t)
                    for X, t in step:
                        work(X, t)

            @block.gpsimd
            def _(pool):
                for step in steps:
                    for X, t in step:
                        if X in "ABE":
                            ms, rs, a, b, n = dict(A=(s["msA"], s["rsA"], msA, rsA, 1), B=(s["msB"], s["rsB"], stq, pwq, 4),
                                                   E=(s["msE"], s["rsE"], msE, rsE, 1))[X]
                            pool.wait_ge(ms, t + 1)
                            nc.gpsimd.tensor_tensor(b[:], a[:], m.mhalf[:, 0:n], ALU.pow).then_inc(rs, 1)

            @block.vector
            def _(dve):
                done = Chain(dve, s["chain"])

                def residual(t, mm, mark):
                    for half in range(2):
                        c = slice(512 * half, 512 * half + 512)
                        dve.wait_ge(mm, 2 * t + half + 1)
                        nc.vector.tensor_tensor(m.x1[:, t, c], m.x1[:, t, c], pj[half][:], ALU.add).then_inc(mark, 1)
                        dve.wait_ge(mark, 2 * t + half + 1)

                def work(X, t):
                    if X == "A":
                        dve.wait_ge(o_in[t % 2], 32 * (t // 2 + 1))
                        residual(t, s["mmA"], s["x1"])
                        dve.wait_ge(s["sqA"], t + 1)
                        nc.vector.tensor_scalar(msA[:], ssA[:], 1.0 / D, EPS, ALU.mult, ALU.add).then_inc(s["msA"], 1)
                        dve.wait_ge(s["w_in"], 64)
                        dve.wait_ge(s["rsA"], t + 1)
                        if t:
                            dve.wait_ge(s["turned"], use["B", t - 1] + 2)
                        nc.vector.scalar_tensor_tensor(h1[:], m.x1[:, t, :], rsA[:], gx[:], ALU.mult,
                                                       ALU.mult).then_inc(s["h1"], 1)
                    elif X == "B":
                        dve.wait_ge(s["qraw"], t + 1)
                        done(nc.vector.tensor_tensor(q2[:], qraw[:], qraw[:], ALU.mult))
                        done(nc.vector.tensor_reduce(stq[:], heads(q2[:], MH), AX.X, ALU.add))
                        nc.vector.tensor_scalar(stq[:], stq[:], 1.0 / HD, EPS, ALU.mult, ALU.add).then_inc(s["msB"], 1)
                        dve.wait_ge(s["rsB"], t + 1)
                        if t:
                            dve.wait_ge(s["turned"], use["C", t - 1] + 1)
                        nc.vector.tensor_tensor(heads(qn[:], MH), heads(qraw[:], MH),
                                                bc(pwq[:].unsqueeze(2), [P, MH, HD]), ALU.mult).then_inc(s["qn"], 1)
                    elif X == "C":
                        dve.wait_ge(s["mmC"], t + 1)
                        if t:
                            dve.wait_ge(s["expd"], MH * t)
                        nc.vector.tensor_reduce(nm[:], heads(sc[:], MH), AX.X, ALU.max, negate=True).then_inc(s["nmax"], 1)
                    elif X == "D":
                        dve.wait_ge(s["mmD"], t + 1)
                        if t:
                            dve.wait_ge(s["turned"], use["E", t - 1] + 1)
                        nc.vector.tensor_tensor(heads(om[:], MH), heads(ov[:, 0:256], MH),
                                                bc(rden[:].unsqueeze(2), [P, MH, HD]), ALU.mult).then_inc(s["om"], 1)
                    elif X == "E":
                        residual(t, s["mmE"], s["x2"])
                        dve.wait_ge(s["sqE"], t + 1)
                        nc.vector.tensor_scalar(msE[:], ssE[:], 1.0 / D, EPS, ALU.mult, ALU.add).then_inc(s["msE"], 1)
                        dve.wait_ge(s["w_in"], 64)
                        dve.wait_ge(s["rsE"], t + 1)
                        if t:
                            dve.wait_ge(s["turned"], use["F", t - 1] + 2)
                            dve.wait_ge(s["h3out"], 16 * t)
                        v = lambda a: a.rearrange("p (q k) -> p q k", k=KT)
                        nc.vector.scalar_tensor_tensor(h3[:].rearrange("p (k q) -> p q k", k=KT), v(m.x1[:, t, :]),
                                                       rsE[:], v(gf[:]), ALU.mult, ALU.mult).then_inc(s["h3"], 1)
                    elif X == "F":
                        dve.wait_ge(s["mmF"], t + 1)
                        nc.vector.tensor_tensor(m.lg[:, t, :], qb[:, 0:36], br[:], ALU.add).then_inc(s["lg"], 1)

                for step in steps:
                    for X, t in step:
                        if X == "D":
                            dve.wait_ge(s["expd"], MH * (t + 1))
                            done(nc.vector.reciprocal(rden[:], den[:]))
                    for X, t in step:
                        work(X, t)


def phase_route(nc, m, io):
    with ExitStack() as st:
        sem = phase_semaphores(nc, m)
        sb = lambda n, s, d=F32: st.enter_context(nc.sbuf_tensor(n, s, d))
        ps = lambda n, w=512: st.enter_context(nc.psum_tensor(n, [P, w], F32))
        gs, gkey, ghot = [sb("r" + n, [P, NT, 4]) for n in "gs gkey ghot".split()]
        gm, gw, km, v1, v2, rec = [sb("r" + n, [P, NT, 1]) for n in "gm gw km v1 v2 rec".split()]
        big = sb("rbig", [P, NT, 4, EG])
        e8, key, h1, h2 = [sb("r" + n, [P, NT, EG]) for n in "e8 key h1 h2".split()]
        hot = [sb(f"rhot{k}", [P, NT, NE]) for k in range(2)]
        both = sb("rboth", [P, NT, NE])
        runs = sb("rruns", [P, NT + 1, NE])
        posf, prod = sb("rposf", [P, NT, NE]), sb("rprod", [P, NT, NE])
        over, ovend, ovst, ones = [sb("r" + n, [P, NE]) for n in "over ovend ovst one".split()]
        cmp_ = sb("rcmp", [P, NE, 16])
        pos, ov, ex, q, item, row, g = [[sb(f"r{n}{k}", [P, NT]) for k in range(2)]
                                        for n in "pos ov ex q item row g".split()]
        rhot = [sb(f"rrh{b}", [P, P]) for b in range(2)]
        ihot = [sb(f"rih{b}", [P, MAXI]) for b in range(2)]
        small = sb("rsmall", [P, 64])
        pp, tot, rm = ps("rpp"), ps("rtot"), ps("rrm")
        s = {n: sem("r_" + n) for n in "gs ge d ex both counted hots mapped chain fin".split()}

        with nc.Block() as block:

            @block.scalar
            def _(act):
                act.wait_ge(s["gs"], 1)
                nc.scalar.activation(gs[:], gs[:], ACT.Exp).then_inc(s["ge"], 1)
                act.wait_ge(s["d"], 1)
                nc.scalar.activation(v2[:], v2[:], ACT.Exp).then_inc(s["ex"], 1)

            @block.tensor
            def _(pe):
                pe.wait_ge(s["both"], 1)
                flat = both[:].rearrange("p t e -> p (t e)")
                nc.tensor.matmul(pp[:, 0:256], m.c("before"), flat, start=True, stop=True)
                nc.tensor.matmul(tot[:, 0:256], m.c("ones"), flat, start=True, stop=True).then_inc(s["counted"], 1)
                for n in range(2 * NT):
                    pe.wait_ge(s["hots"], 2 * n + 2)
                    nc.tensor.matmul(rm[:, 0:MAXI], rhot[n % 2][:], ihot[n % 2][:], start=n == 0,
                                     stop=n == 2 * NT - 1).then_inc(s["mapped"], 1)

            @block.vector
            def _(dve):
                done = Chain(dve, s["chain"])
                tt, ts, red = nc.vector.tensor_tensor, nc.vector.tensor_scalar, nc.vector.tensor_reduce
                G, E = m.lg[:, :, 0:4], m.lg[:, :, 4:36].rearrange("p t (g e) -> p t g e", g=4)

                def hottest(src, mx, pref, n, k, out):
                    done(red(mx[:], src, AX.X, ALU.max))
                    done(tt(k, src, bc(mx[:], [P, NT, n]), ALU.is_equal))
                    done(tt(k, k, bc(pref.unsqueeze(1), [P, NT, n]), ALU.mult))
                    done(red(km[:], k, AX.X, ALU.max))
                    done(tt(out, k, bc(km[:], [P, NT, n]), ALU.is_equal))

                hottest(G, gm, m.c("pref8")[:, 0:4], 4, gkey[:], ghot[:])
                tt(gs[:], G, bc(gm[:], [P, NT, 4]), ALU.subtract).then_inc(s["gs"], 1)
                done(tt(big[:], E, bc(ghot[:].unsqueeze(3), [P, NT, 4, EG]), ALU.mult))
                done(red(e8[:], big[:].rearrange("p t g e -> p t e g"), AX.X, ALU.add))
                hottest(e8[:], v1, m.c("pref8"), EG, key[:], h1[:])
                done(nc.vector.scalar_tensor_tensor(e8[:], h1[:], TAKEN, e8[:], ALU.mult, ALU.add))
                hottest(e8[:], v2, m.c("pref8"), EG, key[:], h2[:])
                tt(v2[:], v2[:], v1[:], ALU.subtract).then_inc(s["d"], 1)
                for k, h in enumerate((h1, h2)):
                    done(tt(hot[k][:].rearrange("p t (g e) -> p t g e", g=4),
                            bc(ghot[:].unsqueeze(3), [P, NT, 4, EG]), bc(h[:].unsqueeze(2), [P, NT, 4, EG]), ALU.mult))
                tt(both[:], hot[0][:], hot[1][:], ALU.add).then_inc(s["both"], 1)
                dve.wait_ge(s["ge"], 1)
                done(red(gw[:], gs[:], AX.X, ALU.add))
                done(nc.vector.reciprocal(gw[:], gw[:]))
                dve.wait_ge(s["ex"], 1)
                done(ts(rec[:], v2[:], 1.0, None, ALU.add))
                done(nc.vector.reciprocal(rec[:], rec[:]))
                done(tt(m.wts[:, 0, :].unsqueeze(2), gw[:], rec[:], ALU.mult))
                done(tt(m.wts[:, 1, :].unsqueeze(2), m.wts[:, 0, :].unsqueeze(2), v2[:], ALU.mult))
                done(nc.vector.memset(runs[:, 0, :], 0.0))
                done(nc.vector.memset(ones[:], 1.0))
                dve.wait_ge(s["counted"], 1)
                for t in range(NT):
                    done(tt(runs[:, t + 1, :], runs[:, t, :], tot[:, t * NE:(t + 1) * NE], ALU.add))
                done(tt(posf[:].rearrange("p t e -> p (t e)"), runs[:, 0:NT, :].rearrange("p t e -> p (t e)"),
                        pp[:, 0:256], ALU.add))
                thr = m.c("thr")[:, 1:8]
                done(tt(cmp_[:, :, 0:7], bc(runs[:, NT, :].unsqueeze(2), [P, NE, 7]),
                        bc(thr.unsqueeze(1), [P, NE, 7]), ALU.is_gt))
                done(red(over[:], cmp_[:, :, 0:7], AX.X, ALU.add))
                done(nc.vector.tensor_tensor_scan(ovend[:], ones[:], over[:], 0.0, ALU.mult, ALU.add))
                done(tt(ovst[:], ovend[:], over[:], ALU.subtract))
                for k in range(2):
                    for dst, table in ((pos[k], posf[:]), (ov[k], bc(ovst[:].unsqueeze(1), [P, NT, NE])),
                                       (ex[k], bc(m.c("eid").unsqueeze(1), [P, NT, NE]))):
                        done(tt(prod[:], hot[k][:], table, ALU.mult))
                        done(red(dst[:], prod[:], AX.X, ALU.add))
                    done(tt(cmp_[:, 0:NT, 0:7], bc(pos[k][:].unsqueeze(2), [P, NT, 7]),
                            bc(thr.unsqueeze(1), [P, NT, 7]), ALU.is_ge))
                    done(red(q[k][:], cmp_[:, 0:NT, 0:7], AX.X, ALU.add))
                    done(nc.vector.scalar_tensor_tensor(row[k][:], q[k][:], -float(P), pos[k][:], ALU.mult, ALU.add))
                    done(tt(item[k][:], ov[k][:], q[k][:], ALU.add))
                    done(nc.vector.scalar_tensor_tensor(item[k][:], item[k][:], float(NE - 1), ex[k][:], ALU.add,
                                                        ALU.subtract))
                    done(ts(g[k][:], q[k][:], 0.0, None, ALU.is_gt))
                    done(tt(item[k][:], item[k][:], g[k][:], ALU.mult))
                    done(tt(item[k][:], item[k][:], ex[k][:], ALU.add))
                    done(nc.vector.scalar_tensor_tensor(m.slot[:, k, :], item[k][:], float(P), row[k][:], ALU.mult,
                                                        ALU.add))
                for n in range(2 * NT):
                    t, k = divmod(n, 2)
                    if n >= 2:
                        dve.wait_ge(s["mapped"], n - 1)
                    ts(rhot[n % 2][:], m.c("iota"), row[k][:, t:t + 1], None, ALU.is_equal).then_inc(s["hots"], 1)
                    ts(ihot[n % 2][:], m.c("item"), item[k][:, t:t + 1], m.c("tokid")[:, t:t + 1], ALU.is_equal,
                       ALU.mult).then_inc(s["hots"], 1)
                done(nc.vector.tensor_copy(m.experts[:, 0:NE], m.c("eid")))
                done(tt(cmp_[:].rearrange("p a b -> p (a b)").rearrange("p (j e) -> p j e", j=16),
                        bc(ovend[:].unsqueeze(1), [P, 16, NE]),
                        bc(m.c("item")[:, 0:16].unsqueeze(2), [P, 16, NE]), ALU.is_le))
                done(red(small[:, 0:16], cmp_[:].rearrange("p a b -> p (a b)").rearrange("p (j e) -> p j e", j=16),
                         AX.X, ALU.add))
                done(ts(m.experts[:, NE:MAXI], small[:, 0:16], float(NE - 1), None, ALU.min))
                done(tt(small[:, 16:20], bc(ovend[:, NE - 1:NE], [P, 4]), m.c("thr4"), ALU.is_gt))
                done(red(small[:, 20:21], small[:, 16:20], AX.X, ALU.add))
                done(ts(m.rounds[:], small[:, 20:21], float(NE // SLOTS - 1), None, ALU.add))
                done(nc.vector.memset(m.rows[:], 0))
                dve.wait_ge(s["mapped"], 2 * NT)
                done(nc.vector.tensor_copy(m.rows[:, 0:MAXI], rm[:, 0:MAXI]))


def phase_experts(nc, m, io):
    with ExitStack() as st:
        sem = phase_semaphores(nc, m)
        sb = lambda n, s, d=F32: st.enter_context(nc.sbuf_tensor(n, s, d))
        ps = lambda n, w=512: st.enter_context(nc.psum_tensor(n, [P, w], F32))
        idx = [sb(f"eidx{k}", [P, 1], I32) for k in range(SLOTS)]
        mark = sb("emark", [P, 1], I32)
        xg = [sb(f"exg{b}", [P, D]) for b in range(2)]
        xT = [sb(f"exT{b}", [P, KT, P]) for b in range(2)]
        sg = [sb(f"esg{b}", [P, FF]) for b in range(2)]
        h = [sb(f"eh{b}", [P, FF]) for b in range(2)]
        hT = sb("ehT", [P, 2, P])
        y = [sb(f"ey{b}", [P, D]) for b in range(2)]
        tp = [ps("etp0"), ps("etp1")]
        gu = [ps("egu0"), ps("egu1")]
        th = ps("eth")
        yp = [ps("eyp0"), ps("eyp1")]
        s = {n: sem("e_" + n) for n in (
            "idx turned xT0 xT1 gated silu h hturned hT down y0 y1 mark").split()}
        got = [sem("e_g0"), sem("e_g1")]
        kept = [sem("e_k0"), sem("e_k1")]
        yv = m.y_d.rearrange("(n p) d -> n p d", p=P)

        def rounds(eng):
            return eng.value_load(m.rounds[0:1, 0:1], min_val=NE // SLOTS - 1, max_val=MAXI // SLOTS - 1)

        with nc.Block() as block:

            @block.sync
            def _(sp):
                last_round = rounds(sp)
                for k in range(2, SLOTS):
                    load_expert(sp, m, io, k, k)

                def store(b, k):
                    sp.wait_ge(s["y0"], 4 * b + k + 1)
                    sp.wait_ge(s["y1"], 4 * b + k + 1)
                    sp.dma_start(yv[4 * b + k], y[k % 2][:]).then_inc(kept[k % 2], 16)

                with sp.Fori(0, last_round) as b:
                    for k in range(SLOTS):
                        e = sp.value_load(m.experts[0:1, bass.ds(4 * b + 4 + k, 1)], min_val=0, max_val=NE - 1)
                        sp.wait_ge(s["down"], 4 * b + k + 1)
                        load_expert(sp, m, io, e, k)
                        store(b, k)
                for k in range(SLOTS):
                    store(last_round, k)

            @block.gpsimd
            def _(pool):
                last_round = rounds(pool)

                def gather(b, k, first=False):
                    if not first:
                        pool.wait_ge(s["turned"], 2 * (4 * b + k - 1))
                    nc.gpsimd.tensor_copy(idx[k][:], m.rows[:, bass.ds(4 * b + k, 1)]).then_inc(s["idx"], 1)
                    pool.wait_ge(s["idx"], 4 * b + k + 1)
                    nc.gpsimd.tensor_tensor(mark[:], idx[k][:], idx[k][:], ALU.add).then_inc(s["mark"], 1)
                    nc.gpsimd.indirect_dma_start(xg[k % 2][:], None, m.h_d, bass.IndirectOffsetOnAxis(idx[k][:], 0)
                                                 ).then_inc(got[k % 2], 16)

                for k in range(SLOTS):
                    gather(0, k, k < 2)
                with pool.Fori(1, last_round + 1) as b:
                    for k in range(SLOTS):
                        gather(b, k)
                gather(last_round + 1, 0)
                pool.wait_ge(got[0], 32 * last_round + 48)
                for p in range(2):
                    pool.wait_ge(kept[p], 32 * last_round + 32)

            def over_rounds(eng, body):
                last_round = rounds(eng)
                body(0)
                with eng.Fori(1, last_round + 1) as b:
                    body(b)
                return last_round

            @block.tensor
            def _(pe):
                def turn_x(b, k):
                    pe.wait_ge(got[k % 2], 32 * b + 16 * (k // 2) + 16)
                    for j in range(2):
                        for c in range(4):
                            last = nc.tensor.transpose(tp[j][:, c * P:(c + 1) * P],
                                                       xg[k % 2][:, (4 * j + c) * P:(4 * j + c + 1) * P],
                                                       m.c("ident"))
                        last.then_inc(s["turned"], 1)

                def down(b, k):
                    pe.wait_ge(s["hT"], 4 * b + k + 1)
                    pe.wait_ge(s["y0"], 4 * b + k)
                    pe.wait_ge(s["y1"], 4 * b + k)
                    for half in range(2):
                        for c in range(2):
                            last = nc.tensor.matmul(yp[half][:], hT[:, c, :],
                                                    m.down[k][:, c, 512 * half:512 * half + 512],
                                                    start=c == 0, stop=c == 1)
                    last.then_inc(s["down"], 1)

                def body(b):
                    for k in range(SLOTS):
                        n = 4 * b + k
                        pe.wait_ge(s["xT0"], n + 1)
                        pe.wait_ge(s["xT1"], n + 1)
                        pe.wait_ge(m.w_sem[k], 48 * b + 48)
                        for c in range(KT):
                            last = nc.tensor.matmul(gu[k % 2][:], xT[k % 2][:, c, :], m.gateup[k][:, c, :],
                                                    start=c == 0, stop=c == KT - 1)
                        last.then_inc(s["gated"], 1)
                        turn_x(b + 1 if k == 3 else b, (k + 1) % 4)
                        if k:
                            down(b, k - 1)
                        elif not isinstance(b, int):
                            down(b - 1, 3)
                        pe.wait_ge(s["h"], n + 1)
                        for c in range(2):
                            last = nc.tensor.transpose(th[:, c * P:(c + 1) * P], h[k % 2][:, c * P:(c + 1) * P],
                                                       m.c("ident"))
                        last.then_inc(s["hturned"], 1)

                turn_x(0, 0)
                last_round = over_rounds(pe, body)
                down(last_round, 3)

            def keep_y(eng, half, copy, b, k, sem_):
                eng.wait_ge(s["down"], 4 * b + k + 1)
                if not (isinstance(b, int) and b == 0 and k < 2):
                    eng.wait_ge(kept[k % 2], 32 * b + 16 * (k // 2))
                copy(y[k % 2][:, 512 * half:512 * half + 512], yp[half][:]).then_inc(sem_, 1)

            def take_x(eng, half, copy, b, k, sem_):
                eng.wait_ge(s["turned"], 2 * (4 * b + k) + half + 1)
                copy(xT[k % 2][:, 4 * half:4 * half + 4, :],
                     tp[half][:].rearrange("p (k q) -> p k q", k=4)).then_inc(sem_, 1)

            @block.scalar
            def _(act):
                copy = lambda o, a: nc.scalar.activation(o, a, ACT.Copy)

                def body(b):
                    for k in range(SLOTS):
                        n = 4 * b + k
                        act.wait_ge(s["gated"], n + 1)
                        nc.scalar.activation(sg[k % 2][:], gu[k % 2][:, 0:FF], ACT.Silu).then_inc(s["silu"], 1)
                        take_x(act, 0, copy, b + 1 if k == 3 else b, (k + 1) % 4, s["xT0"])
                        if k:
                            keep_y(act, 0, copy, b, k - 1, s["y0"])
                        elif not isinstance(b, int):
                            keep_y(act, 0, copy, b - 1, 3, s["y0"])
                        act.wait_ge(s["hturned"], n + 1)
                        copy(hT[:], th[:, 0:2 * P].rearrange("p (k q) -> p k q", k=2)).then_inc(s["hT"], 1)

                take_x(act, 0, copy, 0, 0, s["xT0"])
                last_round = over_rounds(act, body)
                keep_y(act, 0, copy, last_round, 3, s["y0"])

            @block.vector
            def _(dve):
                copy = lambda o, a: nc.vector.tensor_copy(o, a)

                def body(b):
                    for k in range(SLOTS):
                        n = 4 * b + k
                        dve.wait_ge(s["silu"], n + 1)
                        nc.vector.tensor_tensor(h[k % 2][:], sg[k % 2][:], gu[k % 2][:, FF:2 * FF],
                                                ALU.mult).then_inc(s["h"], 1)
                        take_x(dve, 1, copy, b + 1 if k == 3 else b, (k + 1) % 4, s["xT1"])
                        if k:
                            keep_y(dve, 1, copy, b, k - 1, s["y1"])
                        elif not isinstance(b, int):
                            keep_y(dve, 1, copy, b - 1, 3, s["y1"])

                take_x(dve, 1, copy, 0, 0, s["xT1"])
                last_round = over_rounds(dve, body)
                keep_y(dve, 1, copy, last_round, 3, s["y1"])


def phase_combine(nc, m, io, out):
    with ExitStack() as st:
        sem = phase_semaphores(nc, m)
        y = [st.enter_context(nc.sbuf_tensor(f"gy{b}", [P, D], F32)) for b in range(4)]
        idx = st.enter_context(nc.sbuf_tensor("gidx", [P, 2, NT], I32))
        got = [sem(f"g_g{b}") for b in range(4)]
        added, summed, gone, ready = sem("g_added"), sem("g_sum"), sem("g_out"), sem("g_idx")
        with nc.Block() as block:

            @block.gpsimd
            def _(pool):
                pool.wait_ge(ready, 1)
                for n in range(2 * NT):
                    t, k = divmod(n, 2)
                    if n >= 4:
                        pool.wait_ge(added, n - 3)
                    nc.gpsimd.indirect_dma_start(y[n % 4][:], None, m.y_d,
                                                 bass.IndirectOffsetOnAxis(idx[:, k, t:t + 1], 0)).then_inc(got[n % 4], 16)

            @block.vector
            def _(dve):
                nc.vector.tensor_copy(idx[:], m.slot[:]).then_inc(ready, 1)
                for n in range(2 * NT):
                    t, k = divmod(n, 2)
                    dve.wait_ge(got[n % 4], 16 * (n // 4) + 16)
                    if k:
                        dve.wait_ge(added, n)
                    nc.vector.scalar_tensor_tensor(m.x1[:, t, :], y[n % 4][:], m.wts[:, k, t:t + 1], m.x1[:, t, :],
                                                   ALU.mult, ALU.add).then_inc(added, 1)

            @block.sync
            def _(sp):
                ov = out.rearrange("b (t p) d -> (b t) p d", p=P)
                for t in range(NT):
                    sp.wait_ge(added, 2 * t + 2)
                    sp.dma_start(ov[t], m.x1[:, t, :]).then_inc(gone, 16)
                sp.wait_ge(gone, 16 * NT)


def build(nc, io, out):
    with ExitStack() as st:
        sb = lambda n, s, d=F32: st.enter_context(nc.sbuf_tensor(n, s, d))
        sem = lambda n: st.enter_context(nc.semaphore(n))
        m = Memory()
        dram = lambda n, s: nc.dram_tensor(n, s, F32, kind="Internal").ap()
        m.q_d = dram("q_d", [NT, P, 512])
        m.oc_d = dram("oc_d", [S, D])
        m.h_d = dram("h_d", [S, D])
        m.y_d = dram("y_d", [MAXI * P, D])
        m.arena = sb("arena", [P, KT * PROJ])
        m.early = sb("early", [P, NEARLY])
        m.gcol = sb("gcol", [P, 8])
        m.mhalf = sb("mhalf", [P, 16])
        m.qgain, m.mqgain = sb("qgain", [P, 1]), sb("mqgain", [P, 1])
        m.kmT, m.vm = sb("kmT", [P, 2, 2, NMEM]), sb("vm", [P, 2, 256])
        m.w1_in = [sem("w1_k_in"), sem("w1_v_in")]
        m.w_out_in = sem("w_out_in")
        m.w_sem = [sem(f"w_sem{k}") for k in range(SLOTS)]

        def const(name):
            places, tile = next((p, t) for p, t in ((EARLY, m.early), (MIDDLE, m.middle), (LATE, m.late)) if name in p)
            at, n = places[name]
            return tile[:, at:at + n]

        m.c = const
        m.middle = m.late = None
        W = KT * 2 * FF + 2 * D
        m.slot_size = W
        slot = lambda k: m.arena[:, k * W:(k + 1) * W]
        m.gateup = [slot(k)[:, 0:KT * 2 * FF].rearrange("p (k f) -> p k f", k=KT) for k in range(SLOTS)]
        m.down = [slot(k)[:, KT * 2 * FF:W].rearrange("p (k d) -> p k d", k=2) for k in range(SLOTS)]
        upper = m.arena[:, 2 * W:4 * W]
        m.tail = m.arena[:, 4 * W:]
        m.w1 = m.arena[:, KT * (PROJ - 1024):KT * PROJ].rearrange("p (a n) -> p a n", a=2)
        m.w_out = upper[:, 0:KT * D].rearrange("p (k n) -> p k n", k=KT)
        m.wq = upper[:, KT * D:KT * D + KT * 256].rearrange("p (k n) -> p k n", k=KT)
        m.wo = upper[:, KT * D + KT * 256:KT * D + KT * 256 + 2 * D].rearrange("p (k n) -> p k n", k=2)

        with ExitStack() as st2:
            ab = lambda n, s, d=F32: st2.enter_context(nc.sbuf_tensor(n, s, d))
            m.kcvcT, m.ksT, m.kwT = [ab(n, [P, 2, S]) for n in "kcvcT ksT kwT".split()]
            m.vs, m.vw = ab("vs", [P, S]), ab("vw", [P, S])
            m.gate = ab("gate", [P, NT * 24])
            phase_project(nc, m, io)
            m.middle = ab("middle", [P, NMIDDLE])
            m.gout = ab("gout", [P, 512])
            m.identb, m.causalb, m.windowb = [ab(n, [P, P], BF16) for n in "identb causalb windowb".split()]
            m.eselb = ab("eselb", [P, S], BF16)
            m.kcT, m.vc = ab("kcT", [P, NG, 2, NC]), ab("vc", [P, NG, 2, HD])
            phase_keys(nc, m, io)
            m.ocmp = ab("ocmp", [P, NT, 512])
            m.notselT = ab("notselT", [P, NT // 2, NG, P], BF16)
            phase_select(nc, m, io)
            phase_attend(nc, m, io)
        nc.clear_and_free_semaphores(m.taken)
        m.taken = []
        nc.all_engine_barrier()
        m.late = sb("late", [P, NLATE])
        m.x1 = sb("x1", [P, NT, D])
        m.lg = sb("lg", [P, NT, 36])
        phase_mix(nc, m, io)
        m.wts, m.slot = sb("wts", [P, 2, NT]), sb("slot", [P, 2, NT])
        m.experts, m.rounds = sb("experts", [P, MAXI], I32), sb("rounds", [P, 1], I32)
        m.rows = sb("rows", [P, MAXI + SLOTS], I32)
        phase_route(nc, m, io)
        phase_experts(nc, m, io)
        phase_combine(nc, m, io, out)


def early_tables():
    t = np.zeros((P, NEARLY), np.float32)
    at = lambda n: slice(EARLY[n][0], EARLY[n][0] + EARLY[n][1])
    i = np.arange(P)
    t[:, at("ident")] = np.eye(P)
    t[:, at("tri")] = i[None, :] >= i[:, None]
    lg = np.log1p(-2.0 ** (-5.0 - np.arange(NH)))
    own = np.equal.outer(i // HD, i // HD)
    decay = np.exp(P * lg).reshape(4, 2)[:, i // HD]
    t[:, at("gammac")] = (own[:, None, :] * decay[None]).reshape(P, -1)
    return t


def middle_tables():
    t = np.zeros((P, NMIDDLE), np.float32)
    at = lambda n: slice(MIDDLE[n][0], MIDDLE[n][0] + MIDDLE[n][1])
    i = np.arange(P)
    tok = np.arange(NT)[None, :] * P + i[:, None]
    t[:, at("causal")] = np.where(i[None, :] > i[:, None], MASKED, 0)
    t[:, at("window")] = np.where(i[None, :] <= i[:, None], MASKED, 0)
    c = np.arange(NC)
    valid = (CS * c + CB - 1 <= tok[:, :, None]) & (c < NCR)
    t[:, at("cbias")] = np.where(valid, 0, MASKED).reshape(P, -1)
    t[:, at("cmask")] = valid.reshape(P, -1)
    j = np.arange(NSEL)
    cur = (tok // HD)[:, :, None]
    forced = (j == 0) | (j == cur) | (j == cur - 1)
    t[:, at("impa")] = (~forced & (j <= cur)).reshape(P, -1)
    t[:, at("impb")] = np.where(forced, 1e9, np.where(j > cur, MASKED, 0)).reshape(P, -1)
    c0, s0 = CS * np.arange(NCR), HD * np.arange(NSEL)
    ov = np.minimum(c0[None] + CB, s0[:, None] + HD) - np.maximum(c0[None], s0[:, None])
    sel = (np.clip(ov, 0, None) / CB).T
    t[0:NCR, at("selm")] = sel
    t[HD:HD + NCR, at("selm")] = sel
    t[0:NSEL, at("esel")] = np.where(np.arange(S)[None, :] // HD == j[:, None], MASKED, 0)
    return t


def late_tables():
    t = np.zeros((P, NLATE), np.float32)
    at = lambda n: slice(LATE[n][0], LATE[n][0] + LATE[n][1])
    i = np.arange(P)
    t[:, at("before")] = i[:, None] < i[None, :]
    t[:, at("ones")] = 1.0
    t[:, at("iota")] = i[None, :]
    t[:, at("thr")] = P * np.arange(16)[None, :]
    t[:, at("eid")] = np.arange(NE)[None, :]
    t[:, at("pref8")] = 8 - np.arange(8)[None, :]
    t[:, at("tokid")] = np.arange(NT)[None, :] * P + i[:, None]
    t[:, at("item")] = np.arange(MAXI)[None, :]
    t[:, at("thr4")] = SLOTS * np.arange(4)[None, :]
    return t


def rope_tables():
    half = HD // 2
    inv = 10000.0 ** (-np.arange(half, dtype=np.float32) / half)
    ang = (np.arange(S, dtype=np.float32)[:, None] * inv[None, :].astype(np.float32)).astype(np.float64)
    lg = np.log1p(-2.0 ** (-5.0 - np.arange(NH)))
    place = (np.arange(S) % P + 1.0)[:, None, None]
    up, down = np.exp(place * lg[None, :, None]), np.exp(-place * lg[None, :, None]) * HD ** -0.5
    parts = [f(ang)[:, None, :] * w for w in (up, down) for f in (np.cos, np.sin)]
    return np.concatenate([p.reshape(S, NH * half) for p in parts], axis=1).astype(np.float32)


def kernel(**inputs):
    import concourse.bacc as bacc
    from concourse.bass_utils import run_bass_kernel_spmd

    a = {n: np.asarray(v) for n, v in inputs.items()}
    rows = lambda v: np.ascontiguousarray(np.broadcast_to(v.reshape(1, -1), (P, v.size)))
    twice = lambda v: np.concatenate([v.reshape(-1), v.reshape(-1)])
    gcol = np.zeros((P, 8), np.float32)
    for j, n in enumerate(("nsa_q_norm", "nsa_ksel_norm", "nsa_kwin_norm", "mem_q_norm", "mem_k_norm",
                           "nsa_kcmp_norm")):
        gcol[:, j] = twice(a[n])
    posT = np.stack([np.concatenate([a[n][0].T, a[n][0].T]) for n in ("cmp_pos_k", "cmp_pos_v")], axis=1)
    arrays = {
        "x": a["x"][0], "mem": a["mem"][0], "w_in": a["w_in"][0], "w_out": a["w_out"][0],
        "mem_wq": a["mem_wq"][0], "mem_wkv": a["mem_wkv"][0], "mem_wo": a["mem_wo"][0],
        "cmp_k_w1": a["cmp_k_w1"][0], "cmp_v_w1": a["cmp_v_w1"][0],
        "cmp_k_w2": a["cmp_k_w2"][0], "cmp_v_w2": a["cmp_v_w2"][0],
        "cmp_pos": posT.reshape(P, 2 * CB),
        "g_mix": rows(a["mix_norm"]), "g_memx": rows(a["mem_x_norm"]), "g_memkv": rows(a["mem_kv_norm"]),
        "g_ffn": rows(a["ffn_norm"]), "g_out": rows(np.concatenate([a["nsa_out_norm"][0], a["ret_out_norm"][0]])),
        "gcol": gcol,
        "w_router": np.concatenate([a["router_group_w"][0], a["router_expert_w"][0].transpose(1, 0, 2).reshape(D, NE)],
                                   axis=1),
        "b_router": rows(np.concatenate([a["router_group_b"][0], a["router_expert_b"][0].reshape(NE)])),
        "w_gate": a["exp_w_gate"][0], "w_up": a["exp_w_up"][0], "w_down": a["exp_w_down"][0],
        "early": early_tables(), "middle": middle_tables(), "late": late_tables(), "rope": rope_tables(),
    }
    arrays = {n: np.ascontiguousarray(v) for n, v in arrays.items()}
    nc = bacc.Bacc("TRN2", target_bir_lowering=False, num_devices=1)
    io = {n: nc.dram_tensor("in_" + n, v.shape, mybir.dt.from_np(v.dtype), kind="ExternalInput").ap()
                            for n, v in arrays.items()}
    out = nc.dram_tensor("out_0", (1, S, D), F32, kind="ExternalOutput").ap()
    build(nc, io, out)
    r = run_bass_kernel_spmd(nc, [{"in_" + n: v for n, v in arrays.items()}], core_ids=[0])
    return r.results[0]["out_0"]
```

```python
from contextlib import ExitStack

import numpy as np
import concourse.bass as bass
from concourse import mybir

F32 = mybir.dt.float32
F32R = mybir.dt.float32r
BF16 = mybir.dt.bfloat16
I32 = mybir.dt.int32
ALU = mybir.AluOpType
ACT = mybir.ActivationFunctionType
AX = mybir.AxisListType

P = 128
D = 1024
S = 1024
KT = D // P
NT = S // P
HD = 64
NH = 8
NG = 2
HPG = NH // NG
PROJ = 3352
NMEM = 256
MH = 4
NC = 64
NCR = 63
CB = 32
CS = 16
NSEL = 16
NE = 32
EG = 8
FF = 256
MAXI = 48
SLOTS = 4
MASKED = -1e30
TAKEN = -3e38
EPS = 1e-6

CHUNKS = [(1304, 512), (1816, 512), (2328, 512), (0, 512), (512, 512), (1024, 280), (2840, 512)]
RQ, RK, RV, Q, KV1, KV2, RG = range(7)



def pack(items):
    at, places = 0, {}
    for name, n in items:
        places[name] = (at, n)
        at += n
    return places, at


EARLY, NEARLY = pack([("ident", 128), ("tri", 128), ("gammac", 512)])
MIDDLE, NMIDDLE = pack([("causal", 128), ("window", 128), ("cbias", 512), ("cmask", 64), ("impa", 128), ("impb", 128),
                        ("selm", 16), ("esel", 1024)])
LATE, NLATE = pack([("before", 128), ("ones", 128), ("iota", 128), ("thr", 16), ("eid", 32), ("pref8", 8),
                    ("place", 1), ("tile", 16), ("item", 48), ("thr4", 4)])


class Chain:

    def __init__(self, eng, sem, base=0):
        self.eng, self.sem, self.base, self.n = eng, sem, base, 0

    def __call__(self, ins):
        ins.then_inc(self.sem, 1)
        self.n += 1
        self.eng.wait_ge(self.sem, self.base + self.n)


class Memory:

    def __init__(self):
        self.taken = []


def phase_semaphores(nc, m):
    def take(name):
        m.taken.append(nc.alloc_semaphore(name=name))
        return m.taken[-1]

    return take


def bc(ap, shape):
    return ap.to_broadcast(shape)


def heads(ap, n=NH):
    return ap.rearrange("p (h d) -> p h d", h=n)


def phase_project(nc, m, io):
    with ExitStack() as st:
        sem = phase_semaphores(nc, m)
        sb = lambda n, s, d=F32: st.enter_context(nc.sbuf_tensor(n, s, d))
        ps = lambda n: st.enter_context(nc.psum_tensor(n, [P, 512], F32))
        x = sb("x", [P, D])
        grow = sb("grow", [P, D])
        xs = sb("xs", [P, D])
        xT = sb("xT", [P, KT, P])
        rope = sb("rope", [P, 4, 256])
        raw = sb("raw", [P, 7, 512])
        rq, rk, t1, t2 = [sb(n, [P, 512]) for n in "rq rk t1 t2".split()]
        yc, qn = t2, rq
        rqT = sb("rqT", [P, 4, P])
        rkT = sb("rkT", [P, 4, P])
        inT = sb("inT", [P, NH, P])
        qT = sb("qT", [P, 512])
        kd = sb("kd", [P, 2, NG, 2, HD])
        kt = kd[:].rearrange("p b g a d -> p b g (a d)")
        state = sb("state", [P, 4, P])
        gret = sb("gret", [P, 512])
        sg = sb("sg", [P, 512])
        ssx = sb("ssx", [P, 1])
        stat = sb("stat", [P, 16])
        pw = sb("pw", [P, 16])
        ystat = sb("ystat", [P, 16])
        ypw = sb("ypw", [P, 8])
        tp = [ps("tp0"), ps("tp1")]
        pj = [ps("pj0"), ps("pj1")]
        inn = [ps("in0"), ps("in1")]
        yp, sp_ = ps("yp"), ps("stp")
        s = {n: sem("p_" + n) for n in (
            "const_in gret_in x_in rope_in sq xs turned evac proj raw roped inner masked ready2 upd y "
            "ms rs qn yms yrs sig qout out oout chain qgain xms xrs split").split()}
        w_in_sem = [sem(f"w_in{c}") for c in range(7)]
        w, at = {}, 0
        for c in (RV, Q, KV1, KV2, RG, RQ, RK):
            n = CHUNKS[c][1]
            w[c] = m.arena[:, at:at + KT * n].rearrange("p (k n) -> p k n", k=KT)
            at += KT * n
        NCH = 20
        xv = io["x"].rearrange("(t p) d -> t p d", p=P)
        rv = io["rope"].rearrange("(t p) n -> t p n", p=P)
        ocv = m.oc_d.rearrange("(t p) d -> t p d", p=P)

        def tiles(eng, body):
            body(0, False)
            with eng.Fori(1, NT - 1) as i:
                body(i, False)
            body(NT - 1, True)

        def first(i):
            return isinstance(i, int) and i == 0

        with nc.Block() as block:

            @block.sync
            def _(sp):
                sp.dma_start(x[:], xv[0]).then_inc(s["x_in"], 16)
                sp.dma_start(grow[:], io["g_mix"]).then_inc(s["const_in"], 16)
                sp.dma_start(m.early[:], io["early"]).then_inc(s["const_in"], 16)
                sp.dma_start(m.gcol[:], io["gcol"]).then_inc(s["const_in"], 16)
                for c in range(7):
                    at, n = CHUNKS[c]
                    sp.dma_start(w[c], io["w_in"].rearrange("(k p) n -> p k n", p=P)[:, :, at:at + n]
                                 ).then_inc(w_in_sem[c], 16)
                    if c == 0:
                        sp.dma_start(rope[:].rearrange("p a b -> p (a b)"), rv[0]).then_inc(s["rope_in"], 16)
                sp.dma_start(gret[:], io["g_out"][:, 512:1024]).then_inc(s["gret_in"], 16)
                for a in range(2):
                    sp.dma_start(m.w2[:, a, :], (io["cmp_k_w2"], io["cmp_v_w2"])[a]).then_inc(m.w2_in, 16)
                sp.dma_start(m.pos[:].rearrange("p a b -> p (a b)"), io["cmp_pos"]).then_inc(m.w2_in, 16)

                def body(i, last):
                    if not last:
                        sp.wait_ge(s["xs"], i + 1)
                        sp.dma_start(x[:], xv[i + 1]).then_inc(s["x_in"], 16)
                        sp.wait_ge(s["roped"], 2 * i + 2)
                        sp.dma_start(rope[:].rearrange("p a b -> p (a b)"), rv[i + 1]).then_inc(s["rope_in"], 16)
                    sp.wait_ge(s["evac"], 7 * i + (5 if last else 7))
                    sp.dma_start(m.q_d[i], qT[:]).then_inc(s["qout"], 16)
                    sp.wait_ge(s["out"], i + 1)
                    sp.dma_start(ocv[i, :, 512:1024], sg[:]).then_inc(s["oout"], 16)

                with sp.Fori(0, NT - 1) as i:
                    body(i, False)
                sp.wait_ge(s["proj"], 7 * (NT - 1) + RQ + 1)
                for a, w1 in enumerate((io["cmp_k_w1"], io["cmp_v_w1"])):
                    sp.dma_start(m.w1[:, a, :].rearrange("q (p n) -> q p n", p=CB // 2),
                                 w1.rearrange("(p q) n -> q p n", q=P)).then_inc(m.w1_in[a], 16)
                body(NT - 1, True)
                sp.wait_ge(s["qout"], 16 * NT)
                sp.wait_ge(s["oout"], 16 * NT)

            @block.scalar
            def _(act):
                squares = raw[:, Q:Q + 2, :].rearrange("p a b -> p (a b)")

                def square(i):
                    act.wait_ge(s["x_in"], 16 * i + 16)
                    nc.scalar.activation(squares, x[:], ACT.Square, accum_out=ssx[:]).then_inc(s["sq"], 1)

                def turn_x(u):
                    for h in range(2):
                        act.wait_ge(s["turned"], u + h + 1)
                        nc.scalar.activation(xT[:, 4 * h:4 * h + 4, :],
                                             tp[h][:].rearrange("p (k q) -> p k q", k=4),
                                             ACT.Copy).then_inc(s["evac"], 1)

                def evac(i, c):
                    act.wait_ge(s["proj"], 7 * i + c + 1)
                    n = CHUNKS[c][1]
                    src = inn[0] if c == RG else pj[c % 2]
                    nc.scalar.activation(raw[:, c, 0:n], src[:, 0:n], ACT.Copy).then_inc(s["raw"], 1)

                def body(i, last):
                    u = 2 + 7 * i
                    evac(i, RQ)
                    if not last:
                        square(i + 1)
                    evac(i, RK)
                    for n, dst in enumerate((rqT, rkT)):
                        act.wait_ge(s["turned"], u + n + 1)
                        nc.scalar.activation(dst[:], tp[n][:].rearrange("p (k q) -> p k q", k=4),
                                             ACT.Copy).then_inc(s["evac"], 1)
                        evac(i, RV + n)
                    evac(i, KV1)
                    evac(i, KV2)
                    evac(i, RG)
                    if not last:
                        turn_x(u + 2)
                        u += 2
                    act.wait_ge(s["raw"], 7 * i + 7)
                    nc.scalar.activation(m.gate[:, bass.ts(i, 24)], raw[:, KV2, 256:280], ACT.Sigmoid)
                    if not first(i):
                        act.wait_ge(s["oout"], 16 * i)
                    nc.scalar.activation(sg[:], raw[:, RG, :], ACT.Sigmoid).then_inc(s["sig"], 1)
                    act.wait_ge(s["turned"], u + 3)
                    if not first(i):
                        act.wait_ge(s["qout"], 16 * i)
                    nc.scalar.activation(qT[:], tp[0][:], ACT.Copy, scale=m.qgain[:]).then_inc(s["evac"], 1)
                    act.wait_ge(s["turned"], u + 4)
                    nc.scalar.activation(m.kcvcT[:, :, bass.ts(i, P)],
                                         tp[1][:, 0:256].rearrange("p (a q) -> p a q", a=2), ACT.Copy)
                    nc.scalar.activation(kt[:, 0], tp[1][:, 256:512].rearrange("p (a q) -> p a q", a=2), ACT.Copy,
                                         scale=m.gcol[:, 1:2]).then_inc(s["evac"], 1)
                    act.wait_ge(s["turned"], u + 5)
                    nc.scalar.activation(kt[:, 1], tp[0][:, 0:256].rearrange("p (a q) -> p a q", a=2), ACT.Copy,
                                         scale=m.gcol[:, 2:3]).then_inc(s["evac"], 1)

                square(0)
                turn_x(0)
                act.wait_ge(s["qgain"], 1)
                tiles(act, body)

            @block.gpsimd
            def _(pool):
                def root_x(i):
                    pool.wait_ge(s["xms"], i + 1)
                    nc.gpsimd.tensor_tensor(pw[:, 12:13], stat[:, 12:13], m.mhalf[:, 0:1], ALU.pow
                            ).then_inc(s["xrs"], 1)

                def body(i, last):
                    if not last:
                        root_x(i + 1)
                    pool.wait_ge(s["raw"], 7 * i + 6)
                    nc.gpsimd.tensor_copy(m.vs[:, bass.ts(i, P)], raw[:, KV1, 384:512])
                    nc.gpsimd.tensor_copy(m.vw[:, bass.ts(i, P)], raw[:, KV2, 128:256])
                    pool.wait_ge(s["ms"], i + 1)
                    nc.gpsimd.tensor_tensor(pw[:, 0:12], stat[:, 0:12], m.mhalf[:, 0:12], ALU.pow).then_inc(s["rs"], 1)
                    pool.wait_ge(s["yms"], i + 1)
                    nc.gpsimd.tensor_tensor(ypw[:], ystat[:, 0:8], m.mhalf[:, 0:8], ALU.pow).then_inc(s["yrs"], 1)
                    pool.wait_ge(s["evac"], 2 + 7 * i + (5 if last else 7))
                    for b, t in enumerate((m.ksT, m.kwT)):
                        nc.gpsimd.tensor_copy(t[:, :, bass.ts(i, P)], kt[:, b]).then_inc(s["split"], 1)
                        pool.wait_ge(s["split"], 4 * i + 2 * b + 1)
                        nc.gpsimd.tensor_tensor(t[HD:P, :, bass.ts(i, P)], kt[HD:P, b], t[HD:P, :, bass.ts(i, P)],
                                                ALU.subtract).then_inc(s["split"], 1)
                        pool.wait_ge(s["split"], 4 * i + 2 * b + 2)

                root_x(0)
                tiles(pool, body)

            @block.vector
            def _(dve):
                def rotate(done, src, dst, cos, sin, last_sem):
                    v = src.rearrange("p (h a d) -> p h a d", h=NH, a=2)
                    o = dst[:].rearrange("p (h a d) -> p h a d", h=NH, a=2)
                    a = t1[:].rearrange("p (h a d) -> p h a d", h=NH, a=2)
                    b = t2[:].rearrange("p (h a d) -> p h a d", h=NH, a=2)
                    c = rope[:, cos, :].rearrange("p (h o d) -> p h o d", h=NH, o=1)
                    sn = rope[:, sin, :].rearrange("p (h o d) -> p h o d", h=NH, o=1)
                    done(nc.vector.tensor_tensor(a, v, bc(c, [P, NH, 2, 32]), ALU.mult))
                    done(nc.vector.tensor_tensor(b, v, bc(sn, [P, NH, 2, 32]), ALU.mult))
                    done(nc.vector.tensor_tensor(o[:, :, 0], a[:, :, 0], b[:, :, 1], ALU.subtract))
                    nc.vector.tensor_tensor(o[:, :, 1], b[:, :, 0], a[:, :, 1], ALU.add).then_inc(last_sem, 1)

                def norm_x(i):
                    nc.vector.scalar_tensor_tensor(xs[:], x[:], pw[:, 12:13], grow[:], ALU.mult,
                                                   ALU.mult).then_inc(s["xs"], 1)
                    dve.wait_ge(s["xs"], i + 1)

                def body(i, last):
                    done = Chain(dve, s["chain"], 4 + NCH * i)
                    if not last:
                        dve.wait_ge(s["sq"], i + 2)
                        nc.vector.tensor_scalar(stat[:, 12:13], ssx[:], 1.0 / D, EPS, ALU.mult,
                                                ALU.add).then_inc(s["xms"], 1)
                    dve.wait_ge(s["rope_in"], 16 * i + 16)
                    dve.wait_ge(s["raw"], 7 * i + 1)
                    rotate(done, raw[:, RQ, :], rq, 0, 1, s["roped"])
                    dve.wait_ge(s["roped"], 2 * i + 1)
                    dve.wait_ge(s["raw"], 7 * i + 2)
                    rotate(done, raw[:, RK, :], rk, 2, 3, s["roped"])
                    dve.wait_ge(s["roped"], 2 * i + 2)
                    for h in range(2):
                        dve.wait_ge(s["inner"], 2 * i + h + 1)
                        nc.vector.tensor_tensor(inT[:].rearrange("p (a b) q -> p b a q", b=2)[:, h],
                                                inn[h][:].rearrange("p (a q) -> p a q", a=4),
                                                bc(m.c("tri").unsqueeze(1), [P, 4, P]), ALU.mult
                                                        ).then_inc(s["masked"], 1)
                        dve.wait_ge(s["masked"], 2 * i + h + 1)
                    if not last:
                        dve.wait_ge(s["xrs"], i + 2)
                        norm_x(i + 1)
                    dve.wait_ge(s["raw"], 7 * i + 6)
                    done(nc.vector.tensor_tensor(t1[:], raw[:, Q, :], raw[:, Q, :], ALU.mult))
                    done(nc.vector.tensor_reduce(stat[:, 0:8], heads(t1[:]), AX.X, ALU.add))
                    done(nc.vector.tensor_tensor(t1[:, 0:128], raw[:, KV1, 256:384], raw[:, KV1, 256:384], ALU.mult))
                    done(nc.vector.tensor_tensor(t1[:, 128:256], raw[:, KV2, 0:128], raw[:, KV2, 0:128], ALU.mult))
                    done(nc.vector.tensor_reduce(stat[:, 8:12], heads(t1[:, 0:256], 4), AX.X, ALU.add))
                    nc.vector.tensor_scalar(stat[:, 0:12], stat[:, 0:12], 1.0 / HD, EPS, ALU.mult,
                                            ALU.add).then_inc(s["ms"], 1)
                    dve.wait_ge(s["rs"], i + 1)
                    nc.vector.tensor_tensor(heads(qn[:]), heads(raw[:, Q, :]),
                                            bc(pw[:, 0:8].unsqueeze(2), [P, NH, HD]), ALU.mult).then_inc(s["qn"], 1)
                    if not first(i):
                        dve.wait_ge(s["split"], 4 * i)
                    for b, (c, at) in enumerate(((KV1, 256), (KV2, 0))):
                        for dup in range(2):
                            nc.vector.tensor_tensor(kd[:, b, :, dup, :], heads(raw[:, c, at:at + 128], 2),
                                                    bc(pw[:, 8 + 2 * b:10 + 2 * b].unsqueeze(2), [P, NG, HD]),
                                                    ALU.mult).then_inc(s["qn"], 1)
                    dve.wait_ge(s["qn"], 5 * i + 5)
                    dve.wait_ge(s["y"], i + 1)
                    dve.wait_ge(s["upd"], i + 1)
                    st2 = state[:].rearrange("p a b -> p (a b)")
                    done(nc.vector.tensor_tensor(st2, st2, sp_[:], ALU.add))
                    nc.vector.tensor_tensor(st2, st2, m.c("gammac"), ALU.mult).then_inc(s["ready2"], 1)
                    dve.wait_ge(s["ready2"], i + 2)
                    done(nc.vector.tensor_reduce(ystat[:, 0:8], heads(yp[:]), AX.X, ALU.add))
                    done(nc.vector.tensor_scalar(ystat[:, 8:16], ystat[:, 0:8], 1.0 / HD, None, ALU.mult))
                    done(nc.vector.tensor_tensor(heads(yc[:]), heads(yp[:]),
                                                 bc(ystat[:, 8:16].unsqueeze(2), [P, NH, HD]), ALU.subtract))
                    done(nc.vector.tensor_tensor(t1[:], yc[:], yc[:], ALU.mult))
                    done(nc.vector.tensor_reduce(ystat[:, 0:8], heads(t1[:]), AX.X, ALU.add))
                    nc.vector.tensor_scalar(ystat[:, 0:8], ystat[:, 0:8], 1.0 / HD, EPS, ALU.mult,
                                            ALU.add).then_inc(s["yms"], 1)
                    dve.wait_ge(s["sig"], i + 1)
                    done(nc.vector.tensor_tensor(t1[:], raw[:, RG, :], sg[:], ALU.mult))
                    dve.wait_ge(s["gret_in"], 16)
                    done(nc.vector.tensor_tensor(t1[:], t1[:], gret[:], ALU.mult))
                    dve.wait_ge(s["yrs"], i + 1)
                    done(nc.vector.tensor_tensor(heads(yc[:]), heads(yc[:]), bc(ypw[:].unsqueeze(2), [P, NH, HD]),
                                                 ALU.mult))
                    nc.vector.tensor_tensor(sg[:], yc[:], t1[:], ALU.mult).then_inc(s["out"], 1)
                    dve.wait_ge(s["out"], i + 1)
                    if not last:
                        assert done.n == NCH, done.n

                done = Chain(dve, s["chain"])
                done(nc.vector.memset(m.mhalf[:], -0.5))
                done(nc.vector.memset(stat[:], 1.0))
                done(nc.vector.memset(pw[:], 1.0))
                nc.vector.memset(state[:], 0.0).then_inc(s["ready2"], 1)
                dve.wait_ge(s["sq"], 1)
                nc.vector.tensor_scalar(stat[:, 12:13], ssx[:], 1.0 / D, EPS, ALU.mult, ALU.add).then_inc(s["xms"], 1)
                dve.wait_ge(s["xrs"], 1)
                dve.wait_ge(s["const_in"], 48)
                norm_x(0)
                done(nc.vector.tensor_scalar(m.qgain[:], m.gcol[:, 0:1], HD ** -0.5, None, ALU.mult))
                nc.vector.tensor_scalar(m.mqgain[:], m.gcol[:, 3:4], HD ** -0.5, None, ALU.mult).then_inc(s["qgain"], 1)
                tiles(dve, body)

            @block.tensor
            def _(pe):
                def turn(bank, pieces):
                    for k, p in enumerate(pieces):
                        last = nc.tensor.transpose(tp[bank][:, k * P:(k + 1) * P], p, m.c("ident"))
                    last.then_inc(s["turned"], 1)

                def turn_x(i, u, first=False):
                    pe.wait_ge(s["xs"], i + 1)
                    for h in range(2):
                        if not first:
                            pe.wait_ge(s["evac"], u + h - 1)
                        turn(h, [xs[:, (4 * h + k) * P:(4 * h + k + 1) * P] for k in range(4)])

                def project(i, c):
                    n = CHUNKS[c][1]
                    if c >= 2:
                        pe.wait_ge(s["raw"], 7 * i + c - 1)
                    pe.wait_ge(w_in_sem[c], 16)
                    dst = inn[0] if c == RG else pj[c % 2]
                    for k in range(KT):
                        last = nc.tensor.matmul(dst[:, 0:n], xT[:, k, :], w[c][:, k, :],
                                                start=k == 0, stop=k == KT - 1)
                    last.then_inc(s["proj"], 1)

                def body(i, last_tile):
                    u = 2 + 7 * i
                    project(i, RQ)
                    project(i, RK)
                    pe.wait_ge(s["roped"], 2 * i + 1)
                    pe.wait_ge(s["evac"], u)
                    turn(0, [rq[:, k * P:(k + 1) * P] for k in range(4)])
                    project(i, RV)
                    pe.wait_ge(s["roped"], 2 * i + 2)
                    turn(1, [rk[:, k * P:(k + 1) * P] for k in range(4)])
                    project(i, Q)
                    pe.wait_ge(s["evac"], u + 2)
                    for h in [0, 2, 4, 6, 1, 3, 5, 7]:
                        r = slice(HD * (h % 2), HD * (h % 2) + HD)
                        last = nc.tensor.matmul(inn[h % 2][:, (h // 2) * P:(h // 2 + 1) * P], rkT[r, h // 2, :],
                                                rqT[r, h // 2, :], start=True, stop=True)
                        if h >= 6:
                            last.then_inc(s["inner"], 1)
                    pe.wait_ge(s["raw"], 7 * i + 3)
                    for a in range(4):
                        last = nc.tensor.matmul(sp_[:, a * P:(a + 1) * P], rk[:, a * P:(a + 1) * P],
                                                raw[:, RV, a * P:(a + 1) * P], start=True, stop=True)
                    last.then_inc(s["upd"], 1)
                    project(i, KV1)
                    project(i, KV2)
                    pe.wait_ge(s["masked"], 2 * i + 2)
                    project(i, RG)
                    if not last_tile:
                        turn_x(i + 1, u + 2)
                    pe.wait_ge(s["ready2"], i + 1)
                    for a in range(4):
                        nc.tensor.matmul(yp[:, a * P:(a + 1) * P], rqT[:, a, :], state[:, a, :], start=True,
                                         stop=False)
                        for h in (2 * a, 2 * a + 1):
                            last = nc.tensor.matmul(yp[:, h * HD:(h + 1) * HD], inT[:, h, :],
                                                    raw[:, RV, h * HD:(h + 1) * HD], start=False, stop=h % 2 == 1)
                    last.then_inc(s["y"], 1)
                    pe.wait_ge(s["qn"], 5 * i + 1)
                    if last_tile:
                        pe.wait_ge(s["evac"], u + 1)
                        turn(0, [qn[:, k * P:(k + 1) * P] for k in range(4)])
                        u -= 2
                    else:
                        pe.wait_ge(s["evac"], u + 3)
                        turn(0, [qn[:, k * P:(k + 1) * P] for k in range(4)])
                    pe.wait_ge(s["qn"], 5 * i + 5)
                    pe.wait_ge(s["evac"], u + 4)
                    turn(1, [raw[:, KV1, 0:128], raw[:, KV1, 128:256]] +
                         [kd[:, 0, g].rearrange("p a d -> p (a d)") for g in range(NG)])
                    pe.wait_ge(s["evac"], u + 5)
                    turn(0, [kd[:, 1, g].rearrange("p a d -> p (a d)") for g in range(NG)])

                pe.wait_ge(s["const_in"], 48)
                turn_x(0, 0, True)
                pe.wait_ge(s["evac"], 2)
                tiles(pe, body)


def phase_keys(nc, m, io):
    T = 2
    with ExitStack() as st:
        sem = phase_semaphores(nc, m)
        sb = lambda n, s, d=F32: st.enter_context(nc.sbuf_tensor(n, s, d))
        ps = lambda n: st.enter_context(nc.psum_tensor(n, [P, 512], F32))
        w2, pos = m.w2, m.pos
        blk = sb("cblk", [P, CB // 2, NG, NC])
        sg = sb("csg", [P, 2 * NCR])
        hid = sb("chid", [P, 2, 2 * NCR])
        kc = sb("ckc", [NC, NG, HD])
        kn = sb("ckn", [NC, NG, 2, HD])
        stat = sb("cstat", [NC, 2])
        pw = sb("cpw", [NC, 2])
        spare = m.arena[:, 2 * m.slot_size:]
        wkv = spare[:, 0:KT * 512].rearrange("p (k n) -> p k n", k=KT)
        mem = spare[:, KT * 512:KT * 512 + T * D].rearrange("p (t d) -> p t d", t=T)
        hT = sb("memT", [P, KT, NMEM])
        squares = hT[:, 0:4, :].rearrange("p k q -> p (k q)")
        kv = sb("memkv", [P, T, 512])
        mkn = sb("memkn", [P, T, 256])
        mstat = sb("memstat", [P, 4 * T])
        mpw = sb("mempw", [P, 4 * T])
        gmem = sb("gmem", [P, D])
        hp = [ps(f"chp{a}") for a in range(2)]
        op, ctp = ps("cop"), ps("ctp")
        tp = [ps("mtp0"), ps("mtp1")]
        pj = [ps("mpj0"), ps("mpj1")]
        s = {n: sem("k_" + n) for n in (
            "late_in blk hid sig act out ms rs kn cturned chain wkv_in mem_in ssq mms mrs normed turned evac "
            "projected kraw kready cleared").split()}
        with nc.Block() as block:

            @block.sync
            def _(sp):
                sp.dma_start(mem, io["mem"].rearrange("(t p) d -> p t d", p=P)).then_inc(s["mem_in"], 16)
                sp.dma_start(gmem[:], io["g_memkv"]).then_inc(s["mem_in"], 16)
                sp.dma_start(wkv, io["mem_wkv"].rearrange("(k p) n -> p k n", p=P)).then_inc(s["wkv_in"], 16)
                sp.dma_start(m.middle[:], io["middle"]).then_inc(s["late_in"], 16)
                sp.dma_start(m.gout[:], io["g_out"][:, 0:512]).then_inc(s["late_in"], 16)
                for e in range(2):
                    load_expert(sp, m, io, e, e)

            @block.scalar
            def _(act):
                def gates(a):
                    act.wait_ge(s["hid"], a + 1)
                    if a:
                        act.wait_ge(s["act"], 1)
                    nc.scalar.activation(sg[:].rearrange("p (g c) -> p g c", g=NG),
                                         hp[a][:, 0:NG * NC].rearrange("p (g c) -> p g c", g=NG)[:, :, 0:NCR],
                                         ACT.Sigmoid).then_inc(s["sig"], 1)

                act.wait_ge(s["mem_in"], 32)
                for t in range(T):
                    nc.scalar.activation(squares, mem[:, t], ACT.Square, accum_out=mstat[:, t:t + 1]
                            ).then_inc(s["ssq"], 1)
                    act.wait_ge(s["ssq"], t + 1)
                gates(0)
                for n in range(4):
                    act.wait_ge(s["turned"], n + 1)
                    t, h = divmod(n, 2)
                    nc.scalar.activation(hT[:, 4 * h:4 * h + 4, t * P:(t + 1) * P],
                                         tp[n % 2][:].rearrange("p (k q) -> p k q", k=4), ACT.Copy
                                                 ).then_inc(s["evac"], 1)
                for t in range(T):
                    act.wait_ge(s["projected"], t + 1)
                    nc.scalar.activation(kv[:, t], pj[t][:], ACT.Copy).then_inc(s["kraw"], 1)
                gates(1)
                act.wait_ge(s["cleared"], 1)
                for t in range(T):
                    act.wait_ge(s["turned"], 4 + t + 1)
                    for half in range(2):
                        r = slice(HD * half, HD * half + HD)
                        nc.scalar.activation(m.kmT[r, :, half, t * P:(t + 1) * P],
                                             tp[t % 2][r, 0:256].rearrange("p (k q) -> p k q", k=2), ACT.Copy,
                                             scale=m.gcol[r, 4:5])
                act.wait_ge(s["cturned"], 1)
                for half in range(2):
                    r = slice(HD * half, HD * half + HD)
                    nc.scalar.activation(m.kcT[r, :, half, 0:NCR],
                                         ctp[r, 0:2 * NCR].rearrange("p (g c) -> p g c", g=NG),
                                         ACT.Copy, scale=m.gcol[r, 5:6])

            @block.gpsimd
            def _(pool):
                pool.wait_ge(s["mms"], 1)
                nc.gpsimd.tensor_tensor(mpw[:, 0:T], mstat[:, T:2 * T], m.mhalf[:, 0:T], ALU.pow).then_inc(s["mrs"], 1)
                for t in range(T):
                    pool.wait_ge(s["kraw"], t + 1)
                    nc.gpsimd.tensor_copy(m.vm[:, t], kv[:, t, 256:512])
                pool.wait_ge(s["mms"], 2)
                nc.gpsimd.tensor_tensor(mpw[:], mstat[:], m.mhalf[:, 0:4 * T], ALU.pow).then_inc(s["mrs"], 1)
                pool.wait_ge(s["ms"], 1)
                nc.gpsimd.tensor_tensor(pw[0:NCR], stat[0:NCR], m.mhalf[0:NCR, 0:2], ALU.pow).then_inc(s["rs"], 1)

            @block.vector
            def _(dve):
                done = Chain(dve, s["chain"])

                def blocks(a):
                    if a:
                        dve.wait_ge(s["hid"], a)
                    for half in range(2):
                        for g, odd in ((0, 0), (0, 1), (1, 0), (1, 1)):
                            r, to = slice(HD * g, HD * g + HD), slice(HD * odd, HD * odd + HD)
                            v = m.kcvcT[r, a, half * CS: half * CS + CS * NCR].rearrange(
                                "p (c q two) -> p q two c", two=2, q=CS // 2)[:, :, odd, :]
                            w = pos[r, a, half * CS:half * CS + CS].rearrange("p (q two) -> p q two", two=2)
                            nc.vector.tensor_tensor(blk[to, half * CS // 2:(half + 1) * CS // 2, g, 0:NCR], v,
                                                    bc(w[:, :, odd:odd + 1], [HD, CS // 2, NCR]),
                                                    ALU.add).then_inc(s["blk"], 1)

                def hidden(a):
                    dve.wait_ge(s["sig"], a + 1)
                    nc.vector.tensor_tensor(hid[:, a].rearrange("p (g c) -> p g c", g=NG),
                                            hp[a][:, 0:NG * NC].rearrange("p (g c) -> p g c", g=NG)[:, :, 0:NCR],
                                            sg[:].rearrange("p (g c) -> p g c", g=NG), ALU.mult).then_inc(s["act"], 1)

                nc.vector.memset(blk[:, :, :, NCR:NC], 0.0).then_inc(s["blk"], 1)
                dve.wait_ge(m.w2_in, 48)
                blocks(0)
                done(nc.vector.memset(m.kcT[:], 0.0))
                done(nc.vector.memset(m.vc[:], 0.0))
                nc.vector.memset(m.kmT[:], 0.0).then_inc(s["cleared"], 1)
                dve.wait_ge(s["ssq"], T)
                nc.vector.tensor_scalar(mstat[:, T:2 * T], mstat[:, 0:T], 1.0 / D, EPS, ALU.mult,
                                        ALU.add).then_inc(s["mms"], 1)
                dve.wait_ge(s["mem_in"], 32)
                dve.wait_ge(s["mrs"], 1)
                for t in range(T):
                    nc.vector.scalar_tensor_tensor(mem[:, t], mem[:, t], mpw[:, t:t + 1], gmem[:], ALU.mult,
                                                   ALU.mult).then_inc(s["normed"], 1)
                hidden(0)
                blocks(1)
                dve.wait_ge(s["late_in"], 32)
                done(nc.vector.tensor_copy(m.identb[:], m.c("ident")))
                done(nc.vector.tensor_copy(m.causalb[:], m.c("causal")))
                done(nc.vector.tensor_copy(m.windowb[:], m.c("window")))
                done(nc.vector.tensor_copy(m.eselb[:], m.c("esel")))
                done(nc.vector.tensor_copy(m.cbiasb[:], m.c("cbias")))
                dve.wait_ge(s["kraw"], T)
                done(nc.vector.tensor_tensor(mkn[:], kv[:, :, 0:256], kv[:, :, 0:256], ALU.mult))
                done(nc.vector.tensor_reduce(mstat[:], mkn[:].rearrange("p t (h d) -> p (t h) d", d=HD), AX.X, ALU.add))
                nc.vector.tensor_scalar(mstat[:], mstat[:], 1.0 / HD, EPS, ALU.mult, ALU.add).then_inc(s["mms"], 1)
                dve.wait_ge(s["mrs"], 2)
                nc.vector.tensor_tensor(mkn[:].rearrange("p t (h d) -> p t h d", d=HD),
                                        kv[:, :, 0:256].rearrange("p t (h d) -> p t h d", d=HD),
                                        bc(mpw[:].rearrange("p (t h o) -> p t h o", t=T, o=1), [P, T, MH, HD]),
                                        ALU.mult).then_inc(s["kready"], 1)
                hidden(1)
                dve.wait_ge(s["out"], 1)
                o = op[:].rearrange("p (a g d) -> p a g d", a=4, g=NG)
                done(nc.vector.tensor_copy(kc[0:NCR], o[0:NCR, 0]))
                done(nc.vector.tensor_tensor(kn[0:NCR, :, 0, :], kc[0:NCR], kc[0:NCR], ALU.mult))
                done(nc.vector.tensor_reduce(stat[0:NCR], kn[0:NCR, :, 0, :], AX.X, ALU.add))
                nc.vector.tensor_scalar(stat[0:NCR], stat[0:NCR], 1.0 / HD, EPS, ALU.mult, ALU.add).then_inc(s["ms"], 1)
                for half in range(2):
                    r = slice(HD * half, HD * half + NCR)
                    done(nc.vector.tensor_copy(m.vc[r, :, half, :], o[r, 1]))
                dve.wait_ge(s["rs"], 1)
                for dup in range(2):
                    nc.vector.tensor_tensor(kn[0:NCR, :, dup, :], kc[0:NCR],
                                            bc(pw[0:NCR].unsqueeze(2), [NCR, NG, HD]), ALU.mult).then_inc(s["kn"], 1)

            @block.tensor
            def _(pe):
                def first_layer(a):
                    pe.wait_ge(m.w1_in[a], 16)
                    for p in range(CB // 2):
                        if p % (CB // 4) == 0:
                            pe.wait_ge(s["blk"], 8 * a + 5 + 4 * (p // (CB // 4)))
                        last = nc.tensor.matmul(hp[a][:, 0:NG * NC], m.w1[:, a, p * P:(p + 1) * P],
                                                blk[:, p].rearrange("p g c -> p (g c)"), start=p == 0,
                                                stop=p == CB // 2 - 1)
                    last.then_inc(s["hid"], 1)

                first_layer(0)
                for n in range(4):
                    t, h = divmod(n, 2)
                    pe.wait_ge(s["normed"], t + 1)
                    if n >= 2:
                        pe.wait_ge(s["evac"], n - 1)
                    for k in range(4):
                        last = nc.tensor.transpose(tp[n % 2][:, k * P:(k + 1) * P],
                                                   mem[:, t, (4 * h + k) * P:(4 * h + k + 1) * P], m.c("ident"))
                    last.then_inc(s["turned"], 1)
                pe.wait_ge(s["wkv_in"], 16)
                pe.wait_ge(s["evac"], 4)
                for t in range(T):
                    for k in range(KT):
                        last = nc.tensor.matmul(pj[t][:], hT[:, k, t * P:(t + 1) * P], wkv[:, k, :],
                                                start=k == 0, stop=k == KT - 1)
                    last.then_inc(s["projected"], 1)
                first_layer(1)
                pe.wait_ge(s["kready"], 1)
                for t in range(T):
                    for k in range(2):
                        last = nc.tensor.transpose(tp[t][:, k * P:(k + 1) * P], mkn[:, t, k * P:(k + 1) * P],
                                                   m.c("ident"))
                    last.then_inc(s["turned"], 1)
                pe.wait_ge(m.w2_in, 48)
                pe.wait_ge(s["act"], 2)
                for a, half in ((0, 0), (1, 0), (1, 1)):
                    for g in range(NG):
                        last = nc.tensor.matmul(op[HD * half:HD * half + NCR, (a * NG + g) * HD:(a * NG + g + 1) * HD],
                                                hid[:, a, g * NCR:(g + 1) * NCR], w2[:, a, :], start=True, stop=True)
                last.then_inc(s["out"], 1)
                pe.wait_ge(s["kn"], 2)
                for g in range(NG):
                    last = nc.tensor.transpose(ctp[:, g * NCR:(g + 1) * NCR],
                                               kn[0:NCR, g].rearrange("p a d -> p (a d)"), m.c("ident")[0:NCR, 0:NCR])
                last.then_inc(s["cturned"], 1)


def load_expert(eng, m, io, e, slot):
    eng.dma_start(m.gateup[slot][:, :, 0:FF], io["w_gate"][e].rearrange("(p k) f -> p k f", p=P)
            ).then_inc(m.w_sem[slot], 16)
    eng.dma_start(m.gateup[slot][:, :, FF:2 * FF], io["w_up"][e].rearrange("(p k) f -> p k f", p=P)
            ).then_inc(m.w_sem[slot], 16)
    eng.dma_start(m.down[slot], io["w_down"][e].rearrange("(k p) d -> p k d", p=P)).then_inc(m.w_sem[slot], 16)


def phase_select(nc, m, io):
    with ExitStack() as st:
        sem = phase_semaphores(nc, m)
        sb = lambda n, s, d=F32: st.enter_context(nc.sbuf_tensor(n, s, d))
        ps = lambda n: st.enter_context(nc.psum_tensor(n, [P, 512], F32))
        qT = sb("sq", [P, NT, 512])
        sc = [sb(f"ssc{b}", [P, 512]) for b in range(2)]
        pT = [sb(f"spT{b}", [P, 4, P]) for b in range(2)]
        mx, den = [[sb(f"s{n}{b}", [P, NH]) for b in range(2)] for n in ("mx", "den")]
        imp = sb("simp", [P, NG, NSEL])
        top = sb("stop", [P, NG, 8])
        ocmp = [sb(f"socmp{b}", [P, 512]) for b in range(2)]
        notsel = sb("snot", [P, NG, NSEL])
        sp_ = [ps("ssp0"), ps("ssp1")]
        tp = [ps("stp0"), ps("stp1")]
        oc = [ps("soc0"), ps("soc1")]
        im, nt = ps("simp_"), ps("snt")
        s = {n: sem("s_" + n) for n in (
            "scored nmax expd probs turned evac outed taken imped impt notsel nturned nevac chain cleared kept").split()}
        qs = [sem(f"s_q{i}") for i in range(NT)]
        first_sel = (8 * 64) // P
        m.first_sel = first_sel
        with nc.Block() as block:

            @block.sync
            def _(sp):
                for i in range(NT):
                    sp.dma_start(qT[:, i, :], m.q_d[i]).then_inc(qs[i], 16)
                sp.dma_start(m.w_out, io["w_out"].rearrange("(k p) n -> p k n", p=P)).then_inc(m.w_out_in, 16)
                sp.dma_start(m.wq, io["mem_wq"].rearrange("(k p) n -> p k n", p=P)).then_inc(m.w_out_in, 16)
                sp.dma_start(m.wo, io["mem_wo"].rearrange("(k p) n -> p k n", p=P)).then_inc(m.w_out_in, 16)
                for i in range(NT):
                    sp.wait_ge(s["taken"], i + 1)
                    if i:
                        sp.wait_ge(s["kept"], 16 * i)
                    sp.dma_start(m.oc_d[i * P:(i + 1) * P, 0:512], ocmp[i % 2][:]).then_inc(s["kept"], 16)
                sp.wait_ge(s["kept"], 16 * NT)

            @block.tensor
            def _(pe):
                def scores(i):
                    pe.wait_ge(qs[i], 16)
                    if i >= 2:
                        pe.wait_ge(s["expd"], i - 1)
                    for a in range(4):
                        at = slice(a * P, (a + 1) * P)
                        nc.tensor.matmul(sp_[i % 2][:, at], qT[:, i, at], m.kcT[:, a // 2].rearrange("p a c -> p (a c)"),
                                         start=True, stop=False)
                        last = nc.tensor.matmul(sp_[i % 2][:, at], m.identb[:],
                                                bc(m.cbiasb[:, i * NC:(i + 1) * NC].unsqueeze(1), [P, 2, NC]),
                                                start=False, stop=True)
                    last.then_inc(s["scored"], 1)

                def outputs(i):
                    pe.wait_ge(s["probs"], i + 1)
                    if i >= 2:
                        pe.wait_ge(s["evac"], i - 1)
                    for k in range(4):
                        last = nc.tensor.transpose(tp[i % 2][:, k * P:(k + 1) * P], sc[i % 2][:, k * P:(k + 1) * P],
                                                   m.c("ident"))
                    last.then_inc(s["turned"], 1)
                    pe.wait_ge(s["evac"], i + 1)
                    if i >= 2:
                        pe.wait_ge(s["taken"], i - 1)
                    for a in range(4):
                        last = nc.tensor.matmul(oc[i % 2][:, a * P:(a + 1) * P], pT[i % 2][:, a, :],
                                                m.vc[:, a // 2].rearrange("p a d -> p (a d)"), start=True, stop=True)
                    last.then_inc(s["outed"], 1)
                    if i >= first_sel:
                        n = i - first_sel
                        if n:
                            pe.wait_ge(s["impt"], n)
                        for a in range(4):
                            last = nc.tensor.matmul(im[:, a // 2 * NSEL:(a // 2 + 1) * NSEL], pT[i % 2][:, a, :],
                                                    m.c("selm"), start=a % 2 == 0, stop=a % 2 == 1)
                        last.then_inc(s["imped"], 1)

                def unchosen(n):
                    pe.wait_ge(s["notsel"], n + 1)
                    if n:
                        pe.wait_ge(s["nevac"], n)
                    for g in range(NG):
                        last = nc.tensor.transpose(nt[0:NSEL, g * P:(g + 1) * P], notsel[:, g, :], m.c("ident"))
                    last.then_inc(s["nturned"], 1)

                scores(0)
                scores(1)
                for i in range(NT + 1):
                    if i + 2 < NT:
                        scores(i + 2)
                    if i < NT:
                        outputs(i)
                    if i > first_sel:
                        unchosen(i - 1 - first_sel)

            @block.scalar
            def _(act):
                def exponentials(i):
                    act.wait_ge(s["nmax"], i + 1)
                    if i >= 2:
                        act.wait_ge(s["turned"], i - 1)
                        act.wait_ge(s["probs"], i - 1)
                    for h in range(NH):
                        c = slice(h * NC, (h + 1) * NC)
                        last = nc.scalar.activation(sc[i % 2][:, c], sp_[i % 2][:, c], ACT.Exp, bias=mx[i % 2][:, h:h + 1],
                                                    accum_out=den[i % 2][:, h:h + 1])
                    last.then_inc(s["expd"], 1)

                def unchosen(n):
                    act.wait_ge(s["nturned"], n + 1)
                    nc.scalar.activation(m.notselT[0:NSEL, n], nt[0:NSEL, 0:NG * P].rearrange("p (g q) -> p g q", g=NG),
                                         ACT.Copy).then_inc(s["nevac"], 1)

                act.wait_ge(s["cleared"], 1)
                exponentials(0)
                for i in range(NT):
                    if i + 1 < NT:
                        exponentials(i + 1)
                    act.wait_ge(s["turned"], i + 1)
                    if i >= 2:
                        act.wait_ge(s["outed"], i - 1)
                    nc.scalar.activation(pT[i % 2][:], tp[i % 2][:].rearrange("p (k q) -> p k q", k=4),
                                         ACT.Copy).then_inc(s["evac"], 1)
                    act.wait_ge(s["outed"], i + 1)
                    if i >= 2:
                        act.wait_ge(s["kept"], 16 * (i - 1))
                    nc.scalar.activation(ocmp[i % 2][:], oc[i % 2][:], ACT.Copy).then_inc(s["taken"], 1)
                    if i > first_sel:
                        unchosen(i - 1 - first_sel)
                unchosen(NT - 1 - first_sel)

            @block.vector
            def _(dve):
                done = Chain(dve, s["chain"])

                def maximum(i):
                    dve.wait_ge(s["scored"], i + 1)
                    nc.vector.tensor_reduce(mx[i % 2][:], heads(sp_[i % 2][:]), AX.X, ALU.max,
                                            negate=True).then_inc(s["nmax"], 1)

                def finish(i):
                    dve.wait_ge(s["expd"], i + 1)
                    b, d = heads(sc[i % 2][:]), den[i % 2]
                    if i == 0:
                        done(nc.vector.tensor_tensor(b, b, bc(m.c("cmask")[:, 0:NC].unsqueeze(1), [P, NH, NC]), ALU.mult))
                        done(nc.vector.tensor_reduce(d[:], b, AX.X, ALU.add))
                        done(nc.vector.tensor_scalar(d[:], d[:], 1e-30, None, ALU.max))
                    done(nc.vector.reciprocal(d[:], d[:]))
                    nc.vector.tensor_tensor(b, b, bc(d[:].unsqueeze(2), [P, NH, NC]), ALU.mult).then_inc(s["probs"], 1)

                def choose(i):
                    n = i - first_sel
                    dve.wait_ge(s["imped"], n + 1)
                    if n:
                        dve.wait_ge(s["nturned"], n)
                    a = m.c("impa")[:, i * NSEL:(i + 1) * NSEL].unsqueeze(1)
                    b = m.c("impb")[:, i * NSEL:(i + 1) * NSEL].unsqueeze(1)
                    nc.vector.tensor_tensor(imp[:], im[:, 0:NG * NSEL].rearrange("p (g j) -> p g j", g=NG),
                                            bc(a, [P, NG, NSEL]), ALU.mult).then_inc(s["impt"], 1)
                    dve.wait_ge(s["impt"], n + 1)
                    done(nc.vector.tensor_tensor(imp[:], imp[:], bc(b, [P, NG, NSEL]), ALU.add))
                    for g in range(NG):
                        done(nc.vector.max(top[:, g, :], imp[:, g, :]))
                    for g in range(NG):
                        done(nc.vector.match_replace(notsel[:, g, :], top[:, g, :], imp[:, g, :], TAKEN))
                    nc.vector.tensor_scalar(notsel[:], notsel[:], TAKEN, None, ALU.not_equal).then_inc(s["notsel"], 1)

                nc.vector.memset(m.notselT[:], 0.0).then_inc(s["cleared"], 1)
                maximum(0)
                for i in range(NT):
                    if i + 1 < NT:
                        maximum(i + 1)
                    finish(i)
                    if i > first_sel:
                        choose(i - 1)
                choose(NT - 1)


def attention_units():
    for i in range(NT):
        for h in range(NH):
            yield i, h, 0, 0, i + 1
            yield i, h, 1, max(0, i - 4), min(i + 1, 5)


def phase_attend(nc, m, io):
    units = list(attention_units())
    before = list(m.taken)
    with ExitStack() as st:
        sem = phase_semaphores(nc, m)
        sb = lambda n, s, d=F32: st.enter_context(nc.sbuf_tensor(n, s, d))
        qT = sb("aq", [P, 4, 2, P])
        qhi, qlo = [[sb(f"aq{n}{b}", [P, NH, P], F32R) for b in range(2)] for n in ("hi", "lo")]
        ocmp = [sb(f"aoc{b}", [P, 512]) for b in range(2)]
        probs = [sb(f"ap{b}", [P, S]) for b in range(2)]
        pT = [sb(f"apT{b}", [P, NT, P]) for b in range(2)]
        nmax = sb("anm", [P, 4])
        den = [sb(f"aden{b}", [P, 2 * NH]) for b in range(2)]
        w = [sb(f"aw{b}", [P, 3 * NH]) for b in range(2)]
        t1, t2, out = [m.tail[:, k * 512:(k + 1) * 512] for k in range(3)]
        stat, pw = sb("astat", [P, 8]), sb("apw", [P, 8])
        sc = [st.enter_context(nc.psum_tensor(f"asc{b}", [P, S], F32)) for b in range(2)]
        tp = [st.enter_context(nc.psum_tensor(f"atp{b}", [P, 512], F32)) for b in range(2)]
        ov = [st.enter_context(nc.psum_tensor(f"aov{b}", [P, 512], F32)) for b in range(2)]
        s = {n: sem("a_" + n) for n in (
            "scored nmax expd turned evac0 evac1 valued read ms rs out oout chain q_in qsplit spare").split()}
        oc_in = [sem("a_oc0"), sem("a_oc1")]
        nc.clear_and_free_semaphores(before)
        pieces = [[(k, min(4, n - k)) for k in range(0, n, 4)] for _, _, _, _, n in units]
        first_piece = [0]
        for p in pieces:
            first_piece.append(first_piece[-1] + len(p))
        ocv = m.oc_d.rearrange("(t p) d -> t p d", p=P)
        U = len(units)
        PER = 2 * NH

        with nc.Block() as block:

            @block.sync
            def _(sp):
                def store(i):
                    sp.wait_ge(s["out"], i + 1)
                    sp.dma_start(ocv[i, :, 0:512], out[:]).then_inc(s["oout"], 16)

                for i in range(NT):
                    if i:
                        sp.wait_ge(s["qsplit"], 2 * i)
                    for parity in range(2):
                        for half in range(2):
                            sp.dma_start(qT[HD * half:HD * half + HD, :, parity, :],
                                         m.q_d[i, HD * parity:HD * parity + HD, :].rearrange("p (a q) -> p a q", a=4)
                                         ).then_inc(s["q_in"], 16)
                    if i >= 2:
                        store(i - 2)
                    sp.dma_start(ocmp[i % 2][:], ocv[i, :, 0:512]).then_inc(oc_in[i % 2], 16)
                    if i == NT - 1:
                        sp.wait_ge(m.w_out_in, 48)
                        spare = m.y_d.rearrange("(b k p) d -> b p k d", p=P, k=KT)
                        for b in range(NE // KT, MAXI // KT):
                            sp.dma_start(spare[b], m.w_out).then_inc(s["spare"], 16)
                store(NT - 2)
                store(NT - 1)
                sp.wait_ge(s["oout"], 16 * NT)
                sp.wait_ge(s["spare"], 32)

            @block.tensor
            def _(pe):
                def scores(u):
                    i, h, branch, k0, n = units[u]
                    if u % PER == 0:
                        pe.wait_ge(s["qsplit"], 2 * (i + 1))
                    if u >= 2:
                        pe.wait_ge(s["expd"], u - 1)
                    g = h // HPG
                    kT = m.kwT if branch else m.ksT
                    dst = sc[u % 2]
                    for c in range(0, n, 4):
                        m_ = min(4, n - c)
                        marks = []
                        if not branch and i >= m.first_sel:
                            marks.append((c, m_, m.notselT[:, i - m.first_sel, g, :],
                                          m.eselb[:, c * P:(c + m_) * P]))
                        if branch and i >= 4 and c == 0:
                            marks.append((0, 1, m.identb[:], m.windowb[:]))
                        if c <= n - 1 < c + m_:
                            marks.append((n - 1, 1, m.identb[:], m.causalb[:]))
                        keys = kT[:, g, (k0 + c) * P:(k0 + c + m_) * P]
                        nc.tensor.matmul(dst[:, c * P:(c + m_) * P], qhi[i % 2][:, h, :], keys, start=True, stop=False)
                        last = nc.tensor.matmul(dst[:, c * P:(c + m_) * P], qlo[i % 2][:, h, :], keys,
                                                start=False, stop=not marks)
                        for j, (at, w_, a, b) in enumerate(marks):
                            last = nc.tensor.matmul(dst[:, at * P:(at + w_) * P], a, b, start=False,
                                                    stop=j == len(marks) - 1)
                    last.then_inc(s["scored"], 1)

                def turn(u):
                    pe.wait_ge(s["expd"], u + 1)
                    for j, (k, n) in enumerate(pieces[u]):
                        f = first_piece[u] + j
                        if f >= 2:
                            pe.wait_ge((s["evac0"], s["evac1"])[f % 2], f // 2)
                        for b in range(n):
                            last = nc.tensor.transpose(tp[f % 2][:, b * P:(b + 1) * P],
                                                       probs[u % 2][:, (k + b) * P:(k + b + 1) * P], m.c("ident"))
                        last.then_inc(s["turned"], 1)

                def values(u):
                    i, h, branch, k0, n = units[u]
                    v = m.vw if branch else m.vs
                    g = h // HPG
                    f = first_piece[u + 1]
                    pe.wait_ge(s["evac0"], (f + 1) // 2)
                    pe.wait_ge(s["evac1"], f // 2)
                    if h == 0 and i:
                        pe.wait_ge(s["read"], 2 * i)
                    for b in range(n):
                        at = (k0 + b) * P + g * HD
                        last = nc.tensor.matmul(ov[branch][:, h * HD:(h + 1) * HD], pT[u % 2][:, b, :],
                                                v[:, at:at + HD], start=b == 0, stop=b == n - 1)
                    last.then_inc(s["valued"], 1)

                for u in range(U + 3):
                    if u < U:
                        scores(u)
                    if 2 <= u < U + 2:
                        turn(u - 2)
                    if u >= 3:
                        values(u - 3)

            def evacuate(eng, copy, u, parity, sem_):
                for j, (k, n) in enumerate(pieces[u]):
                    f = first_piece[u] + j
                    if f % 2 == parity:
                        eng.wait_ge(s["turned"], f + 1)
                        if u >= 2:
                            eng.wait_ge(s["valued"], u - 1)
                        copy(pT[u % 2][:, k:k + n, :],
                             tp[f % 2][:, 0:n * P].rearrange("p (k q) -> p k q", k=n)).then_inc(sem_, 1)

            @block.scalar
            def _(act):
                def softmax(u):
                    i, h, branch, _, n = units[u]
                    act.wait_ge(s["nmax"], u + 1)
                    if u >= 2:
                        act.wait_ge(s["turned"], first_piece[u - 1])
                    if h == 0 and i >= 2:
                        act.wait_ge(s["rs"], i - 1)
                    nc.scalar.activation(probs[u % 2][:, 0:n * P], sc[u % 2][:, 0:n * P], ACT.Exp,
                                         bias=nmax[:, u % 4:u % 4 + 1],
                                         accum_out=den[i % 2][:, branch * NH + h:branch * NH + h + 1]
                                                 ).then_inc(s["expd"], 1)

                act.wait_ge(s["q_in"], 64)
                nc.scalar.activation(qhi[0][:], qT[:].rearrange("p a b q -> p (a b) q"), ACT.Copy).then_inc(s["qsplit"], 1)
                for u in range(U + 2):
                    if u < U:
                        softmax(u)
                    if u >= 2:
                        evacuate(act, lambda o, a: nc.scalar.activation(o, a, ACT.Copy), u - 2, 0, s["evac0"])

            @block.gpsimd
            def _(pool):
                def split(i):
                    pool.wait_ge(s["q_in"], 64 * (i + 1))
                    if i >= 2:
                        pool.wait_ge(s["scored"], PER * (i - 1))
                    q = qT[:].rearrange("p a b q -> p (a b) q")
                    nc.gpsimd.tensor_copy(qhi[i % 2][:], q).then_inc(s["qsplit"], 1)
                    pool.wait_ge(s["qsplit"], 2 * i + 1)
                    nc.gpsimd.tensor_tensor(qlo[i % 2][:], q, qhi[i % 2][:], ALU.subtract).then_inc(s["qsplit"], 1)

                split(1)
                for i in range(NT):
                    if i + 2 < NT:
                        split(i + 2)
                    pool.wait_ge(s["ms"], i + 1)
                    nc.gpsimd.tensor_tensor(pw[:], stat[:], m.mhalf[:, 0:8], ALU.pow).then_inc(s["rs"], 1)

            @block.vector
            def _(dve):
                done = Chain(dve, s["chain"])

                def maximum(u):
                    n = units[u][4]
                    dve.wait_ge(s["scored"], u + 1)
                    nc.vector.tensor_reduce(nmax[:, u % 4:u % 4 + 1], sc[u % 2][:, 0:n * P], AX.X, ALU.max,
                                            negate=True).then_inc(s["nmax"], 1)

                def gates(i):
                    b = i % 2
                    g3 = m.gate[:, i * 24:(i + 1) * 24].rearrange("p (h c) -> p c h", c=3)
                    dve.wait_ge(s["valued"], PER * (i + 1))
                    done(nc.vector.reciprocal(w[b][:, 0:16], den[b][:]))
                    done(nc.vector.tensor_tensor(w[b][:, 0:16].rearrange("p (c h) -> p c h", c=2),
                                                 w[b][:, 0:16].rearrange("p (c h) -> p c h", c=2), g3[:, 1:3, :],
                                                 ALU.mult))
                    nc.vector.tensor_tensor(heads(t1[:]), heads(ov[0][:]), bc(w[b][:, 0:8].unsqueeze(2), [P, NH, HD]),
                                            ALU.mult).then_inc(s["read"], 1)
                    nc.vector.tensor_tensor(heads(t2[:]), heads(ov[1][:]), bc(w[b][:, 8:16].unsqueeze(2), [P, NH, HD]),
                                            ALU.mult).then_inc(s["read"], 1)

                STEPS = 6

                def finish(i, step):
                    b = i % 2
                    g3 = m.gate[:, i * 24:(i + 1) * 24].rearrange("p (h c) -> p c h", c=3)
                    if step == 1:
                        dve.wait_ge(s["read"], 2 * i + 2)
                        done(nc.vector.tensor_tensor(t1[:], t1[:], t2[:], ALU.add))
                        done(nc.vector.tensor_copy(w[b][:, 16:24], g3[:, 0, :]))
                    elif step == 2:
                        dve.wait_ge(oc_in[b], 16 * (i // 2 + 1))
                        done(nc.vector.tensor_tensor(heads(t2[:]), heads(ocmp[b][:]),
                                                     bc(w[b][:, 16:24].unsqueeze(2), [P, NH, HD]), ALU.mult))
                        done(nc.vector.tensor_tensor(t1[:], t1[:], t2[:], ALU.add))
                    elif step == 3:
                        done(nc.vector.tensor_tensor(t2[:], t1[:], t1[:], ALU.mult))
                    elif step == 4:
                        done(nc.vector.tensor_reduce(stat[:], heads(t2[:]), AX.X, ALU.add))
                        nc.vector.tensor_scalar(stat[:], stat[:], 1.0 / HD, EPS, ALU.mult,
                                                ALU.add).then_inc(s["ms"], 1)
                    elif step == 5:
                        dve.wait_ge(s["rs"], i + 1)
                        done(nc.vector.tensor_tensor(heads(t1[:]), heads(t1[:]), bc(pw[:].unsqueeze(2), [P, NH, HD]),
                                                     ALU.mult))
                    else:
                        if i:
                            dve.wait_ge(s["oout"], 16 * i)
                        nc.vector.tensor_tensor(out[:], t1[:], m.gout[:], ALU.mult).then_inc(s["out"], 1)
                        dve.wait_ge(s["out"], i + 1)

                dve.wait_ge(s["qsplit"], 1)
                nc.vector.tensor_tensor(qlo[0][:], qT[:].rearrange("p a b q -> p (a b) q"), qhi[0][:],
                                        ALU.subtract).then_inc(s["qsplit"], 1)
                for u in range(U + 3 + STEPS):
                    if u < U:
                        maximum(u)
                    if 2 <= u < U + 2:
                        evacuate(dve, lambda o, a: nc.vector.tensor_copy(o, a), u - 2, 1, s["evac1"])
                    i, since = divmod(u - 2, PER)
                    if i >= 1 and since == 0:
                        gates(i - 1)
                    elif i >= 1 and since <= STEPS:
                        finish(i - 1, since)


AGE = dict(A=0, B=1, C=2, D=3, E=4, F=5)
ORDER = "EFDCBA"
TURNS = dict(A=2, B=2, C=1, D=2, E=1, F=2)


def phase_mix(nc, m, io):
    steps = [[(X, st - AGE[X]) for X in ORDER if 0 <= st - AGE[X] < NT] for st in range(NT + 5)]
    use, f = {}, 0
    for step in steps:
        for X, t in step:
            use[X, t] = f
            f += TURNS[X]
    with ExitStack() as st:
        sem = phase_semaphores(nc, m)
        sb = lambda n, s, d=F32: st.enter_context(nc.sbuf_tensor(n, s, d))
        ps = lambda n, w=512: st.enter_context(nc.psum_tensor(n, [P, w], F32))
        o = [sb(f"xo{b}", [P, D]) for b in range(2)]
        gx, gf = sb("xgx", [P, D]), sb("xgf", [P, D])
        wr = sb("xwr", [P, KT, 36])
        br = sb("xbr", [P, 36])
        h1, h3, junk = sb("xh1", [P, D]), sb("xh3", [P, D]), sb("xjunk", [P, D], BF16)
        pr = sb("xpr", [P, MH, NMEM])
        big, e8, key, km = [sb("x" + n, [P, c]) for n, c in (("big", NE), ("e8", EG), ("key", EG), ("km", 1))]
        qraw, qn, q2, om = [sb("x" + n, [P, 256]) for n in "qraw qn q2 om".split()]
        turned_to = {X: sb("xT" + X, [P, n, P]) for X, n in dict(A=8, B=8, C=2, D=8, E=2, F=8).items()}
        nm, den, rden, stq, pwq = [sb("x" + n, [P, 4]) for n in "nm den rden stq pwq".split()]
        ssA, msA, rsA, ssE, msE, rsE = [sb("x" + n, [P, 1]) for n in "ssA msA rsA ssE msE rsE".split()]
        sc = ps("xsc", 1024)
        tp = [ps("xtp0"), ps("xtp1")]
        pj = [ps("xpj0"), ps("xpj1")]
        qb, ov = ps("xqb"), ps("xov")
        s = {n: sem("x_" + n) for n in (
            "w_in turned evac mmA mmB mmC mmD mmE mmF x1 x2 sqA sqE msA msE msB rsA rsE rsB h1 h3 h3out qraw qn nmax "
            "expd om lg chain late_in").split()}
        o_in = [sem("x_o0"), sem("x_o1")]
        ocv = m.oc_d.rearrange("(t p) d -> t p d", p=P)
        xv = io["x"].rearrange("(t p) d -> t p d", p=P)
        hv = m.h_d.rearrange("(t p) d -> t p d", p=P)

        with nc.Block() as block:

            @block.sync
            def _(sp):
                def load(t):
                    if t >= 2:
                        sp.wait_ge(s["turned"], use["A", t - 2] + 2)
                    sp.dma_start(o[t % 2][:], ocv[t]).then_inc(o_in[t % 2], 16)
                    sp.dma_start(m.x1[:, t, :], xv[t]).then_inc(o_in[t % 2], 16)

                load(0)
                sp.dma_start(gx[:], io["g_memx"]).then_inc(s["w_in"], 16)
                sp.dma_start(gf[:], io["g_ffn"]).then_inc(s["w_in"], 16)
                sp.dma_start(wr[:], io["w_router"].rearrange("(p k) e -> p k e", p=P)).then_inc(s["w_in"], 16)
                sp.dma_start(br[:], io["b_router"]).then_inc(s["w_in"], 16)
                sp.dma_start(m.late[:], io["late"]).then_inc(s["late_in"], 16)
                for step in range(1, len(steps)):
                    if step < NT:
                        load(step)
                    t = step - AGE["E"]
                    if 0 <= t < NT:
                        sp.wait_ge(s["h3"], t + 1)
                        sp.dma_start(hv[t], h3[:]).then_inc(s["h3out"], 16)
                    if step == NT - 1 + AGE["E"]:
                        sp.wait_ge(s["mmA"], 2 * NT)
                        load_expert(sp, m, io, 2, 2)
                        sp.wait_ge(s["mmE"], 2 * NT)
                        load_expert(sp, m, io, 3, 3)
                sp.wait_ge(s["h3out"], 16 * NT)
                sp.wait_ge(s["late_in"], 16)

            @block.tensor
            def _(pe):
                def turn(X, t):
                    f = use[X, t]
                    src = dict(A=lambda k: o[t % 2][:, k * P:(k + 1) * P], B=lambda k: h1[:, k * P:(k + 1) * P],
                               C=lambda k: qn[:, k * P:(k + 1) * P],
                               D=lambda k: pr[:].rearrange("p h c -> p (h c)")[:, k * P:(k + 1) * P],
                               E=lambda k: om[:, k * P:(k + 1) * P], F=lambda k: h3[:, k * P:(k + 1) * P])[X]
                    if X == "A":
                        pe.wait_ge(o_in[t % 2], 32 * (t // 2 + 1))
                    else:
                        ready, n = dict(B=(s["h1"], 1), C=(s["qn"], 1), D=(s["expd"], MH), E=(s["om"], 1), F=(s["h3"], 1))[X]
                        pe.wait_ge(ready, n * (t + 1))
                    for j in range(TURNS[X]):
                        if f + j >= 2:
                            pe.wait_ge(s["evac"], f + j - 1)
                        for k in range(4 if TURNS[X] == 2 else 2):
                            last = nc.tensor.transpose(tp[(f + j) % 2][:, k * P:(k + 1) * P], src(4 * j + k),
                                                       m.c("ident"))
                        last.then_inc(s["turned"], 1)

                def dense(X, t, out, w, n, kt):
                    for k in range(kt):
                        last = nc.tensor.matmul(out, turned_to[X][:, k, :], w(k), start=k == 0, stop=k == kt - 1)
                    last.then_inc(finished[X], 1)

                finished = dict(A=s["mmA"], B=s["mmB"], C=s["mmC"], D=s["mmD"], E=s["mmE"], F=s["mmF"])

                def product(X, t):
                    pe.wait_ge(s["evac"], use[X, t] + TURNS[X])
                    if X in "AE":
                        first, second = (t, max(0, t - AGE["E"] + 1)) if X == "A" else (min(NT, t + AGE["E"]), t)
                        if first:
                            pe.wait_ge(s["x1"], 2 * first)
                        if second:
                            pe.wait_ge(s["x2"], 2 * second)
                        w, kt = (m.w_out, KT) if X == "A" else (m.wo, 2)
                        for half in range(2):
                            dense(X, t, pj[half][:], lambda k: w[:, k, 512 * half:512 * half + 512], 512, kt)
                    elif X == "B":
                        f_before = max(0, t + AGE["B"] - AGE["F"] + 1)
                        if t:
                            pe.wait_ge(s["qraw"], t)
                        if f_before:
                            pe.wait_ge(s["lg"], min(NT, f_before))
                        dense(X, t, qb[:, 0:256], lambda k: m.wq[:, k, :], 256, KT)
                    elif X == "F":
                        pe.wait_ge(s["w_in"], 64)
                        b_before = min(NT, t + AGE["F"] - AGE["B"])
                        pe.wait_ge(s["qraw"], b_before)
                        if t:
                            pe.wait_ge(s["lg"], t)
                        dense(X, t, qb[:, 0:36], lambda k: wr[:, k, :], 36, KT)
                    elif X == "C":
                        if t:
                            pe.wait_ge(s["expd"], MH * t)
                        for a in range(2):
                            last = nc.tensor.matmul(sc[:, a * 512:(a + 1) * 512], turned_to[X][:, a, :],
                                                    m.kmT[:, a].rearrange("p a c -> p (a c)"), start=True, stop=True)
                        last.then_inc(s["mmC"], 1)
                    elif X == "D":
                        if t:
                            pe.wait_ge(s["om"], t)
                        for h in range(MH):
                            for k in range(2):
                                last = nc.tensor.matmul(ov[:, h * HD:(h + 1) * HD], turned_to[X][:, 2 * h + k, :],
                                                        m.vm[:, k, h * HD:(h + 1) * HD], start=k == 0, stop=k == 1)
                        last.then_inc(s["mmD"], 1)

                pe.wait_ge(m.w_out_in, 48)
                for step in steps:
                    for k, (X, t) in enumerate(step):
                        turn(X, t)
                        if k:
                            product(*step[k - 1])
                    product(*step[-1])

            @block.scalar
            def _(act):
                counts = dict(A=(s["mmA"], 2), B=(s["mmB"], 1), C=(s["mmC"], 1), D=(s["mmD"], 1), E=(s["mmE"], 2), F=(s["mmF"], 1))

                def evac(X, t):
                    f = use[X, t]
                    if t:
                        sm, n = counts[X]
                        act.wait_ge(sm, n * t)
                    for j in range(TURNS[X]):
                        act.wait_ge(s["turned"], f + j + 1)
                        k = 4 if TURNS[X] == 2 else 2
                        nc.scalar.activation(turned_to[X][:, 4 * j:4 * j + k, :],
                                             tp[(f + j) % 2][:, 0:k * P].rearrange("p (k q) -> p k q", k=k), ACT.Copy,
                                             scale=m.mqgain[:] if X == "C" else 1.0).then_inc(s["evac"], 1)

                def work(X, t):
                    if X == "A":
                        act.wait_ge(s["x1"], 2 * t + 2)
                        nc.scalar.activation(junk[:], m.x1[:, t, :], ACT.Square, accum_out=ssA[:]).then_inc(s["sqA"], 1)
                    elif X == "E":
                        act.wait_ge(s["x2"], 2 * t + 2)
                        nc.scalar.activation(junk[:], m.x1[:, t, :], ACT.Square, accum_out=ssE[:]).then_inc(s["sqE"], 1)
                    elif X == "B":
                        act.wait_ge(s["mmB"], t + 1)
                        nc.scalar.activation(qraw[:], qb[:, 0:256], ACT.Copy).then_inc(s["qraw"], 1)
                    elif X == "C":
                        act.wait_ge(s["nmax"], t + 1)
                        for h in range(MH):
                            nc.scalar.activation(pr[:, h, :], sc[:, h * NMEM:(h + 1) * NMEM], ACT.Exp,
                                                 bias=nm[:, h:h + 1], accum_out=den[:, h:h + 1]).then_inc(s["expd"], 1)

                def squares_A(st):
                    if 0 <= st - 1 < NT:
                        work("A", st - 1)

                for st, step in enumerate(steps):
                    todo = dict(step)
                    for X in "EFDC":
                        if X == "D":
                            squares_A(st)
                        if X in todo:
                            evac(X, todo[X])
                    if "E" in todo:
                        work("E", todo["E"])
                    for X in "BA":
                        if X in todo:
                            evac(X, todo[X])
                    for X in "CB":
                        if X in todo:
                            work(X, todo[X])

            @block.gpsimd
            def _(pool):
                for step in steps:
                    for X, t in step:
                        if X in "ABE":
                            ms, rs, a, b, n = dict(A=(s["msA"], s["rsA"], msA, rsA, 1), B=(s["msB"], s["rsB"], stq, pwq, 4),
                                                   E=(s["msE"], s["rsE"], msE, rsE, 1))[X]
                            pool.wait_ge(ms, t + 1)
                            nc.gpsimd.tensor_tensor(b[:], a[:], m.mhalf[:, 0:n], ALU.pow).then_inc(rs, 1)

            @block.vector
            def _(dve):
                done = Chain(dve, s["chain"])

                def residual(t, mm, mark):
                    for half in range(2):
                        c = slice(512 * half, 512 * half + 512)
                        dve.wait_ge(mm, 2 * t + half + 1)
                        nc.vector.tensor_tensor(m.x1[:, t, c], m.x1[:, t, c], pj[half][:], ALU.add).then_inc(mark, 1)
                        dve.wait_ge(mark, 2 * t + half + 1)

                def hottest(src, mx, n, k, out):
                    done(nc.vector.tensor_reduce(mx, src, AX.X, ALU.max))
                    done(nc.vector.scalar_tensor_tensor(k, src, mx, m.c("pref8")[:, 0:n], ALU.is_equal, ALU.mult))
                    done(nc.vector.tensor_reduce(km[:], k, AX.X, ALU.max))
                    done(nc.vector.tensor_scalar(out, k, km[:], None, ALU.is_equal))

                def choose(t):
                    dve.wait_ge(s["lg"], t + 1)
                    if t == 0:
                        dve.wait_ge(s["late_in"], 16)
                    G, E = m.lg[:, t, 0:4], m.lg[:, t, 4:36].rearrange("p (g e) -> p e g", g=4)
                    hottest(G, m.gmax[:, t:t + 1], 4, key[:, 0:4], m.ghot[:, t, :])
                    done(nc.vector.tensor_tensor(big[:].rearrange("p (g e) -> p e g", g=4), E,
                                                 bc(m.ghot[:, t, :].unsqueeze(1), [P, EG, 4]), ALU.mult))
                    done(nc.vector.tensor_reduce(e8[:], big[:].rearrange("p (g e) -> p e g", g=4), AX.X, ALU.add))
                    hottest(e8[:], m.top[:, 0, t:t + 1], EG, key[:], m.ehot[:, 0, t, :])
                    done(nc.vector.scalar_tensor_tensor(e8[:], m.ehot[:, 0, t, :], TAKEN, e8[:], ALU.mult, ALU.add))
                    hottest(e8[:], m.top[:, 1, t:t + 1], EG, key[:], m.ehot[:, 1, t, :])

                def work(X, t):
                    if X == "A":
                        dve.wait_ge(o_in[t % 2], 32 * (t // 2 + 1))
                        residual(t, s["mmA"], s["x1"])
                        dve.wait_ge(s["sqA"], t + 1)
                        nc.vector.tensor_scalar(msA[:], ssA[:], 1.0 / D, EPS, ALU.mult, ALU.add).then_inc(s["msA"], 1)
                        dve.wait_ge(s["w_in"], 64)
                        dve.wait_ge(s["rsA"], t + 1)
                        if t:
                            dve.wait_ge(s["turned"], use["B", t - 1] + 2)
                        nc.vector.scalar_tensor_tensor(h1[:], m.x1[:, t, :], rsA[:], gx[:], ALU.mult,
                                                       ALU.mult).then_inc(s["h1"], 1)
                    elif X == "B":
                        dve.wait_ge(s["qraw"], t + 1)
                        done(nc.vector.tensor_tensor(q2[:], qraw[:], qraw[:], ALU.mult))
                        done(nc.vector.tensor_reduce(stq[:], heads(q2[:], MH), AX.X, ALU.add))
                        nc.vector.tensor_scalar(stq[:], stq[:], 1.0 / HD, EPS, ALU.mult, ALU.add).then_inc(s["msB"], 1)
                        dve.wait_ge(s["rsB"], t + 1)
                        if t:
                            dve.wait_ge(s["turned"], use["C", t - 1] + 1)
                        nc.vector.tensor_tensor(heads(qn[:], MH), heads(qraw[:], MH),
                                                bc(pwq[:].unsqueeze(2), [P, MH, HD]), ALU.mult).then_inc(s["qn"], 1)
                    elif X == "C":
                        dve.wait_ge(s["mmC"], t + 1)
                        if t:
                            dve.wait_ge(s["expd"], MH * t)
                        nc.vector.tensor_reduce(nm[:], heads(sc[:], MH), AX.X, ALU.max, negate=True
                                ).then_inc(s["nmax"], 1)
                    elif X == "D":
                        dve.wait_ge(s["mmD"], t + 1)
                        if t:
                            dve.wait_ge(s["turned"], use["E", t - 1] + 1)
                        nc.vector.tensor_tensor(heads(om[:], MH), heads(ov[:, 0:256], MH),
                                                bc(rden[:].unsqueeze(2), [P, MH, HD]), ALU.mult).then_inc(s["om"], 1)
                    elif X == "E":
                        residual(t, s["mmE"], s["x2"])
                        dve.wait_ge(s["sqE"], t + 1)
                        nc.vector.tensor_scalar(msE[:], ssE[:], 1.0 / D, EPS, ALU.mult, ALU.add).then_inc(s["msE"], 1)
                        dve.wait_ge(s["w_in"], 64)
                        dve.wait_ge(s["rsE"], t + 1)
                        if t:
                            dve.wait_ge(s["turned"], use["F", t - 1] + 2)
                            dve.wait_ge(s["h3out"], 16 * t)
                        v = lambda a: a.rearrange("p (q k) -> p q k", k=KT)
                        nc.vector.scalar_tensor_tensor(h3[:].rearrange("p (k q) -> p q k", k=KT), v(m.x1[:, t, :]),
                                                       rsE[:], v(gf[:]), ALU.mult, ALU.mult).then_inc(s["h3"], 1)
                    elif X == "F":
                        dve.wait_ge(s["mmF"], t + 1)
                        nc.vector.tensor_tensor(m.lg[:, t, :], qb[:, 0:36], br[:], ALU.add).then_inc(s["lg"], 1)

                for step in steps:
                    for X, t in step:
                        if X == "D":
                            dve.wait_ge(s["expd"], MH * (t + 1))
                            done(nc.vector.reciprocal(rden[:], den[:]))
                    todo = dict(step)
                    for X in "EFDCB":
                        if X in todo:
                            work(X, todo[X])
                    if "F" in todo:
                        choose(todo["F"])
                    if "A" in todo:
                        work("A", todo["A"])


def phase_route(nc, m, io):
    with ExitStack() as st:
        sem = phase_semaphores(nc, m)
        sb = lambda n, s, d=F32: st.enter_context(nc.sbuf_tensor(n, s, d))
        ps = lambda n, w=512: st.enter_context(nc.psum_tensor(n, [P, w], F32))
        gs, d = m.gexp, m.dexp
        hot = sb("rhot", [P, 2, NT, NE])
        both = sb("rboth", [P, NT, NE])
        runs = sb("rruns", [P, NT + 1, NE])
        posf, prod = sb("rposf", [P, NT, NE]), sb("rprod", [P, 2, NT, NE])
        over, ovend, ovst, ones = [sb("r" + n, [P, NE]) for n in "over ovend ovst one".split()]
        cmp_ = sb("rcmp", [P, NE, 16])
        pos, ov, ex, q, item, row = [sb("rt" + n, [P, 2, NT]) for n in "pos ov ex q item row".split()]
        rhot = sb("rrh", [P, 2 * NT, P], BF16)
        hits = sb("rhits", [P, 2 * NT, MAXI])
        ihot = sb("rih", [P, 2 * NT, 2, MAXI], BF16)
        small = sb("rsmall", [P, 64])
        pp, tot, rm = ps("rpp"), ps("rtot"), ps("rrm")
        s = {n: sem("r_" + n) for n in "gs d both counted rhot ihot mapped chain".split()}
        PART = NT // 2
        flat = lambda t: t[:].rearrange("p k t -> p (k t)")

        with nc.Block() as block:

            @block.scalar
            def _(act):
                act.wait_ge(s["gs"], 1)
                nc.scalar.activation(gs[:], gs[:], ACT.Exp)
                act.wait_ge(s["d"], 1)
                nc.scalar.activation(d[:], d[:], ACT.Exp)

            @block.tensor
            def _(pe):
                pe.wait_ge(s["both"], 1)
                rows = both[:].rearrange("p t e -> p (t e)")
                nc.tensor.matmul(pp[:, 0:256], m.c("before"), rows, start=True, stop=True)
                nc.tensor.matmul(tot[:, 0:256], m.c("ones"), rows, start=True, stop=True).then_inc(s["counted"], 1)
                pe.wait_ge(s["ihot"], 2)
                for n in range(2 * NT):
                    pe.wait_ge(s["rhot"], n // PART + 1)
                    last = nc.tensor.matmul(rm[:, 0:2 * MAXI], rhot[:, n, :], ihot[:, n].rearrange("p a i -> p (a i)"),
                                            start=n == 0, stop=n == 2 * NT - 1)
                last.then_inc(s["mapped"], 1)

            @block.vector
            def _(dve):
                done = Chain(dve, s["chain"])
                tt, ts, red = nc.vector.tensor_tensor, nc.vector.tensor_scalar, nc.vector.tensor_reduce
                for k in range(2):
                    done(tt(hot[:, k].rearrange("p t (g e) -> p t g e", g=4),
                            bc(m.ghot[:].unsqueeze(3), [P, NT, 4, EG]),
                            bc(m.ehot[:, k].unsqueeze(2), [P, NT, 4, EG]), ALU.mult))
                tt(both[:], hot[:, 0], hot[:, 1], ALU.add).then_inc(s["both"], 1)
                tt(gs[:], m.lg[:, :, 0:4], bc(m.gmax[:].unsqueeze(2), [P, NT, 4]), ALU.subtract).then_inc(s["gs"], 1)
                tt(d[:], m.top[:, 1], m.top[:, 0], ALU.subtract).then_inc(s["d"], 1)
                done(nc.vector.memset(runs[:, 0, :], 0.0))
                done(nc.vector.memset(ones[:], 1.0))
                done(tt(prod[:], hot[:], bc(m.c("eid").unsqueeze(1).unsqueeze(1), [P, 2, NT, NE]), ALU.mult))
                done(red(flat(ex), prod[:].rearrange("p k t e -> p (k t) e"), AX.X, ALU.add))
                dve.wait_ge(s["counted"], 1)
                for t in range(NT):
                    done(tt(runs[:, t + 1, :], runs[:, t, :], tot[:, t * NE:(t + 1) * NE], ALU.add))
                done(tt(posf[:].rearrange("p t e -> p (t e)"), runs[:, 0:NT, :].rearrange("p t e -> p (t e)"),
                        pp[:, 0:256], ALU.add))
                thr = m.c("thr")[:, 1:8]
                done(tt(cmp_[:, :, 0:7], bc(runs[:, NT, :].unsqueeze(2), [P, NE, 7]),
                        bc(thr.unsqueeze(1), [P, NE, 7]), ALU.is_gt))
                done(red(over[:], cmp_[:, :, 0:7], AX.X, ALU.add))
                done(nc.vector.tensor_tensor_scan(ovend[:], ones[:], over[:], 0.0, ALU.mult, ALU.add))
                done(tt(ovst[:], ovend[:], over[:], ALU.subtract))
                for dst, table in ((pos, bc(posf[:].unsqueeze(1), [P, 2, NT, NE])),
                                   (ov, bc(ovst[:].unsqueeze(1).unsqueeze(1), [P, 2, NT, NE]))):
                    done(tt(prod[:], hot[:], table, ALU.mult))
                    done(red(flat(dst), prod[:].rearrange("p k t e -> p (k t) e"), AX.X, ALU.add))
                done(tt(cmp_[:, 0:2 * NT, 0:7], bc(flat(pos).unsqueeze(2), [P, 2 * NT, 7]),
                        bc(thr.unsqueeze(1), [P, 2 * NT, 7]), ALU.is_ge))
                done(red(flat(q), cmp_[:, 0:2 * NT, 0:7], AX.X, ALU.add))
                done(nc.vector.scalar_tensor_tensor(row[:], q[:], -float(P), pos[:], ALU.mult, ALU.add))
                done(tt(item[:], ov[:], q[:], ALU.add))
                done(nc.vector.scalar_tensor_tensor(item[:], item[:], float(NE - 1), ex[:], ALU.add, ALU.subtract))
                done(nc.vector.scalar_tensor_tensor(item[:], q[:], 0.0, item[:], ALU.is_gt, ALU.mult))
                done(tt(item[:], item[:], ex[:], ALU.add))
                done(tt(hits[:], bc(m.c("item").unsqueeze(1), [P, 2 * NT, MAXI]),
                        bc(flat(item).unsqueeze(2), [P, 2 * NT, MAXI]), ALU.is_equal))
                tt(ihot[:, :, 0], hits[:], bc(m.c("place").unsqueeze(2), [P, 2 * NT, MAXI]),
                   ALU.mult).then_inc(s["ihot"], 1)
                tt(ihot[:, :, 1], hits[:], bc(m.c("tile").unsqueeze(2), [P, 2 * NT, MAXI]),
                   ALU.mult).then_inc(s["ihot"], 1)
                for b in range(2 * NT // PART):
                    c = slice(b * PART, (b + 1) * PART)
                    tt(rhot[:, c], bc(m.c("iota").unsqueeze(1), [P, PART, P]),
                       bc(flat(row)[:, c].unsqueeze(2), [P, PART, P]), ALU.is_equal).then_inc(s["rhot"], 1)
                done(nc.vector.memset(m.rows[:], 0))
                done(nc.vector.tensor_copy(m.experts[:, 0:NE], m.c("eid")))
                pairs = cmp_[:].rearrange("p a b -> p (a b)").rearrange("p (j e) -> p j e", j=16)
                done(tt(pairs, bc(ovend[:].unsqueeze(1), [P, 16, NE]),
                        bc(m.c("item")[:, 0:16].unsqueeze(2), [P, 16, NE]), ALU.is_le))
                done(red(small[:, 0:16], pairs, AX.X, ALU.add))
                done(ts(m.experts[:, NE:MAXI], small[:, 0:16], float(NE - 1), None, ALU.min))
                done(tt(small[:, 16:20], bc(ovend[:, NE - 1:NE], [P, 4]), m.c("thr4"), ALU.is_gt))
                done(red(small[:, 20:21], small[:, 16:20], AX.X, ALU.add))
                done(ts(m.rounds[:], small[:, 20:21], float(NE // SLOTS - 1), None, ALU.add))
                done(nc.vector.scalar_tensor_tensor(m.slot[:], item[:], float(P), row[:], ALU.mult, ALU.add))
                dve.wait_ge(s["mapped"], 1)
                done(nc.vector.tensor_copy(hits[:, 0, :], rm[:, 0:MAXI]))
                done(nc.vector.scalar_tensor_tensor(m.rows[:, 0:MAXI], rm[:, MAXI:2 * MAXI], float(P), hits[:, 0, :],
                                                    ALU.mult, ALU.add))


def phase_experts(nc, m, io):
    with ExitStack() as st:
        sem = phase_semaphores(nc, m)
        sb = lambda n, s, d=F32: st.enter_context(nc.sbuf_tensor(n, s, d))
        ps = lambda n, w=512: st.enter_context(nc.psum_tensor(n, [P, w], F32))
        idx = [sb(f"eidx{k}", [P, 1], I32) for k in range(SLOTS)]
        mark = sb("emark", [P, 1], I32)
        xg = [sb(f"exg{b}", [P, D]) for b in range(2)]
        xT = [sb(f"exT{b}", [P, KT, P]) for b in range(2)]
        sg = [sb(f"esg{b}", [P, FF]) for b in range(2)]
        h = [sb(f"eh{b}", [P, FF]) for b in range(2)]
        hT = sb("ehT", [P, 2, P])
        y = [sb(f"ey{b}", [P, D]) for b in range(2)]
        tp = [ps("etp0"), ps("etp1")]
        gu = [ps("egu0"), ps("egu1")]
        th = ps("eth")
        yp = [ps("eyp0"), ps("eyp1")]
        s = {n: sem("e_" + n) for n in (
            "idx turned xT0 xT1 gated silu h hturned hT down y0 y1 mark").split()}
        got = [sem("e_g0"), sem("e_g1")]
        kept = [sem("e_k0"), sem("e_k1")]
        yv = m.y_d.rearrange("(n p) d -> n p d", p=P)

        def rounds(eng):
            return eng.value_load(m.rounds[0:1, 0:1], min_val=NE // SLOTS - 1, max_val=MAXI // SLOTS - 1)

        with nc.Block() as block:

            @block.sync
            def _(sp):
                last_round = rounds(sp)
                def store(b, k):
                    sp.wait_ge(s["y0"], 4 * b + k + 1)
                    sp.wait_ge(s["y1"], 4 * b + k + 1)
                    sp.dma_start(yv[4 * b + k], y[k % 2][:]).then_inc(kept[k % 2], 16)

                with sp.Fori(0, last_round) as b:
                    for k in range(SLOTS):
                        e = sp.value_load(m.experts[0:1, bass.ds(4 * b + 4 + k, 1)], min_val=0, max_val=NE - 1)
                        sp.wait_ge(s["down"], 4 * b + k + 1)
                        load_expert(sp, m, io, e, k)
                        store(b, k)
                for k in range(SLOTS):
                    store(last_round, k)

            @block.gpsimd
            def _(pool):
                last_round = rounds(pool)

                def gather(b, k, first=False):
                    if not first:
                        pool.wait_ge(s["turned"], 2 * (4 * b + k - 1))
                    nc.gpsimd.tensor_copy(idx[k][:], m.rows[:, bass.ds(4 * b + k, 1)]).then_inc(s["idx"], 1)
                    pool.wait_ge(s["idx"], 4 * b + k + 1)
                    nc.gpsimd.tensor_tensor(mark[:], idx[k][:], idx[k][:], ALU.add).then_inc(s["mark"], 1)
                    nc.gpsimd.indirect_dma_start(xg[k % 2][:], None, m.h_d, bass.IndirectOffsetOnAxis(idx[k][:], 0)
                                                 ).then_inc(got[k % 2], 16)

                for k in range(SLOTS):
                    gather(0, k, k < 2)
                with pool.Fori(1, last_round + 1) as b:
                    for k in range(SLOTS):
                        gather(b, k)
                gather(last_round + 1, 0)
                pool.wait_ge(got[0], 32 * last_round + 48)
                for p in range(2):
                    pool.wait_ge(kept[p], 32 * last_round + 32)

            def over_rounds(eng, body):
                last_round = rounds(eng)
                body(0)
                with eng.Fori(1, last_round + 1) as b:
                    body(b)
                return last_round

            @block.tensor
            def _(pe):
                def turn_x(b, k):
                    pe.wait_ge(got[k % 2], 32 * b + 16 * (k // 2) + 16)
                    for j in range(2):
                        for c in range(4):
                            last = nc.tensor.transpose(tp[j][:, c * P:(c + 1) * P],
                                                       xg[k % 2][:, (4 * j + c) * P:(4 * j + c + 1) * P],
                                                       m.c("ident"))
                        last.then_inc(s["turned"], 1)

                def down(b, k):
                    pe.wait_ge(s["hT"], 4 * b + k + 1)
                    pe.wait_ge(s["y0"], 4 * b + k)
                    pe.wait_ge(s["y1"], 4 * b + k)
                    for half in range(2):
                        for c in range(2):
                            last = nc.tensor.matmul(yp[half][:], hT[:, c, :],
                                                    m.down[k][:, c, 512 * half:512 * half + 512],
                                                    start=c == 0, stop=c == 1)
                    last.then_inc(s["down"], 1)

                def body(b):
                    for k in range(SLOTS):
                        n = 4 * b + k
                        pe.wait_ge(s["xT0"], n + 1)
                        pe.wait_ge(s["xT1"], n + 1)
                        pe.wait_ge(m.w_sem[k], 48 * b + 48)
                        for c in range(KT):
                            last = nc.tensor.matmul(gu[k % 2][:], xT[k % 2][:, c, :], m.gateup[k][:, c, :],
                                                    start=c == 0, stop=c == KT - 1)
                        last.then_inc(s["gated"], 1)
                        turn_x(b + 1 if k == 3 else b, (k + 1) % 4)
                        if k:
                            down(b, k - 1)
                        elif not isinstance(b, int):
                            down(b - 1, 3)
                        pe.wait_ge(s["h"], n + 1)
                        for c in range(2):
                            last = nc.tensor.transpose(th[:, c * P:(c + 1) * P], h[k % 2][:, c * P:(c + 1) * P],
                                                       m.c("ident"))
                        last.then_inc(s["hturned"], 1)

                turn_x(0, 0)
                last_round = over_rounds(pe, body)
                down(last_round, 3)

            def keep_y(eng, half, copy, b, k, sem_):
                eng.wait_ge(s["down"], 4 * b + k + 1)
                if not (isinstance(b, int) and b == 0 and k < 2):
                    eng.wait_ge(kept[k % 2], 32 * b + 16 * (k // 2))
                copy(y[k % 2][:, 512 * half:512 * half + 512], yp[half][:]).then_inc(sem_, 1)

            def take_x(eng, half, copy, b, k, sem_):
                eng.wait_ge(s["turned"], 2 * (4 * b + k) + half + 1)
                copy(xT[k % 2][:, 4 * half:4 * half + 4, :],
                     tp[half][:].rearrange("p (k q) -> p k q", k=4)).then_inc(sem_, 1)

            @block.scalar
            def _(act):
                copy = lambda o, a: nc.scalar.activation(o, a, ACT.Copy)

                def body(b):
                    for k in range(SLOTS):
                        n = 4 * b + k
                        act.wait_ge(s["gated"], n + 1)
                        nc.scalar.activation(sg[k % 2][:], gu[k % 2][:, 0:FF], ACT.Silu).then_inc(s["silu"], 1)
                        take_x(act, 0, copy, b + 1 if k == 3 else b, (k + 1) % 4, s["xT0"])
                        if k:
                            keep_y(act, 0, copy, b, k - 1, s["y0"])
                        elif not isinstance(b, int):
                            keep_y(act, 0, copy, b - 1, 3, s["y0"])
                        act.wait_ge(s["hturned"], n + 1)
                        copy(hT[:], th[:, 0:2 * P].rearrange("p (k q) -> p k q", k=2)).then_inc(s["hT"], 1)

                take_x(act, 0, copy, 0, 0, s["xT0"])
                last_round = over_rounds(act, body)
                keep_y(act, 0, copy, last_round, 3, s["y0"])

            @block.vector
            def _(dve):
                copy = lambda o, a: nc.vector.tensor_copy(o, a)

                def body(b):
                    for k in range(SLOTS):
                        n = 4 * b + k
                        dve.wait_ge(s["silu"], n + 1)
                        nc.vector.tensor_tensor(h[k % 2][:], sg[k % 2][:], gu[k % 2][:, FF:2 * FF],
                                                ALU.mult).then_inc(s["h"], 1)
                        take_x(dve, 1, copy, b + 1 if k == 3 else b, (k + 1) % 4, s["xT1"])
                        if k:
                            keep_y(dve, 1, copy, b, k - 1, s["y1"])
                        elif not isinstance(b, int):
                            keep_y(dve, 1, copy, b - 1, 3, s["y1"])

                take_x(dve, 1, copy, 0, 0, s["xT1"])
                last_round = over_rounds(dve, body)
                keep_y(dve, 1, copy, last_round, 3, s["y1"])


def phase_combine(nc, m, io, out):
    with ExitStack() as st:
        sem = phase_semaphores(nc, m)
        NB = 8
        y = [st.enter_context(nc.sbuf_tensor(f"gy{b}", [P, D], F32)) for b in range(NB)]
        idx = st.enter_context(nc.sbuf_tensor("gidx", [P, 2, NT], I32))
        got = [sem(f"g_g{b}") for b in range(NB)]
        gw, rec = [st.enter_context(nc.sbuf_tensor("g" + n, [P, NT], F32)) for n in ("w", "rec")]
        added, gone, ready, chain = sem("g_added"), sem("g_out"), sem("g_idx"), sem("g_chain")
        with nc.Block() as block:

            @block.gpsimd
            def _(pool):
                pool.wait_ge(ready, 1)
                for n in range(2 * NT):
                    t, k = divmod(n, 2)
                    if n >= NB:
                        pool.wait_ge(added, n - NB + 1)
                    nc.gpsimd.indirect_dma_start(y[n % NB][:], None, m.y_d,
                                                 bass.IndirectOffsetOnAxis(idx[:, k, t:t + 1], 0)
                                                         ).then_inc(got[n % NB], 16)

            @block.vector
            def _(dve):
                nc.vector.tensor_copy(idx[:], m.slot[:]).then_inc(ready, 1)
                done = Chain(dve, chain)
                done(nc.vector.tensor_reduce(gw[:], m.gexp[:], AX.X, ALU.add))
                done(nc.vector.reciprocal(gw[:], gw[:]))
                done(nc.vector.tensor_scalar(rec[:], m.dexp[:], 1.0, None, ALU.add))
                done(nc.vector.reciprocal(rec[:], rec[:]))
                done(nc.vector.tensor_tensor(m.wts[:, 0, :], gw[:], rec[:], ALU.mult))
                done(nc.vector.tensor_tensor(m.wts[:, 1, :], m.wts[:, 0, :], m.dexp[:], ALU.mult))
                for n in range(2 * NT):
                    t, k = divmod(n, 2)
                    dve.wait_ge(got[n % NB], 16 * (n // NB) + 16)
                    if k:
                        dve.wait_ge(added, n)
                    nc.vector.scalar_tensor_tensor(m.x1[:, t, :], y[n % NB][:], m.wts[:, k, t:t + 1], m.x1[:, t, :],
                                                   ALU.mult, ALU.add).then_inc(added, 1)

            @block.sync
            def _(sp):
                ov = out.rearrange("b (t p) d -> (b t) p d", p=P)
                for t in range(NT):
                    sp.wait_ge(added, 2 * t + 2)
                    sp.dma_start(ov[t], m.x1[:, t, :]).then_inc(gone, 16)
                sp.wait_ge(gone, 16 * NT)


def build(nc, io, out):
    with ExitStack() as st:
        sb = lambda n, s, d=F32: st.enter_context(nc.sbuf_tensor(n, s, d))
        sem = lambda n: st.enter_context(nc.semaphore(n))
        m = Memory()
        dram = lambda n, s: nc.dram_tensor(n, s, F32, kind="Internal").ap()
        m.q_d = dram("q_d", [NT, P, 512])
        m.oc_d = dram("oc_d", [S, D])
        m.h_d = dram("h_d", [S, D])
        m.y_d = dram("y_d", [MAXI * P, D])
        m.arena = sb("arena", [P, KT * PROJ])
        m.early = sb("early", [P, NEARLY])
        m.gcol = sb("gcol", [P, 8])
        m.mhalf = sb("mhalf", [P, 16])
        m.qgain, m.mqgain = sb("qgain", [P, 1]), sb("mqgain", [P, 1])
        m.kmT, m.vm = sb("kmT", [P, 2, 2, NMEM]), sb("vm", [P, 2, 256])
        m.w1_in, m.w2_in = [sem("w1_k_in"), sem("w1_v_in")], sem("w2_in")
        m.w_out_in = sem("w_out_in")
        m.w_sem = [sem(f"w_sem{k}") for k in range(SLOTS)]

        def const(name):
            places, tile = next((p, t) for p, t in ((EARLY, m.early), (MIDDLE, m.middle), (LATE, m.late)) if name in p)
            at, n = places[name]
            return tile[:, at:at + n]

        m.c = const
        m.middle = m.late = None
        W = KT * 2 * FF + 2 * D
        m.slot_size = W
        slot = lambda k: m.arena[:, k * W:(k + 1) * W]
        m.gateup = [slot(k)[:, 0:KT * 2 * FF].rearrange("p (k f) -> p k f", k=KT) for k in range(SLOTS)]
        m.down = [slot(k)[:, KT * 2 * FF:W].rearrange("p (k d) -> p k d", k=2) for k in range(SLOTS)]
        upper = m.arena[:, 2 * W:4 * W]
        m.tail = m.arena[:, 4 * W:]
        m.w1 = m.arena[:, KT * (PROJ - 1024):KT * (PROJ - 1024) + CB * P].rearrange("p (a n) -> p a n", a=2)
        m.w_out = upper[:, 0:KT * D].rearrange("p (k n) -> p k n", k=KT)
        m.wq = upper[:, KT * D:KT * D + KT * 256].rearrange("p (k n) -> p k n", k=KT)
        m.wo = upper[:, KT * D + KT * 256:KT * D + KT * 256 + 2 * D].rearrange("p (k n) -> p k n", k=2)

        with ExitStack() as st2:
            ab = lambda n, s, d=F32: st2.enter_context(nc.sbuf_tensor(n, s, d))
            m.kcvcT = ab("kcvcT", [P, 2, S])
            m.ksT, m.kwT = ab("ksT", [P, NG, S], F32R), ab("kwT", [P, NG, S], F32R)
            m.vs, m.vw = ab("vs", [P, S]), ab("vw", [P, S])
            m.gate = ab("gate", [P, NT * 24])
            m.w2, m.pos = ab("cw2", [P, 2, HD]), ab("cpos", [P, 2, CB])
            phase_project(nc, m, io)
            m.middle = ab("middle", [P, NMIDDLE])
            m.gout = ab("gout", [P, 512])
            m.identb, m.causalb, m.windowb = [ab(n, [P, P], BF16) for n in "identb causalb windowb".split()]
            m.eselb = ab("eselb", [P, S], BF16)
            m.cbiasb = ab("cbiasb", [P, NT * NC], BF16)
            m.kcT, m.vc = ab("kcT", [P, NG, 2, NC]), ab("vc", [P, NG, 2, HD])
            phase_keys(nc, m, io)
            m.notselT = ab("notselT", [P, NT // 2, NG, P], BF16)
            phase_select(nc, m, io)
            phase_attend(nc, m, io)
        m.late = sb("late", [P, NLATE])
        m.x1 = sb("x1", [P, NT, D])
        m.lg = sb("lg", [P, NT, 36])
        m.gmax, m.ghot, m.top = sb("gmax", [P, NT]), sb("ghot", [P, NT, 4]), sb("top", [P, 2, NT])
        m.ehot = sb("ehot", [P, 2, NT, EG])
        phase_mix(nc, m, io)
        m.gexp, m.dexp = sb("gexp", [P, NT, 4]), sb("dexp", [P, NT])
        m.wts, m.slot = sb("wts", [P, 2, NT]), sb("slot", [P, 2, NT])
        m.experts, m.rounds = sb("experts", [P, MAXI], I32), sb("rounds", [P, 1], I32)
        m.rows = sb("rows", [P, MAXI + SLOTS], I32)
        phase_route(nc, m, io)
        phase_experts(nc, m, io)
        phase_combine(nc, m, io, out)


def early_tables():
    t = np.zeros((P, NEARLY), np.float32)
    at = lambda n: slice(EARLY[n][0], EARLY[n][0] + EARLY[n][1])
    i = np.arange(P)
    t[:, at("ident")] = np.eye(P)
    t[:, at("tri")] = i[None, :] >= i[:, None]
    lg = np.log1p(-2.0 ** (-5.0 - np.arange(NH)))
    own = np.equal.outer(i // HD, i // HD)
    decay = np.exp(P * lg).reshape(4, 2)[:, i // HD]
    t[:, at("gammac")] = (own[:, None, :] * decay[None]).reshape(P, -1)
    return t


def middle_tables():
    t = np.zeros((P, NMIDDLE), np.float32)
    at = lambda n: slice(MIDDLE[n][0], MIDDLE[n][0] + MIDDLE[n][1])
    i = np.arange(P)
    tok = np.arange(NT)[None, :] * P + i[:, None]
    t[:, at("causal")] = np.where(i[None, :] > i[:, None], MASKED, 0)
    t[:, at("window")] = np.where(i[None, :] <= i[:, None], MASKED, 0)
    c = np.arange(NC)
    valid = (CS * c + CB - 1 <= tok[:, :, None]) & (c < NCR)
    t[:, at("cbias")] = np.where(valid, 0, MASKED).reshape(P, -1)
    t[:, at("cmask")] = valid[:, 0]
    j = np.arange(NSEL)
    cur = (tok // HD)[:, :, None]
    forced = (j == 0) | (j == cur) | (j == cur - 1)
    t[:, at("impa")] = (~forced & (j <= cur)).reshape(P, -1)
    t[:, at("impb")] = np.where(forced, 1e9, np.where(j > cur, MASKED, 0)).reshape(P, -1)
    c0, s0 = CS * np.arange(NCR), HD * np.arange(NSEL)
    ov = np.minimum(c0[None] + CB, s0[:, None] + HD) - np.maximum(c0[None], s0[:, None])
    sel = (np.clip(ov, 0, None) / CB).T
    t[0:NCR, at("selm")] = sel
    t[HD:HD + NCR, at("selm")] = sel
    t[0:NSEL, at("esel")] = np.where(np.arange(S)[None, :] // HD == j[:, None], MASKED, 0)
    return t


def late_tables():
    t = np.zeros((P, NLATE), np.float32)
    at = lambda n: slice(LATE[n][0], LATE[n][0] + LATE[n][1])
    i = np.arange(P)
    t[:, at("before")] = i[:, None] < i[None, :]
    t[:, at("ones")] = 1.0
    t[:, at("iota")] = i[None, :]
    t[:, at("thr")] = P * np.arange(16)[None, :]
    t[:, at("eid")] = np.arange(NE)[None, :]
    t[:, at("pref8")] = 8 - np.arange(8)[None, :]
    t[:, at("place")] = i[:, None]
    t[:, at("tile")] = np.arange(2 * NT)[None, :] % NT
    t[:, at("item")] = np.arange(MAXI)[None, :]
    t[:, at("thr4")] = SLOTS * np.arange(4)[None, :]
    return t


def rope_tables():
    half = HD // 2
    inv = 10000.0 ** (-np.arange(half, dtype=np.float32) / half)
    ang = (np.arange(S, dtype=np.float32)[:, None] * inv[None, :].astype(np.float32)).astype(np.float64)
    lg = np.log1p(-2.0 ** (-5.0 - np.arange(NH)))
    place = (np.arange(S) % P + 1.0)[:, None, None]
    up, down = np.exp(place * lg[None, :, None]), np.exp(-place * lg[None, :, None]) * HD ** -0.5
    parts = [f(ang)[:, None, :] * w for w in (up, down) for f in (np.cos, np.sin)]
    return np.concatenate([p.reshape(S, NH * half) for p in parts], axis=1).astype(np.float32)


def kernel(**inputs):
    import concourse.bacc as bacc
    from concourse.bass_utils import run_bass_kernel_spmd

    a = {n: np.asarray(v) for n, v in inputs.items()}
    rows = lambda v: np.ascontiguousarray(np.broadcast_to(v.reshape(1, -1), (P, v.size)))
    twice = lambda v: np.concatenate([v.reshape(-1), v.reshape(-1)])
    gcol = np.zeros((P, 8), np.float32)
    for j, n in enumerate(("nsa_q_norm", "nsa_ksel_norm", "nsa_kwin_norm", "mem_q_norm", "mem_k_norm",
                           "nsa_kcmp_norm")):
        gcol[:, j] = twice(a[n])
    posT = np.stack([np.concatenate([a[n][0].T, a[n][0].T]) for n in ("cmp_pos_k", "cmp_pos_v")], axis=1)
    arrays = {
        "x": a["x"][0], "mem": a["mem"][0], "w_in": a["w_in"][0], "w_out": a["w_out"][0],
        "mem_wq": a["mem_wq"][0], "mem_wkv": a["mem_wkv"][0], "mem_wo": a["mem_wo"][0],
        "cmp_k_w1": a["cmp_k_w1"][0], "cmp_v_w1": a["cmp_v_w1"][0],
        "cmp_k_w2": a["cmp_k_w2"][0], "cmp_v_w2": a["cmp_v_w2"][0],
        "cmp_pos": posT.reshape(P, 2 * CB),
        "g_mix": rows(a["mix_norm"]), "g_memx": rows(a["mem_x_norm"]), "g_memkv": rows(a["mem_kv_norm"]),
        "g_ffn": rows(a["ffn_norm"]), "g_out": rows(np.concatenate([a["nsa_out_norm"][0], a["ret_out_norm"][0]])),
        "gcol": gcol,
        "w_router": np.concatenate([a["router_group_w"][0], a["router_expert_w"][0].transpose(1, 0, 2).reshape(D, NE)],
                                   axis=1),
        "b_router": rows(np.concatenate([a["router_group_b"][0], a["router_expert_b"][0].reshape(NE)])),
        "w_gate": a["exp_w_gate"][0], "w_up": a["exp_w_up"][0], "w_down": a["exp_w_down"][0],
        "early": early_tables(), "middle": middle_tables(), "late": late_tables(), "rope": rope_tables(),
    }
    arrays = {n: np.ascontiguousarray(v) for n, v in arrays.items()}
    nc = bacc.Bacc("TRN2", target_bir_lowering=False, num_devices=1)
    io = {n: nc.dram_tensor("in_" + n, v.shape, mybir.dt.from_np(v.dtype), kind="ExternalInput").ap()
                            for n, v in arrays.items()}
    out = nc.dram_tensor("out_0", (1, S, D), F32, kind="ExternalOutput").ap()
    build(nc, io, out)
    r = run_bass_kernel_spmd(nc, [{"in_" + n: v for n, v in arrays.items()}], core_ids=[0])
    return r.results[0]["out_0"]
```
